# Optimizing a Trainium2 kernel written in Bass

```python
import math
import jax, jax.numpy as jnp
from jax import lax
import numpy as np

D_MODEL = 2048
BATCH = 1
SEQ = 256
DEPTH = 1

GRID_W = 64
CTX_LEN = 256

A_HEADS = 8
A_HD = 64
A_W = A_HEADS * A_HD
A_DECAY_R = 32
A_ICLR_R = 32
A_GATE_R = 96
W_DECAY_SCALE = math.exp(-0.5)
RWKV_GN_EPS = 64e-5

B_HEADS = 8
B_NOPE = 128
B_ROPE = 64
B_VD = 128
B_QR = 512
B_KVR = 256
B_W = B_HEADS * B_VD

C_HEADS = 4
C_KD = 64
C_VD = 128
C_W = C_HEADS * C_VD
CHUNK = 128
RET_GN_EPS = 1e-5

MIX_W = A_W + B_W + C_W

A_COLS = 3 * A_W + 2 * A_DECAY_R + 2 * A_ICLR_R + A_GATE_R
B_COLS = B_QR + B_KVR + B_ROPE
C_COLS = 2 * C_HEADS * C_KD + C_W + C_W
IN_COLS = A_COLS + B_COLS + C_COLS
IN_SPLITS = (A_COLS, A_COLS + B_COLS)
A_SPLITS = (A_W, 2 * A_W, 3 * A_W, 3 * A_W + 2 * A_DECAY_R, 3 * A_W + 2 * A_DECAY_R + 2 * A_ICLR_R)
B_SPLITS = (B_QR, B_QR + B_KVR)
C_SPLITS = (C_HEADS * C_KD, 2 * C_HEADS * C_KD, 2 * C_HEADS * C_KD + C_W)

N_EXPERTS = 16
N_GROUPS = 4
EXPERTS_PER_GROUP = N_EXPERTS // N_GROUPS
TOP_K = 2
D_EXPERT = 512
ROUTE_SCALE = 2.5

ALPHA = (2 * DEPTH) ** 0.25
BETA = (8 * DEPTH) ** -0.25
ROPE_BASE = 10000.0
QBLOCK = 128
LN_EPS = 1e-5

kernel_name = 'hybrid_rwkv7_mla_retention_moe_dit'

def layer_norm(x, g, b, eps=LN_EPS):
    xf = x.astype(jnp.float32)
    xc = xf - jnp.mean(xf, -1, keepdims=True)
    var = jnp.mean(xc * xc, -1, keepdims=True)
    return (xc * lax.rsqrt(var + eps) * g + b).astype(x.dtype)

def rms_norm(x, g, eps=LN_EPS):
    xf = x.astype(jnp.float32)
    return (xf * lax.rsqrt(jnp.mean(xf * xf, -1, keepdims=True) + eps) * g).astype(x.dtype)

def centred_shift(x):
    xp = jnp.pad(x, ((0, 0), (1, 1), (0, 0)))
    return 0.5 * (xp[:, :-2] + xp[:, 2:])

def grid_rope_tables(rows, dim):
    n = dim // 4
    inv = ROPE_BASE ** (-jnp.arange(n, dtype=jnp.float32) / n)
    r = jnp.repeat(jnp.arange(rows, dtype=jnp.float32), GRID_W)
    col = jnp.tile(jnp.arange(GRID_W, dtype=jnp.float32), rows)
    ang = jnp.concatenate([r[:, None] * inv, col[:, None] * inv], -1)
    return jnp.cos(ang), jnp.sin(ang)

def apply_rope(x, cos, sin):
    x1, x2 = jnp.split(x, 2, axis=-1)
    return jnp.concatenate([x1 * cos - x2 * sin, x1 * sin + x2 * cos], -1).astype(x.dtype)

def rwkv7_scan(r, w, k, v, kk, a, state0):
    def step(S, inp):
        r_t, w_t, k_t, v_t, kk_t, a_t = inp
        sa = jnp.einsum('bhvk,bhk->bhv', S, -kk_t)
        S = (S * w_t[:, :, None, :] + sa[..., None] * (kk_t * a_t)[:, :, None, :]
             + v_t[..., None] * k_t[:, :, None, :])
        return S, jnp.einsum('bhvk,bhk->bhv', S, r_t)
    xs = tuple(jnp.moveaxis(t, 1, 0) for t in (r, w, k, v, kk, a))
    S, ys = lax.scan(step, state0, xs)
    return jnp.moveaxis(ys, 0, 1), S

def rwkv_feats(pa, mu, w0, w_up, a0, a_up, g_up, k_k, k_a):
    B, L, _ = pa.shape
    pa = pa + (centred_shift(pa) - pa) * mu
    r, k, v, wd, ad, gd = jnp.split(pa, A_SPLITS, axis=-1)
    wd = wd.reshape(B, L, 2, A_DECAY_R)
    ad = ad.reshape(B, L, 2, A_ICLR_R)
    w = jnp.exp(-W_DECAY_SCALE * jax.nn.sigmoid(w0 + jnp.einsum('bldr,drc->bldc', jnp.tanh(wd), w_up)))
    a = jax.nn.sigmoid(a0 + jnp.einsum('bldr,drc->bldc', ad, a_up))
    g = jax.nn.sigmoid(gd) @ g_up
    heads = lambda t: t.reshape(t.shape[:-1] + (A_HEADS, A_HD)).astype(jnp.float32)
    kk = heads(k * k_k)
    kk = kk * lax.rsqrt(jnp.sum(kk * kk, -1, keepdims=True) + 1e-12)
    kd = k[:, :, None] * (1.0 + (a - 1.0) * k_a)
    return heads(r), heads(v), kk, heads(w), heads(a), heads(kd), g

def rwkv_mixer(pa_ctx, pa_lat, mu, w0, w_up, a0, a_up, g_up, k_k, k_a, r_k, gn_g, gn_b, with_ctx):
    fc = rwkv_feats(pa_ctx, mu, w0, w_up, a0, a_up, g_up, k_k, k_a)
    fl = rwkv_feats(pa_lat, mu, w0, w_up, a0, a_up, g_up, k_k, k_a)
    zero = jnp.zeros((pa_lat.shape[0], A_HEADS, A_HD, A_HD), jnp.float32)
    flip = lambda t: jnp.flip(t, 1)

    def bi_scan(f, s0_fwd, s0_bwd):
        r, v, kk, w, a, kd, _ = f
        yf, sf = rwkv7_scan(r, w[:, :, 0], kd[:, :, 0], v, kk, a[:, :, 0], s0_fwd)
        yb, sb = rwkv7_scan(flip(r), flip(w[:, :, 1]), flip(kd[:, :, 1]), flip(v), flip(kk),
                            flip(a[:, :, 1]), s0_bwd)
        return yf + flip(yb), sf, sb

    def finish(f, y, dtype):
        r, v, kk, w, a, kd, g = f
        bonus = jnp.sum(jnp.sum(r[:, :, None] * kd * r_k, -1, keepdims=True), 2) * v
        o = layer_norm(y, gn_g.reshape(A_HEADS, A_HD), gn_b.reshape(A_HEADS, A_HD), RWKV_GN_EPS) + bonus
        return (o.reshape(o.shape[0], o.shape[1], A_W) * g).astype(dtype)

    yc, sfc, sbc = bi_scan(fc, zero, zero)
    yl, _, _ = bi_scan(fl, sfc, sbc)
    out_ctx = finish(fc, yc, pa_ctx.dtype) if with_ctx else None
    return out_ctx, finish(fl, yl, pa_lat.dtype)

def mla_qkv(pb, q_norm, kv_norm, w_uq, w_ukv, rope):
    B, L, _ = pb.shape
    cq, ckv, kr = jnp.split(pb, B_SPLITS, axis=-1)
    q = jnp.swapaxes((rms_norm(cq, q_norm) @ w_uq).reshape(B, L, B_HEADS, B_NOPE + B_ROPE), 1, 2)
    kv = jnp.swapaxes((rms_norm(ckv, kv_norm) @ w_ukv).reshape(B, L, B_HEADS, B_NOPE + B_VD), 1, 2)
    q_nope, q_rope = q[..., :B_NOPE], q[..., B_NOPE:]
    k_nope, v = kv[..., :B_NOPE], kv[..., B_NOPE:]
    kr = kr[:, None]
    if rope is not None:
        cos, sin = rope
        q_rope = apply_rope(q_rope, cos, sin)
        kr = apply_rope(kr, cos, sin)
    q = jnp.concatenate([q_nope, q_rope], -1)
    k = jnp.concatenate([k_nope, jnp.broadcast_to(kr, (B, B_HEADS, L, B_ROPE))], -1)
    return q, k, v

def block_attention(q, k, v):
    B, H, L, dq = q.shape
    nb = L // QBLOCK
    qb = jnp.moveaxis(q.reshape(B, H, nb, QBLOCK, dq), 2, 0)
    scale = dq ** -0.5

    def one(qi):
        s = jnp.einsum('bhqd,bhkd->bhqk', qi, k).astype(jnp.float32) * scale
        p = jax.nn.softmax(s, axis=-1).astype(v.dtype)
        return jnp.einsum('bhqk,bhkd->bhqd', p, v)
    o = lax.map(one, qb)
    return jnp.moveaxis(o, 0, 2).reshape(B, H, L, v.shape[-1])

def mla_mixer(pb_ctx, pb_lat, q_norm, kv_norm, w_uq, w_ukv, rope, with_ctx):
    qc, kc, vc = mla_qkv(pb_ctx, q_norm, kv_norm, w_uq, w_ukv, None)
    ql, kl, vl = mla_qkv(pb_lat, q_norm, kv_norm, w_uq, w_ukv, rope)
    merge = lambda o: jnp.swapaxes(o, 1, 2).reshape(o.shape[0], o.shape[2], B_W)
    o_lat = block_attention(ql, jnp.concatenate([kc, kl], 2), jnp.concatenate([vc, vl], 2))
    o_ctx = merge(block_attention(qc, kc, vc)) if with_ctx else None
    return o_ctx, merge(o_lat)

def retention_gammas():
    h = jnp.arange(C_HEADS, dtype=jnp.float32)
    return jnp.stack([1.0 - 2.0 ** (-5.0 - h), 1.0 - 2.0 ** (-5.5 - h)])

def retention_chunks(q, k, v, gamma, state0):
    B, H, L, dk = q.shape
    dv = v.shape[-1]
    nc = L // CHUNK
    lg = jnp.log(gamma)
    pos = jnp.arange(CHUNK, dtype=jnp.float32)
    diff = pos[:, None] - pos[None, :]
    intra = jnp.where(diff >= 0, jnp.exp(lg[:, None, None] * jnp.maximum(diff, 0.0)), 0.0)
    q_decay = jnp.exp(lg[:, None] * (pos + 1.0))[:, :, None]
    k_decay = jnp.exp(lg[:, None] * (CHUNK - 1.0 - pos))[:, :, None]
    chunk_decay = jnp.exp(lg * CHUNK)[:, None, None]
    split = lambda t: jnp.moveaxis(t.reshape(B, H, nc, CHUNK, t.shape[-1]), 2, 0)

    def step(R, inp):
        qc, kc, vc = inp
        att = jnp.einsum('bhqd,bhkd->bhqk', qc, kc) * intra
        o = jnp.einsum('bhqk,bhkv->bhqv', att, vc) + jnp.einsum('bhqd,bhdv->bhqv', qc, R) * q_decay
        R = R * chunk_decay + jnp.einsum('bhkd,bhkv->bhdv', kc * k_decay, vc)
        return R, o
    R, o = lax.scan(step, state0, (split(q), split(k), split(v)))
    return jnp.moveaxis(o, 0, 2).reshape(B, H, L, dv), R

def ret_qkvg(pc, rope):
    B, L, _ = pc.shape
    q, k, v, gt = jnp.split(pc, C_SPLITS, axis=-1)
    hs = lambda t, d: jnp.swapaxes(t.reshape(B, L, C_HEADS, d), 1, 2)
    q, k, v = hs(q, C_KD), hs(k, C_KD) * C_KD ** -0.5, hs(v, C_VD)
    if rope is not None:
        cos, sin = rope
        q = apply_rope(q, cos, sin)
        k = apply_rope(k, cos, sin)
    return q.astype(jnp.float32), k.astype(jnp.float32), v.astype(jnp.float32), gt

def retention_mixer(pc_ctx, pc_lat, gn_g, gn_b, rope, with_ctx):
    qc, kc, vc, gc = ret_qkvg(pc_ctx, None)
    ql, kl, vl, gl = ret_qkvg(pc_lat, rope)
    gam = retention_gammas()
    zero = jnp.zeros((pc_lat.shape[0], C_HEADS, C_KD, C_VD), jnp.float32)
    flip = lambda t: jnp.flip(t, 2)

    def bi(q, k, v, s0f, s0b):
        of, sf = retention_chunks(q, k, v, gam[0], s0f)
        ob, sb = retention_chunks(flip(q), flip(k), flip(v), gam[1], s0b)
        return of + flip(ob), sf, sb

    def finish(o, gt):
        o = layer_norm(jnp.swapaxes(o, 1, 2), gn_g.reshape(C_HEADS, C_VD), gn_b.reshape(C_HEADS, C_VD),
                       RET_GN_EPS)
        return (o.reshape(o.shape[0], o.shape[1], C_W) * jax.nn.silu(gt)).astype(gt.dtype)

    oc, sfc, sbc = bi(qc, kc, vc, zero, zero)
    ol, _, _ = bi(ql, kl, vl, sfc, sbc)
    out_ctx = finish(oc, gc) if with_ctx else None
    return out_ctx, finish(ol, gl)

def moe(u, router_w, router_b, w1, w3, w2):
    s = jax.nn.sigmoid((u @ router_w).astype(jnp.float32))
    sb = s + router_b
    grouped = sb.reshape(sb.shape[:-1] + (N_GROUPS, EXPERTS_PER_GROUP))
    group_score = jnp.sum(lax.top_k(grouped, 2)[0], -1)
    best = jnp.argmax(group_score, -1)
    in_group = jnp.repeat(best[..., None] == jnp.arange(N_GROUPS), EXPERTS_PER_GROUP, axis=-1)
    _, idx = lax.top_k(jnp.where(in_group, sb, -jnp.inf), TOP_K)
    sel = jnp.take_along_axis(s, idx, -1)
    wts = sel / jnp.sum(sel, -1, keepdims=True) * ROUTE_SCALE
    gates = jnp.sum(jax.nn.one_hot(idx, N_EXPERTS, dtype=jnp.float32) * wts[..., None], -2).astype(u.dtype)
    out = jnp.zeros_like(u)
    for e in range(N_EXPERTS):
        hdn = jax.nn.silu(u @ w1[e]) * (u @ w3[e])
        out = out + gates[..., e:e + 1] * (hdn @ w2[e])
    return out

def setup_inputs(seed: int = 0) -> dict:
    key = jax.random.key(seed)
    ks = iter(jax.random.split(key, 40))
    nrm = lambda shape, s: jax.random.normal(next(ks), shape, jnp.float32) * s
    D = D_MODEL
    chan = jnp.arange(A_W, dtype=jnp.float32) / (A_W - 1)
    decay_speed = -6.5 + 5.0 * chan ** 0.85
    return {
        'x': nrm((BATCH, SEQ, D), 1.0),
        'c': nrm((BATCH, D), 1.0),
        'ctx': nrm((BATCH, CTX_LEN, D), 1.0),
        'c_ctx': nrm((D,), 1.0),
        'mod_w': nrm((DEPTH, D, 6 * D), 0.5 * D ** -0.5),
        'mod_b': nrm((DEPTH, 6 * D), 0.02),
        'w_in': nrm((DEPTH, D, IN_COLS), D ** -0.5),
        'w_out': nrm((DEPTH, MIX_W, D), BETA * MIX_W ** -0.5),
        'rw_mu': jax.random.uniform(next(ks), (DEPTH, A_COLS), jnp.float32),
        'rw_w0': decay_speed + nrm((DEPTH, 2, A_W), 0.1),
        'rw_w_up': nrm((DEPTH, 2, A_DECAY_R, A_W), 0.1 * A_DECAY_R ** -0.5),
        'rw_a0': nrm((DEPTH, 2, A_W), 0.3),
        'rw_a_up': nrm((DEPTH, 2, A_ICLR_R, A_W), 0.3 * A_ICLR_R ** -0.5),
        'rw_g_up': nrm((DEPTH, A_GATE_R, A_W), A_GATE_R ** -0.5),
        'rw_k_k': 0.85 + nrm((DEPTH, A_W), 0.05),
        'rw_k_a': 1.0 + nrm((DEPTH, A_W), 0.05),
        'rw_r_k': nrm((DEPTH, A_HEADS, A_HD), 0.1),
        'rw_gn_g': 1.0 + nrm((DEPTH, A_W), 0.05),
        'rw_gn_b': nrm((DEPTH, A_W), 0.02),
        'mla_q_norm': 1.0 + nrm((DEPTH, B_QR), 0.05),
        'mla_kv_norm': 1.0 + nrm((DEPTH, B_KVR), 0.05),
        'mla_w_uq': nrm((DEPTH, B_QR, B_HEADS * (B_NOPE + B_ROPE)), B_QR ** -0.5),
        'mla_w_ukv': nrm((DEPTH, B_KVR, B_HEADS * (B_NOPE + B_VD)), B_KVR ** -0.5),
        'ret_gn_g': 1.0 + nrm((DEPTH, C_W), 0.05),
        'ret_gn_b': nrm((DEPTH, C_W), 0.02),
        'ln1_g': 1.0 + nrm((DEPTH, D), 0.05),
        'ln1_b': nrm((DEPTH, D), 0.02),
        'ln2_g': 1.0 + nrm((DEPTH, D), 0.05),
        'ln2_b': nrm((DEPTH, D), 0.02),
        'router_w': nrm((D, N_EXPERTS), D ** -0.5),
        'router_b': nrm((N_EXPERTS,), 0.01),
        'exp_w1': nrm((DEPTH, N_EXPERTS, D, D_EXPERT), D ** -0.5),
        'exp_w3': nrm((DEPTH, N_EXPERTS, D, D_EXPERT), D ** -0.5),
        'exp_w2': nrm((DEPTH, N_EXPERTS, D_EXPERT, D), BETA * D_EXPERT ** -0.5),
    }

def reference(x, c, ctx, c_ctx, mod_w, mod_b, w_in, w_out, rw_mu, rw_w0, rw_w_up, rw_a0, rw_a_up,
              rw_g_up, rw_k_k, rw_k_a, rw_r_k, rw_gn_g, rw_gn_b, mla_q_norm, mla_kv_norm, mla_w_uq,
              mla_w_ukv, ret_gn_g, ret_gn_b, ln1_g, ln1_b, ln2_g, ln2_b, router_w, router_b,
              exp_w1, exp_w3, exp_w2):
    rows = x.shape[1] // GRID_W
    rope_b = grid_rope_tables(rows, B_ROPE)
    rope_c = grid_rope_tables(rows, C_KD)
    silu_c = jax.nn.silu(c)
    silu_cc = jax.nn.silu(c_ctx)
    h = ctx
    for l in range(DEPTH):
        with_ctx = l < DEPTH - 1
        sh1, sc1, g1, sh2, sc2, g2 = jnp.split((silu_c @ mod_w[l] + mod_b[l])[:, None, :], 6, axis=-1)
        csh1, csc1, cg1, csh2, csc2, cg2 = jnp.split(silu_cc @ mod_w[l] + mod_b[l], 6, axis=-1)
        pa_l, pb_l, pc_l = jnp.split((x * (1.0 + sc1) + sh1) @ w_in[l], IN_SPLITS, axis=-1)
        pa_c, pb_c, pc_c = jnp.split((h * (1.0 + csc1) + csh1) @ w_in[l], IN_SPLITS, axis=-1)
        a_c, a_l = rwkv_mixer(pa_c, pa_l, rw_mu[l], rw_w0[l], rw_w_up[l], rw_a0[l], rw_a_up[l], rw_g_up[l],
                              rw_k_k[l], rw_k_a[l], rw_r_k[l], rw_gn_g[l], rw_gn_b[l], with_ctx)
        b_c, b_l = mla_mixer(pb_c, pb_l, mla_q_norm[l], mla_kv_norm[l], mla_w_uq[l], mla_w_ukv[l],
                             rope_b, with_ctx)
        r_c, r_l = retention_mixer(pc_c, pc_l, ret_gn_g[l], ret_gn_b[l], rope_c, with_ctx)
        mix_l = jnp.concatenate([a_l, b_l, r_l], axis=-1) @ w_out[l]
        if with_ctx:
            mix_c = jnp.concatenate([a_c, b_c, r_c], axis=-1) @ w_out[l]
            h = layer_norm(ALPHA * h + cg1 * mix_c, ln1_g[l], ln1_b[l])
            ffn_c = moe(h * (1.0 + csc2) + csh2, router_w, router_b, exp_w1[l], exp_w3[l], exp_w2[l])
            h = layer_norm(ALPHA * h + cg2 * ffn_c, ln2_g[l], ln2_b[l])
        x = layer_norm(ALPHA * x + g1 * mix_l, ln1_g[l], ln1_b[l])
        ffn_l = moe(x * (1.0 + sc2) + sh2, router_w, router_b, exp_w1[l], exp_w3[l], exp_w2[l])
        x = layer_norm(ALPHA * x + g2 * ffn_l, ln2_g[l], ln2_b[l])
    return x


_drawn_inputs = setup_inputs


def setup_inputs(seed=0):
    import zlib

    import numpy as np

    out = dict(_drawn_inputs(seed))
    spreads = {}
    factors = {'rw_w_up': 4.574,
     'rw_a0': 3.132,
     'rw_k_k': 9.678,
     'rw_k_a': 4.344,
     'rw_gn_g': 24.495,
     'rw_gn_b': 25.814,
     'mla_q_norm': 8.0,
     'mla_kv_norm': 5.143,
     'ret_gn_g': 5.041,
     'ret_gn_b': 8.0,
     'ln2_b': 2.735}
    for name, (base, spread) in spreads.items():
        noise = np.random.default_rng([zlib.crc32(name.encode()), seed]).standard_normal(out[name].shape)
        drawn = base * np.exp(spread * noise) if base else spread * noise
        out[name] = __import__('jax').numpy.asarray(drawn.astype(out[name].dtype))
    for name, factor in factors.items():
        out[name] = (out[name] * factor).astype(out[name].dtype)
    return out
```

```python
from contextlib import ExitStack
import math

import concourse.bass as bass
from concourse import mybir

F32 = mybir.dt.float32
ALU = mybir.AluOpType
ACT = mybir.ActivationFunctionType
AX = mybir.AxisListType

P = 128
D = 2048
KT = D // P
LAT = 256
CTX = 256
TOK = LAT + CTX
TT = TOK // P
LT = LAT // P
BANK = 512

A_HEADS, A_HD = 8, 64
A_W = A_HEADS * A_HD
A_PAIRS = A_HEADS // 2
CH = 64
DECAY = math.exp(-0.5)
B_HEADS, B_NOPE, B_ROPE, B_VD, B_QR, B_KVR = 8, 128, 64, 128, 512, 256
C_HEADS, C_KD, C_VD = 4, 64, 128
C_W = C_HEADS * C_VD
N_EXPERTS, N_GROUPS, D_EXPERT = 16, 4, 512
ROUTE_SCALE = 2.5
ALPHA = 2 ** 0.25
LN_EPS, RWKV_GN_EPS, KK_EPS = 1e-5, 64e-5, 1e-12

COL_R, COL_K, COL_V = 0, A_W, 2 * A_W
COL_WAD = 3 * A_W
COL_GD = COL_WAD + 128
GD = 96
COL_CQ = COL_GD + GD
COL_CKV = COL_CQ + B_QR
COL_KR = COL_CKV + B_KVR
COL_RQ = COL_KR + B_ROPE
COL_RK = COL_RQ + C_HEADS * C_KD
COL_RV = COL_RK + C_HEADS * C_KD
COL_GT = COL_RV + C_W

V_MU, V_W0, V_A0, V_KK, V_KA, V_RK, V_QN, V_KVN, V_MODB = 0, 14, 22, 30, 34, 38, 42, 46, 48
N_VEC = 80


def const_layout():
    sizes = [("ident", P), ("ones", P), ("zero", P), ("headones", P), ("rot", P), ("cos", LAT), ("sin", LAT),
             ("iota16", N_EXPERTS), ("reset", BANK), ("mask_f", BANK), ("mask_b", BANK), ("lower", 6 * P), ("upper", 6 * P),
             ("headsel", 2), ("eps", 4), ("iota4", 4)]
    at, out = 0, {}
    for name, n in sizes:
        out[name] = (at, n)
        at += n
    return out, at


CONST, N_CONST = const_layout()


STEPS = {
    "vector": ("vst_zero", "acc_zero", "c_silu", "cond", "vecs", "rms_sq", "cq_norm", "ckv_norm", "kr_ready", "ret_qk", "ret_done", "wad_shift", "gd_shift", "kk_sq", "rw_prep", "rw_s_reset", "u_ready", "ln1_rows_used", "gated"),
    "gpsimd": ("pads", "qrz_zero", "rqz_zero", "lw_zero", "rw_zero"),
    "scalar": ("c_sig", "ret_gate", "wad_tanh", "gd_sig", "logits_out", "scored"),
    "tensor": ("mod", "kr_rot", "logits", "logits_t"),
}


def build_program(nc, t):
    with ExitStack() as ctx:
        arena = ctx.enter_context(nc.sbuf_tensor("arena", [P, 52800], F32))
        bank = [ctx.enter_context(nc.psum_tensor(f"bank{i}", [P, BANK], F32)) for i in range(8)]
        S = {}

        def sem(name):
            if name not in S:
                S[name] = ctx.enter_context(nc.semaphore(name))
            return S[name]

        def step(name):
            for engine, names in STEPS.items():
                if name in names:
                    return sem(f"{engine}_steps"), names.index(name) + 1
            raise KeyError(name)

        class Counter:

            def __init__(self, eng, name):
                self.eng, self.name, self.n = eng, name, {}

            def __call__(self, ins, signal=None):
                name = signal or self.name
                if name in sum(STEPS.values(), ()):
                    s, n = step(name)
                    ins.then_inc(s, 1)
                    self.eng.wait_ge(s, n)
                    return
                self.n[name] = self.n.get(name, 0) + 1
                ins.then_inc(sem(name), 1)
                self.eng.wait_ge(sem(name), self.n[name])

        def cols(at, *dims):
            n = math.prod(dims)
            v = arena[:, at:at + n]
            if len(dims) == 2:
                v = v.rearrange("p (a b) -> p a b", a=dims[0])
            elif len(dims) == 3:
                v = v.rearrange("p (a b c) -> p a b c", a=dims[0], b=dims[1])
            elif len(dims) == 4:
                v = v.rearrange("p (a b c d) -> p a b c d", a=dims[0], b=dims[1], c=dims[2])
            return v

        def split(ap, *dims):
            if len(dims) == 2:
                return ap.rearrange("p (a b) -> p a b", a=dims[0])
            return ap.rearrange("p (a b c) -> p a b c", a=dims[0], b=dims[1])

        at = 0

        def take(*dims):
            nonlocal at
            v = cols(at, *dims)
            at += math.prod(dims)
            return v

        cst = take(N_CONST)
        vec = take(N_VEC)
        cT = take(KT, 2)
        modT = take(32, 2)
        small = take(600)
        acc = take(4, D)
        gaterow0 = at
        x0 = at
        xT = cols(x0, KT, TOK)
        gr0 = x0 + 8192
        wr0 = gr0 + 4096
        o0 = wr0 + 12288
        xtok = cols(o0, TT, D)
        end = 52800

        def const(name):
            a, n = CONST[name]
            return cst[:, a:a + n]

        ident, ones, zero, headones, rot = (const(n) for n in ("ident", "ones", "zero", "headones", "rot"))
        cosT, sinT, reset = const("cos"), const("sin"), const("reset")
        lower, upper = split(const("lower"), 6, P), split(const("upper"), 6, P)
        masks = [split(const("mask_f"), 4, P), split(const("mask_b"), 4, P)]
        headsel = const("headsel")
        eps = const("eps")

        a2 = o0

        def out(*dims):
            nonlocal a2
            v = cols(a2, *dims)
            a2 += math.prod(dims)
            return v

        cq = out(4, LAT)
        ckv = out(2, TOK)
        kr = out(TOK)
        ret0 = a2
        rq = out(2, LAT)
        rk = out(2, TOK)
        rv = out(TT, C_W)
        gt = out(LT, C_W)
        ret1 = a2
        rp = out(4, LAT + 2)
        kp = out(4, 2, 258)
        vp = out(4, 2, 258)
        wp = out(2, 258)
        gp = out(LAT + 2)
        assert a2 <= end, a2
        spare0 = a2

        vst = cols(gr0, P)
        crow = cols(gr0 + P, P)
        csig = cols(gr0 + 2 * P, P)
        mring = [cols(wr0 + 4096 * s, 8, BANK) for s in range(3)]
        mrow = cols(gr0, 8, BANK)[0:2]
        wring = [cols(wr0 + 4096 * s, KT, 256) for s in range(3)]
        gring = [cols(gr0 + 1024 * s, 1024) for s in range(4)]

        groups = ([(c, 256) for c in range(0, COL_WAD, 256)] + [(COL_WAD, 224), (COL_CQ, 256), (COL_CQ + 256, 256),
                  (COL_CKV, 256), (COL_KR, 64), (COL_RQ, 256), (COL_RK, 256), (COL_RV, 256), (COL_RV + 256, 256),
                  (COL_GT, 256), (COL_GT + 256, 256)])
        tiles = []
        both = (0, TOK)
        lat = (CTX, TOK)
        for g, (c0, n) in enumerate(groups):
            for j in range(0, n, P):
                c = c0 + j
                w = min(P, n - j)
                if c < COL_K:
                    tiles.append((g, True, j, w, lat, rp[:, c // P, 1:1 + LAT]))
                elif c < COL_V:
                    tiles.append((g, True, j, w, both, kp[:, (c - COL_K) // P, :, 1:257]))
                elif c < COL_WAD:
                    tiles.append((g, True, j, w, both, vp[:, (c - COL_V) // P, :, 1:257]))
                elif c == COL_WAD:
                    tiles.append((g, True, j, w, both, wp[:, :, 1:257]))
                elif c == COL_GD:
                    tiles.append((g, True, j, w, lat, gp[:GD, 1:1 + LAT]))
                elif c < COL_CKV:
                    tiles.append((g, True, j, w, lat, cq[:, (c - COL_CQ) // P, :]))
                elif c < COL_KR:
                    tiles.append((g, True, j, w, both, ckv[:, (c - COL_CKV) // P, :]))
                elif c == COL_KR:
                    tiles.append((g, True, 0, P, both, kr))
                elif c < COL_RK:
                    tiles.append((g, True, j, w, lat, rq[:, (c - COL_RQ) // P, :]))
                elif c < COL_RV:
                    tiles.append((g, True, j, w, both, rk[:, (c - COL_RK) // P, :]))
            if c0 >= COL_RV:
                gate = c0 >= COL_GT
                dst, cc = (gt, c0 - COL_GT) if gate else (rv, c0 - COL_RV)
                for tt in range(LT if gate else TT):
                    t0 = tt * P + (CTX if gate else 0)
                    tiles.append((g, False, 0, 256, (t0, t0 + P), dst[:, tt, cc:cc + 256]))
        last_tile = {g: n for n, (g, *_) in enumerate(tiles)}

        wuq = cols(wr0, 4, 8 * 192)
        wukv = cols(wr0 + 6144, 2, 2048)
        oB = cols(wr0 + 10240, B_HEADS, LAT)
        qn = cols(x0, B_HEADS, LAT)
        qrz = cols(x0 + 2048, B_HEADS, LAT)
        kn = cols(x0 + 4096, B_HEADS, TOK)
        sqq = cols(gr0, 4, LAT)
        sqk = cols(gr0 + 1024, 2, TOK)
        rsq = cols(gr0 + 2048, LAT)
        rsk = cols(gr0 + 2304, TOK)
        qr = cols(gr0 + 2816, 4, LAT)
        rtmpk = cols(gr0 + 3840, LAT)
        vB = cols(wr0, TT, B_HEADS * B_VD)
        prob = [cols(wr0 + 4096 + BANK * s, TOK) for s in range(2)]
        probT = [cols(wr0 + 5120 + BANK * s, TT, P) for s in range(2)]
        mx, den, rden = small[:, 0:16], small[:, 16:32], small[:, 32:48]

        dTall = cols(gr0, C_HEADS * TT, LAT)
        rqz = cols(x0, C_HEADS, LAT)
        att = [cols(x0 + 1024 * (1 + s), TT, LAT) for s in range(2)]
        oC = cols(x0 + 3072, LT, C_W)
        nt = cols(x0 + 4096, LT, C_W)
        rtmp2 = cols(x0 + 5120, BANK)
        gnc = cols(x0 + 6144, 2, C_W)
        oCT = cols(o0, 4, LAT)
        oAT = cols(o0 + 1024, 4, LAT)
        stat = small[:, 48:304]

        b1 = x0

        def r1(*dims):
            nonlocal b1
            v = cols(b1, *dims)
            b1 += math.prod(dims)
            return v

        sigw = [r1(TT, 4, P) for _ in range(2)]
        siga = [r1(TT, 4, P) for _ in range(2)]
        kkn = r1(TT, 4, P)
        ks = r1(TT, 4, P)
        rs = r1(LT, 4, P)
        rrk = r1(LT, 4, P)
        vtok = r1(TT, A_W)
        gsig = r1(LAT)
        gup = r1(A_W)
        lw0 = b1
        lw = [r1(A_W) for _ in range(4)]
        wadt = r1(2, 256)
        assert b1 <= wr0 + 10240, (b1, wr0)
        vs = cols(ret0, TT, 4, P)
        sqa = cols(ret0 + 2048, 4, TOK)
        pools = [[lw0, wr0 + 10240], [ret0, ret1], [ret1, end]]

        def tmp(*dims):
            n = math.prod(dims)
            for p in pools:
                if p[1] - p[0] >= n:
                    v = cols(p[0], *dims)
                    p[0] += n
                    return v
            raise AssertionError((pools, dims))

        arp = tmp(4, 2, P)
        bz = tmp(A_HEADS, P)
        kz = tmp(A_HEADS, P)
        rz = [tmp(4, P) for _ in range(2)]
        btz = [tmp(A_W) for _ in range(2)]
        ktz = [tmp(A_W) for _ in range(2)]
        um = tmp(4, 4, P)
        yacc = tmp(LT, A_W)
        sst = [tmp(4, P) for _ in range(2)]
        cum = [tmp(4, P) for _ in range(4)]
        kd = tmp(4, P)
        bb = tmp(4, P)
        atok = tmp(A_W)
        ls, xm, gm, zm = (tmp(4, P) for _ in range(4))
        prod = tmp(4, P)
        w1t = tmp(2, P)
        mv = tmp(2 * P)
        w2 = tmp(2 * P)
        stmp = tmp(2, P)
        pc = small[:, 304:312]
        nka = small[:, 312:316]
        bonus = small[:, 316:332]
        sel_lo, sel_hi = slice(0, 64), slice(64, 128)

        def bc(ap, n, axis):
            shape = list(ap.shape)
            shape.insert(axis, n)
            return ap.unsqueeze(axis).to_broadcast(shape)

        block = ctx.enter_context(nc.Block())

        batches = [(0, 0), (0, 1), (0, 2), (0, 3), (1, 1), (1, 0), (1, 3), (1, 2)]
        LEVELS = 5
        mu5, omu = small[:, 332:346], small[:, 346:360]
        cols_a = small[:, 360:384]
        umf = um.rearrange("p a b c -> p (a b c)")
        gna = split(umf[:, 0:2 * A_W], 2, A_W)
        na = split(umf[:, 2 * A_W:4 * A_W], LT, A_W)

        x1 = cols(x0, LT, D)
        ln = cols(x0 + 4096, 2, D)
        ub = cols(x0 + 12288, LT, D)
        uT = cols(x0 + 8192, KT, LAT)
        rw0 = o0 + 2048 + 6 * 2048
        rwt = cols(rw0, KT, N_EXPERTS)
        rbias = cols(rw0 + 256, N_EXPERTS)
        lgT = cols(rw0 + 272, LAT)
        woring = [cols(o0 + 2048 + 2048 * s, D) for s in range(6)]
        mix = ([(A_W // P + h, oB[:, h, :]) for h in range(B_HEADS)] +
               [((A_W + B_HEADS * B_VD) // P + c, oCT[:, c, :]) for c in range(4)] +
               [(c, oAT[:, c, :]) for c in range(4)])
        ye = cols(x0 + 4096, LT, D)
        ew0 = x0 + 12288
        ering = [cols(ew0 + 2048 * s, 4, BANK) for s in range(12)]
        h0 = ew0 + 12 * 2048
        hd = cols(h0, LT, D_EXPERT)
        hT = cols(h0 + 1024, 4, LAT)
        hs = cols(h0 + 2048, D_EXPERT)
        assert h0 + 2048 + D_EXPERT <= end
        ln2 = acc[:, 0:2, :]
        g1r, sh2r, sc2r, g2r = (acc[:, i, :] for i in range(4))
        rt0 = 48
        def rt(i):
            return split(small[:, rt0 + 32 * i:rt0 + 32 * (i + 1)], 2, N_EXPERTS)
        def rg(i):
            return split(small[:, rt0 + 288 + 8 * i:rt0 + 288 + 8 * (i + 1)], 2, 4)
        gates = rt(0)
        @block.sync
        def _(sp):
            sp.wait_ge(*step("acc_zero"))
            sp.dma_start(acc[0:1, :, :].rearrange("p a b -> p (a b)"), t["mod_b"][:, 4096:12288]).then_inc(
                sem("accb_in"), 16)
            sp.dma_start(cst[:, :], t["const"]).then_inc(sem("const_in"), 16)
            sp.dma_start(crow[0:16, :], t["c"].rearrange("a (k p) -> (a k) p", p=P)).then_inc(sem("c_in"), 16)
            sp.dma_start(crow[16:32, :], t["c_ctx"].rearrange("(k p) -> k p", p=P)).then_inc(sem("c_in"), 16)
            for tt in range(TT):
                src = t["ctx"] if tt < 2 else t["x"]
                sp.dma_start(xtok[:, tt, :], src[0, (tt % 2) * P:(tt % 2 + 1) * P, :]).then_inc(
                    sem(f"x_in{tt}"), 16)
            mw = t["mod_w"][0]
            for k in range(KT):
                if k >= 3:
                    sp.wait_ge(sem("mod_used"), k - 2)
                sp.dma_start(mring[k % 3].rearrange("p a b -> p (a b)"), mw[k * P:(k + 1) * P, 0:4096]).then_inc(
                    sem(f"mod_in{k % 3}"), 16)
            win = t["w_in"][0].rearrange("(k p) n -> p k n", p=P)
            for g, (c0, n) in enumerate(groups):
                s = g % 3
                if g == 0:
                    sp.wait_ge(sem("mod_used"), KT)
                if g >= 3:
                    sp.wait_ge(sem("proj"), last_tile[g - 3] + 1)
                sp.dma_start(wring[s][:, :, 0:n], win[:, :, c0:c0 + n]).then_inc(sem(f"win_in{s}"), 16)
                if c0 == COL_KR:
                    sp.dma_start(wring[s][:, :, n:2 * n], win[:, :, c0:c0 + n]).then_inc(sem("kr_in"), 16)

            sp.wait_ge(sem("proj"), len(tiles))
            sp.dma_start(wuq, t["mla_w_uq"][0].rearrange("(k p) n -> p k n", p=P)).then_inc(sem("uq_in"), 16)
            sp.dma_start(wukv, t["mla_w_ukv"][0].rearrange("(k p) n -> p k n", p=P)).then_inc(sem("ukv_in"), 16)
            sp.wait_ge(sem("qr_ready"), 4)
            sp.wait_ge(sem("rms_sum"), 2)
            sp.dma_start(dTall.rearrange("p a b -> p (a b)"), t["decay"]).then_inc(sem("decay_in"), 16)
            sp.wait_ge(sem("scores"), 2 * B_HEADS)
            sp.dma_start(gnc[:, 0, :], t["ret_gn_g"][0].partition_broadcast(P)).then_inc(sem("gnc_in"), 16)
            sp.dma_start(gnc[:, 1, :], t["ret_gn_b"][0].partition_broadcast(P)).then_inc(sem("gnc_in"), 16)
            sp.wait_ge(*step("lw_zero"))
            for i, name in enumerate(("rw_w_up", "rw_w_up", "rw_a_up", "rw_a_up")):
                sp.dma_start(lw[i][32 * i:32 * i + 32, :], t[name][0, i % 2]).then_inc(sem("lora_in"), 16)
            sp.dma_start(gup[0:GD, :], t["rw_g_up"][0]).then_inc(sem("gup_in"), 16)
            sp.wait_ge(sem("rw_y"), 8)
            sp.wait_ge(sem("rw_y_mm"), 8)
            sp.dma_start(gna[:, 0, :], t["rw_gn_g"][0].partition_broadcast(P)).then_inc(sem("gna_in"), 16)
            sp.dma_start(gna[:, 1, :], t["rw_gn_b"][0].partition_broadcast(P)).then_inc(sem("gna_in"), 16)
            sp.dma_start(x1, t["x"][0].rearrange("(a p) n -> p a n", p=P)).then_inc(sem("xl_in"), 16)
            sp.dma_start(ln[:, 0, :], t["ln1_g"][0].partition_broadcast(P)).then_inc(sem("ln_in"), 16)
            sp.dma_start(ln[:, 1, :], t["ln1_b"][0].partition_broadcast(P)).then_inc(sem("ln_in"), 16)
            sp.wait_ge(sem("a_t"), LT)
            for n, (kt, _) in enumerate(mix):
                if n >= 6:
                    sp.wait_ge(sem("wo_used"), n - 5)
                sp.dma_start(woring[n % 6], t["w_out"][0, kt * P:(kt + 1) * P, :]).then_inc(sem(f"wo_in{n % 6}"), 16)
            sp.wait_ge(sem("a_t_out"), LT)
            sp.dma_start(rwt, t["router_w"].rearrange("(k p) n -> p k n", p=P)).then_inc(sem("router_in"), 16)
            sp.dma_start(rbias, t["router_b"].partition_broadcast(P)).then_inc(sem("router_in"), 16)
            sp.wait_ge(*step("ln1_rows_used"))
            sp.dma_start(ln2[:, 0, :], t["ln2_g"][0].partition_broadcast(P)).then_inc(sem("ln2_in"), 16)
            sp.dma_start(ln2[:, 1, :], t["ln2_b"][0].partition_broadcast(P)).then_inc(sem("ln2_in"), 16)

            def expert(e, first):
                for s in range(12):
                    if not first and s in (0, 2, 4):
                        sp.wait_ge(sem(f"ew_used{s // 2}"), e)
                    elif not first and s == 6:
                        sp.wait_ge(sem("h_mm"), e)
                    elif not first and s == 8:
                        sp.wait_ge(sem("y_mm"), e * 8)
                    if s < 8:
                        w = t["exp_w1" if s % 2 == 0 else "exp_w3"][0]
                        src = w[bass.ds(e, 1), BANK * (s // 2):BANK * (s // 2 + 1), :].rearrange(
                            "a (k p) n -> p (a k) n", p=P)
                    else:
                        src = t["exp_w2"][0][bass.ds(e, 1), P * (s - 8):P * (s - 7), :].rearrange(
                            "a p (k n) -> p (a k) n", n=BANK)
                    sp.dma_start(ering[s], src).then_inc(sem(f"ew_in{min(4, s // 2)}"), 16)

            sp.wait_ge(*step("logits"))
            expert(0, True)
            with sp.Fori(1, N_EXPERTS) as e:
                expert(e, False)
            for tt in range(LT):
                sp.wait_ge(sem("done"), tt + 1)
                sp.dma_start(t["out"][0, tt * P:(tt + 1) * P, :], x1[:, tt, :]).then_inc(sem("stored"), 16)
            sp.wait_ge(sem("stored"), 16 * LT)
        @block.gpsimd
        def _(pool):
            pool.wait_ge(sem("xt_raw"), KT)
            nc.gpsimd.memset(rp[:, :, 0:LAT + 2:LAT + 1], 0.0)
            nc.gpsimd.memset(kp[:, :, :, 0:258:257].rearrange("p a b c -> p (a b) c"), 0.0)
            nc.gpsimd.memset(vp[:, :, :, 0:258:257].rearrange("p a b c -> p (a b) c"), 0.0)
            nc.gpsimd.memset(wp[:, :, 0:258:257], 0.0)
            nc.gpsimd.memset(gp[:, 0:LAT + 2:LAT + 1], 0.0).then_inc(step("pads")[0], 1)
            mw = t["mod_w"][0]
            pool.wait_ge(*step("mod"))
            for q in range(8):
                s = q % 4
                if q >= 4:
                    pool.wait_ge(sem(f"gate_used{s}"), 1)
                pool.dma_start(gring[s], mw[0:P, 4096 + 1024 * q:4096 + 1024 * (q + 1)]).then_inc(
                    sem(f"gate_in{s}"), 16)
            with pool.Fori(1, KT) as k:
                for q in range(8):
                    s = q % 4
                    pool.wait_ge(sem(f"gate_used{s}"), k * 2 + q // 4)
                    pool.dma_start(gring[s], mw[bass.ds(k * P, P), 4096 + 1024 * q:4096 + 1024 * (q + 1)]).then_inc(
                        sem(f"gate_in{s}"), 16)

            pool.wait_ge(sem("proj"), len(tiles))
            nc.gpsimd.memset(qrz, 0.0).then_inc(step("qrz_zero")[0], 1)
            pool.wait_ge(sem("scores"), 2 * B_HEADS)
            nc.gpsimd.memset(rqz, 0.0).then_inc(step("rqz_zero")[0], 1)
            pool.wait_ge(sem("ret_t_out"), 2)
            pool.wait_ge(sem("ret_att"), 2 * C_HEADS)
            for i in range(4):
                last = nc.gpsimd.memset(lw[i], 0.0)
            last.then_inc(step("lw_zero")[0], 1)
            pool.wait_ge(sem("lora"), 16)
            pool.wait_ge(*step("rw_prep"))
            for v in (bz, kz, rz[0], rz[1], btz[0], btz[1], ktz[0], ktz[1], sst[0], sst[1]):
                last = nc.gpsimd.memset(v, 0.0)
            last.then_inc(step("rw_zero")[0], 1)
        @block.scalar
        def _(act):
            A = Counter(act, "act_chain")
            act.wait_ge(*step("vst_zero"))

            def rows(at, src, n):
                act.dma_start(vst[at:at + n, :], src).then_inc(sem("vec_in"), 16)

            mu = t["rw_mu"][0]
            rows(V_MU, mu[0:13 * P].rearrange("(r p) -> r p", p=P), 13)
            act.dma_start(vst[V_MU + 13:V_MU + 14, 0:GD], mu[13 * P:13 * P + GD].rearrange(
                "(r p) -> r p", p=GD)).then_inc(sem("vec_in"), 16)
            rows(V_W0, t["rw_w0"][0].rearrange("d (r p) -> (d r) p", p=P), 8)
            rows(V_A0, t["rw_a0"][0].rearrange("d (r p) -> (d r) p", p=P), 8)
            rows(V_KK, t["rw_k_k"][0].rearrange("(r p) -> r p", p=P), 4)
            rows(V_KA, t["rw_k_a"][0].rearrange("(r p) -> r p", p=P), 4)
            rows(V_RK, t["rw_r_k"][0].rearrange("h e -> (h e)").rearrange("(r p) -> r p", p=P), 4)
            rows(V_QN, t["mla_q_norm"][0].rearrange("(r p) -> r p", p=P), 4)
            rows(V_KVN, t["mla_kv_norm"][0].rearrange("(r p) -> r p", p=P), 2)
            rows(V_MODB, t["mod_b"][0, 0:4096].rearrange("(r p) -> r p", p=P), 32)
            act.wait_ge(sem("c_in"), 32)
            nc.scalar.activation(csig[0:32, :], crow[0:32, :], ACT.Sigmoid).then_inc(step("c_sig")[0], 1)
            for k in range(KT):
                act.wait_ge(sem("xt_raw"), k + 1)
                nc.scalar.activation(xT[:, k, :], bank[2 + k % 4][:, :], ACT.Copy).then_inc(sem("xt_out"), 1)
            for b in range(8):
                act.wait_ge(sem("mod_used"), KT)
                nc.scalar.activation(mrow[:, b, :], bank[b][0:2, :], ACT.Copy).then_inc(sem("mod_row"), 1)
            act.wait_ge(*step("pads"))
            for n, (g, stationary, j, w, (t0, t1), dst) in enumerate(tiles):
                act.wait_ge(sem("proj"), n + 1)
                rows_ = w if stationary else P
                width = t1 - t0 if stationary else 256
                src = bank[n % 8][0:rows_, 0:width]
                if len(dst.shape) == 3:
                    src = src.rearrange("p (a b) -> p a b", a=2)
                nc.scalar.activation(dst, src, ACT.Copy).then_inc(sem("proj_out"), 1)
            for q in range(16):
                act.wait_ge(sem("rows"), q + 1)
                nc.scalar.activation(acc.rearrange("p a b -> p (a b)")[:, BANK * q:BANK * (q + 1)], bank[q % 2][:, :],
                                     ACT.Copy).then_inc(sem("rows_out"), 1)

            act.wait_ge(sem("rms_sum"), 1)
            A(nc.scalar.activation(rsq, bank[0][:, 0:LAT], ACT.Sqrt, bias=eps[:, 0:1], scale=1.0 / B_QR), "rms_root")
            act.wait_ge(sem("rms_sum"), 2)
            A(nc.scalar.activation(rsk, bank[1][:, :], ACT.Sqrt, bias=eps[:, 0:1], scale=1.0 / B_KVR), "rms_root")
            for p in range(4):
                act.wait_ge(sem("qr_mm"), p + 1)
                nc.scalar.activation(qr[:, p, :], bank[4 + p % 2][:, 0:LAT], ACT.Copy).then_inc(sem("qr_raw"), 1)
            for h in range(B_HEADS):
                act.wait_ge(sem("qn_mm"), h + 1)
                nc.scalar.activation(qn[:, h, :], bank[h % 4][:, 0:LAT], ACT.Copy).then_inc(sem("qn_out"), 1)
            for h in range(B_HEADS):
                act.wait_ge(sem("kn_mm"), h + 1)
                nc.scalar.activation(kn[:, h, :], bank[h % 4][:, :], ACT.Copy).then_inc(sem("kn_out"), 1)
            for n in range(2 * TT):
                act.wait_ge(sem("v_mm"), n + 1)
                nc.scalar.activation(vB[:, n // 2, BANK * (n % 2):BANK * (n % 2 + 1)], bank[4 + n % 4][:, :],
                                     ACT.Copy).then_inc(sem("v_out"), 1)
            for u in range(2 * B_HEADS + 2):
                if u < 2 * B_HEADS:
                    act.wait_ge(sem("row_max"), u + 1)
                    if u >= 2:
                        act.wait_ge(sem("prob_t"), u - 1)
                    A(nc.scalar.activation(prob[u % 2], bank[u % 2][:, :], ACT.Exp, bias=mx[:, u:u + 1],
                                           scale=(B_NOPE + B_ROPE) ** -0.5, accum_out=den[:, u:u + 1]), "exps")
                if 1 <= u <= 2 * B_HEADS:
                    w = u - 1
                    act.wait_ge(sem("prob_t"), w + 1)
                    if w >= 2:
                        act.wait_ge(sem("att_o"), w - 1)
                    nc.scalar.activation(probT[w % 2].rearrange("p a b -> p (a b)"), bank[2 + w % 2][:, :],
                                         ACT.Copy).then_inc(sem("prob_t_out"), 1)
                if u >= 2:
                    w = u - 2
                    act.wait_ge(sem("att_o"), w + 1)
                    nc.scalar.activation(oB[:, w // 2, (w % 2) * P:(w % 2 + 1) * P], bank[4 + w % 2][:, 0:P],
                                         ACT.Copy).then_inc(sem("att_out"), 1)
            for h in range(C_HEADS):
                act.wait_ge(sem("ret_o"), h + 1)
                nc.scalar.activation(oC[:, :, h * P:(h + 1) * P], split(bank[4 + h % 2][:, 0:2 * P], 2, P),
                                     ACT.Copy).then_inc(sem("ret_out"), 1)
            act.wait_ge(sem("variance"), 1)
            st = split(stat[:, 0:24], 3, 8)
            nc.scalar.activation(st[:, 2, :], st[:, 1, :], ACT.Sqrt, bias=eps[:, 0:1], scale=1.0 / C_VD).then_inc(
                sem("norm_root"), 1)
            nc.scalar.activation(nt, gt, ACT.Sigmoid).then_inc(step("ret_gate")[0], 1)
            for q in range(LT):
                act.wait_ge(sem("ret_t"), q + 1)
                nc.scalar.activation(oCT[:, :, q * P:(q + 1) * P], split(bank[5 + q][:, :], 4, P), ACT.Copy).then_inc(
                    sem("ret_t_out"), 1)
            act.wait_ge(*step("wad_shift"))
            nc.scalar.activation(wadt[sel_lo], wadt[sel_lo], ACT.Tanh).then_inc(step("wad_tanh")[0], 1)
            act.wait_ge(*step("gd_shift"))
            nc.scalar.activation(gsig[0:GD, :], gsig[0:GD, :], ACT.Sigmoid).then_inc(step("gd_sig")[0], 1)
            for n in range(16):
                i, c = n // 4, n % 4
                act.wait_ge(sem("lora"), n + 1)
                bias = (V_W0 if i < 2 else V_A0) + 4 * (i % 2) + c
                dst = (sigw if i < 2 else siga)[i % 2][:, :, c, :]
                nc.scalar.activation(dst, split(bank[n % 4][:, :], 4, P), ACT.Sigmoid,
                                     bias=vec[:, bias:bias + 1]).then_inc(sem("lora_out"), 1)
            for tt in range(TT):
                act.wait_ge(sem("v_t"), tt + 1)
                nc.scalar.activation(vtok[:, tt, :], bank[4 + tt][:, :], ACT.Copy).then_inc(sem("v_t_out"), 1)
            for tt in range(TT):
                act.wait_ge(sem("kk_sum"), tt + 1)
                nc.scalar.activation(sqa[:, tt, :], bank[tt][:, :], ACT.Sqrt, bias=eps[:, 2:3]).then_inc(
                    sem("kk_root"), 1)
            for b, (d, tt) in enumerate(batches):
                e_in, e_ex, e_end, e_inv = (cum[0], cum[1], cum[2], cum[3]) if d == 0 else (cum[3], cum[2], cum[1],
                                                                                            cum[0])
                act.wait_ge(sem("rw_cum"), b + 1)
                total = cum[0].rearrange("p a (c e) -> p (a c) e", e=CH)[:, :, CH - 1]
                A(nc.scalar.activation(pc, total, ACT.Exp, scale=-DECAY), "rw_exp")
                A(nc.scalar.activation(e_ex, e_ex, ACT.Exp, scale=-DECAY), "rw_exp")
                A(nc.scalar.activation(e_inv, e_in, ACT.Exp, scale=DECAY), "rw_exp")
                A(nc.scalar.activation(e_in, e_in, ACT.Exp, scale=-DECAY), "rw_exp")
                A(nc.scalar.activation(e_end, e_end, ACT.Exp, scale=-DECAY), "rw_exp")
                act.wait_ge(sem("rw_t"), 3 * b + 1)
                nc.scalar.activation(atok, bank[5][:, :], ACT.Copy)
                for n, dst in ((2, btz), (3, ktz)):
                    act.wait_ge(sem("rw_t"), 3 * b + n)
                    for c, rows in enumerate((sel_lo, sel_hi)):
                        last = nc.scalar.activation(dst[c][rows, :], bank[4 + n][rows, :], ACT.Copy)
                last.then_inc(sem("rw_tok"), 1)
                for hf in range(2):
                    hb = 2 * b + hf
                    act.wait_ge(sem("rw_w1_mm"), hb + 1)
                    nc.scalar.activation(w1t.rearrange("p a b -> p (a b)"), bank[0][:, 0:2 * P], ACT.Copy)
                    act.wait_ge(sem("rw_mv_mm"), hb + 1)
                    nc.scalar.activation(mv, bank[1][:, 0:2 * P], ACT.Copy).then_inc(sem("rw_mv"), 1)
                    act.wait_ge(sem("rw_w2_mm"), hb + 1)
                    nc.scalar.activation(w2, bank[2][:, 0:2 * P], ACT.Copy).then_inc(sem("rw_w2"), 1)

            def root(n, width, groups_, which):
                act.wait_ge(sem("variance"), n)
                st = split(stat[:, 0:3 * groups_], 3, groups_)
                nc.scalar.activation(st[:, 2, :], st[:, 1, :], ACT.Sqrt, bias=eps[:, which:which + 1],
                                     scale=1.0 / width).then_inc(sem("norm_root"), 1)

            root(2, A_HD, 16, 1)
            for q in range(LT):
                act.wait_ge(sem("a_t"), q + 1)
                nc.scalar.activation(oAT[:, :, q * P:(q + 1) * P], split(bank[q][:, :], 4, P), ACT.Copy).then_inc(
                    sem("a_t_out"), 1)
            root(3, D, LT, 0)
            for n in range(8):
                act.wait_ge(sem("u_t"), n + 1)
                nc.scalar.activation(uT[:, 2 * n:2 * n + 2, :], split(bank[n % 4][:, :], 2, LAT), ACT.Copy).then_inc(
                    sem("u_t_out"), 1)
            act.wait_ge(*step("logits"))
            A(nc.scalar.activation(lgT[0:N_EXPERTS, :], bank[4][0:N_EXPERTS, 0:LAT], ACT.Copy), "logits_out")
            act.wait_ge(*step("logits_t"))
            nc.scalar.activation(rt(1), split(bank[5][:, 0:32], 2, N_EXPERTS), ACT.Sigmoid).then_inc(step("scored")[0], 1)

            def expert(e):
                act.wait_ge(sem("h_mm"), e + 1)
                for tt in range(LT):
                    if tt == 1:
                        act.wait_ge(sem("h_out"), e * 2 + 1)
                    nc.scalar.activation(hs, bank[tt][:, :], ACT.Sigmoid).then_inc(sem("silu"), 1)
                for tt in range(LT):
                    act.wait_ge(sem("h_t"), e * 2 + tt + 1)
                    nc.scalar.activation(hT[:, :, tt * P:(tt + 1) * P], split(bank[4 + tt][:, :], 4, P),
                                         ACT.Copy).then_inc(sem("h_t_out"), 1)

            with act.Fori(0, N_EXPERTS) as e:
                expert(e)
            root(4, D, LT, 0)
        @block.vector
        def _(dve):
            V = Counter(dve, "dve_chain")
            nc.vector.memset(vst[:, :], 0.0).then_inc(step("vst_zero")[0], 1)
            V(nc.vector.memset(acc[:, :, :], 0.0), "acc_zero")
            dve.wait_ge(*step("c_sig"))
            nc.vector.tensor_tensor(crow[0:32, :], crow[0:32, :], csig[0:32, :], ALU.mult).then_inc(step("c_silu")[0], 1)
            dve.wait_ge(sem("small_t"), 1)
            V(nc.vector.tensor_copy(cT[:, :, :], bank[0][:, 0:32].rearrange("p (j k) -> p k j", j=2)), "cond")
            dve.wait_ge(sem("small_t"), 2)
            V(nc.vector.tensor_copy(vec[:, :], bank[1][:, 0:N_VEC]), "vecs")
            dve.wait_ge(*step("mod"))
            V(nc.vector.tensor_tensor(modT[:, :, :], split(bank[0][:, 0:64], 32, 2),
                                      vec[:, V_MODB:V_MODB + 32].unsqueeze(2).to_broadcast([P, 32, 2]), ALU.add))
            V(nc.vector.tensor_scalar(modT[:, 16:32, :], modT[:, 16:32, :], 1.0, None, ALU.add))
            for k in range(KT):
                dve.wait_ge(sem("xt_out"), k + 1)
                for j, half in enumerate((slice(CTX, TOK), slice(0, CTX))):
                    last = nc.vector.tensor_scalar(xT[:, k, half], xT[:, k, half], modT[:, 16 + k, j:j + 1],
                                                   modT[:, k, j:j + 1], ALU.mult, ALU.add)
                last.then_inc(sem("xt_mod"), 1)
            dve.wait_ge(sem("accb_in"), 16)

            def gate_rows(k, first):
                for q in range(8):
                    s = q % 4
                    row = acc.rearrange("p a b -> p (a b)")[:, 1024 * q:1024 * (q + 1)]
                    dve.wait_ge(sem(f"gate_in{s}"), k * 32 + 16 * (q // 4 + 1))
                    if not first:
                        dve.wait_ge(sem(f"gate_used{s}"), k * 2 + (q // 4 - 1))
                    nc.vector.scalar_tensor_tensor(row, gring[s], cT[:, k, 0:1] if first else cT[:, bass.ds(k, 1), 0:1].rearrange("p a b -> p (a b)"), row, ALU.mult,
                                                   ALU.add).then_inc(sem(f"gate_used{s}"), 1)

            gate_rows(0, True)
            with dve.Fori(1, KT) as k:
                gate_rows(k, False)

            dve.wait_ge(sem("proj_out"), len(tiles))
            for s in range(4):
                dve.wait_ge(sem(f"gate_used{s}"), 2 * KT)
            nc.vector.tensor_tensor(sqq, cq, cq, ALU.mult)
            V(nc.vector.tensor_tensor(sqk, ckv, ckv, ALU.mult), "rms_sq")
            dve.wait_ge(sem("rms_root"), 1)
            V(nc.vector.reciprocal(rsq, rsq))
            V(nc.vector.tensor_tensor(cq, cq, bc(rsq, 4, 1), ALU.mult))
            for c in range(4):
                ins = nc.vector.tensor_scalar(cq[:, c, :], cq[:, c, :], vec[:, V_QN + c:V_QN + c + 1], None, ALU.mult)
            V(ins, "cq_norm")
            dve.wait_ge(sem("rms_root"), 2)
            V(nc.vector.reciprocal(rsk, rsk))
            V(nc.vector.tensor_tensor(ckv, ckv, bc(rsk, 2, 1), ALU.mult))
            for c in range(2):
                ins = nc.vector.tensor_scalar(ckv[:, c, :], ckv[:, c, :], vec[:, V_KVN + c:V_KVN + c + 1], None,
                                              ALU.mult)
            V(ins, "ckv_norm")
            dve.wait_ge(*step("kr_rot"))
            V(nc.vector.tensor_tensor(rtmpk, bank[2][:, 0:LAT], sinT, ALU.mult))
            V(nc.vector.tensor_tensor(kr[:, CTX:TOK], kr[:, CTX:TOK], cosT, ALU.mult))
            V(nc.vector.tensor_tensor(kr[:, CTX:TOK], kr[:, CTX:TOK], rtmpk, ALU.add), "kr_ready")
            dve.wait_ge(*step("qrz_zero"))
            for p in range(4):
                dve.wait_ge(sem("q_rot"), p + 1)
                V(nc.vector.tensor_tensor(rtmpk, bank[6 + p % 2][:, 0:LAT], sinT, ALU.mult), "q_rot_read")
                V(nc.vector.tensor_tensor(qr[:, p, :], qr[:, p, :], cosT, ALU.mult))
                nc.vector.tensor_tensor(qrz[sel_lo, 2 * p, :], qr[sel_lo, p, :], rtmpk[sel_lo, :], ALU.add)
                V(nc.vector.tensor_tensor(qrz[sel_hi, 2 * p + 1, :], qr[sel_hi, p, :], rtmpk[sel_hi, :], ALU.add),
                  "qr_ready")
            for u in range(2 * B_HEADS + 1):
                if u < 2 * B_HEADS:
                    dve.wait_ge(sem("scores"), u + 1)
                    V(nc.vector.tensor_reduce(mx[:, u:u + 1], bank[u % 2][:, :], AX.X, ALU.max))
                    V(nc.vector.tensor_scalar(mx[:, u:u + 1], mx[:, u:u + 1], -((B_NOPE + B_ROPE) ** -0.5), None,
                                              ALU.mult), "row_max")
                if u >= 1:
                    w = u - 1
                    dve.wait_ge(sem("exps"), w + 1)
                    V(nc.vector.reciprocal(rden[:, w:w + 1], den[:, w:w + 1]))
                    V(nc.vector.tensor_scalar(prob[w % 2], prob[w % 2], rden[:, w:w + 1], None, ALU.mult), "probs")
            rtv = rtmp2.rearrange("p (a b) -> p a b", a=2)
            cos2, sin2 = bc(cosT, 2, 1), bc(sinT, 2, 1)
            dve.wait_ge(*step("rqz_zero"))
            dve.wait_ge(sem("ret_rot"), 1)
            V(nc.vector.tensor_tensor(rtv, split(bank[6][:, :], 2, LAT), sin2, ALU.mult))
            V(nc.vector.tensor_tensor(rq, rq, cos2, ALU.mult))
            nc.vector.tensor_tensor(rqz[sel_lo, 0:4:2, :], rq[sel_lo], rtv[sel_lo], ALU.add)
            V(nc.vector.tensor_tensor(rqz[sel_hi, 1:4:2, :], rq[sel_hi], rtv[sel_hi], ALU.add))
            dve.wait_ge(sem("ret_rot"), 2)
            V(nc.vector.tensor_tensor(rtv, split(bank[7][:, :], 2, LAT), sin2, ALU.mult))
            V(nc.vector.tensor_tensor(rk[:, :, CTX:TOK], rk[:, :, CTX:TOK], cos2, ALU.mult))
            V(nc.vector.tensor_tensor(rk[:, :, CTX:TOK], rk[:, :, CTX:TOK], rtv, ALU.add), "ret_qk")
            dve.wait_ge(sem("decay_in"), 16)
            for h in range(C_HEADS):
                if h >= 2:
                    dve.wait_ge(sem("ret_o"), h - 1)
                for j in range(2):
                    dve.wait_ge(sem("ret_s"), 2 * h + j + 1)
                    nc.vector.tensor_tensor(att[h % 2][:, 2 * j:2 * j + 2, :],
                                            split(bank[(2 * h + j) % 4][:, :], 2, LAT),
                                            dTall[:, h * TT + 2 * j:h * TT + 2 * j + 2, :], ALU.mult).then_inc(
                                                sem("ret_att"), 1)

            def norm(x, scratch, groups_, width, st, root_wait):
                V(nc.vector.tensor_reduce(st[:, 0, :], x, AX.X, ALU.add))
                V(nc.vector.tensor_scalar(st[:, 0, :], st[:, 0, :], -1.0 / width, None, ALU.mult))
                V(nc.vector.tensor_tensor(x, x, bc(st[:, 0, :], width, 2), ALU.add))
                V(nc.vector.tensor_tensor(scratch, x, x, ALU.mult))
                V(nc.vector.tensor_reduce(st[:, 1, :], scratch, AX.X, ALU.add), "variance")
                root_wait()
                V(nc.vector.reciprocal(st[:, 2, :], st[:, 2, :]))
                V(nc.vector.tensor_tensor(x, x, bc(st[:, 2, :], width, 2), ALU.mult))

            dve.wait_ge(sem("ret_out"), C_HEADS)
            norm(oC.rearrange("p a (h e) -> p (a h) e", e=C_VD), nt.rearrange("p a (h e) -> p (a h) e", e=C_VD), 8,
                 C_VD, split(stat[:, 0:24], 3, 8), lambda: dve.wait_ge(sem("norm_root"), 1))
            dve.wait_ge(sem("gnc_in"), 32)
            V(nc.vector.tensor_tensor(oC, oC, bc(gnc[:, 0, :], LT, 1), ALU.mult))
            V(nc.vector.tensor_tensor(oC, oC, bc(gnc[:, 1, :], LT, 1), ALU.add))
            dve.wait_ge(*step("ret_gate"))
            V(nc.vector.tensor_tensor(gt, gt, nt, ALU.mult))
            V(nc.vector.tensor_tensor(oC, oC, gt, ALU.mult), "ret_done")
            dve.wait_ge(sem("ret_t_out"), 2)
            dve.wait_ge(sem("ret_o"), C_HEADS)
            nc.vector.tensor_scalar(mu5, vec[:, V_MU:V_MU + 14], 0.5, None, ALU.mult)
            V(nc.vector.tensor_scalar(omu, vec[:, V_MU:V_MU + 14], -1.0, 1.0, ALU.mult, ALU.add))

            def shift(dst, padded, row, parts=P, signal=None):
                t4 = sqa[0:parts, 0, 0:math.prod(dst.shape[1:])].rearrange("p (a b c) -> p a b c", a=dst.shape[1], b=2)
                prev, cur, nxt = (padded[0:parts, :, i:i + LAT].rearrange("p s (u e) -> p s u e", u=2)
                                  for i in range(3))
                V(nc.vector.tensor_tensor(t4, prev, nxt, ALU.add))
                V(nc.vector.tensor_scalar(t4, t4, mu5[0:parts, row:row + 1], None, ALU.mult))
                V(nc.vector.scalar_tensor_tensor(dst, cur, omu[0:parts, row:row + 1], t4, ALU.mult, ALU.add), signal)

            def tiles4(x, c):
                return x[:, :, c, :].rearrange("p (s u) e -> p s u e", u=2)

            shift(wadt.rearrange("p s (u e) -> p s u e", u=2), wp, 12, signal="wad_shift")
            shift(split(gsig[0:GD, :], 1, LAT).rearrange("p s (u e) -> p s u e", u=2), split(gp[:, :], 1, LAT + 2), 13,
                  parts=GD, signal="gd_shift")
            for c in range(4):
                shift(tiles4(ks, c), kp[:, c], 4 + c)
            for c in range(4):
                shift(tiles4(vs, c), vp[:, c], 8 + c, signal="v_shift")
            for c in range(4):
                shift(tiles4(rs, c), split(rp[:, c, :], 1, LAT + 2), c)
            for c in range(4):
                nc.vector.tensor_scalar(kkn[:, :, c, :], ks[:, :, c, :], vec[:, V_KK + c:V_KK + c + 1], None, ALU.mult)
                last = nc.vector.tensor_scalar(rrk[:, :, c, :], rs[:, :, c, :], vec[:, V_RK + c:V_RK + c + 1], None,
                                               ALU.mult)
            V(last)
            flat = kkn.rearrange("p a b c -> p a (b c)")
            V(nc.vector.tensor_tensor(sqa, flat, flat, ALU.mult), "kk_sq")
            for tt in range(TT):
                dve.wait_ge(sem("kk_root"), tt + 1)
                V(nc.vector.reciprocal(sqa[:, tt, :], sqa[:, tt, :]))
                V(nc.vector.tensor_tensor(flat[:, tt, :], flat[:, tt, :], sqa[:, tt, :], ALU.mult))
            V(nc.vector.tensor_scalar(nka, vec[:, V_KA:V_KA + 4], -1.0, 1.0, ALU.mult, ALU.add), "rw_prep")
            ka = vec[:, V_KA:V_KA + 4]
            dve.wait_ge(*step("rw_zero"))

            def halves(dst, x, y):
                nc.vector.tensor_tensor(dst[sel_lo, 0:8:2, :], x[sel_lo], y[sel_lo], ALU.mult)
                V(nc.vector.tensor_tensor(dst[sel_hi, 1:8:2, :], x[sel_hi], y[sel_hi], ALU.mult))

            nlat = 0
            for b, (d, tt) in enumerate(batches):
                latent = tt >= 2
                q = tt - 2
                sig = sigw[d][:, tt]
                V(nc.vector.tensor_tensor_scan(cum[0].rearrange("p a b -> p (a b)"), reset,
                                               sig.rearrange("p a b -> p (a b)"), 0.0, ALU.mult, ALU.add))
                total = cum[0].rearrange("p a (c e) -> p (a c) e", e=CH)[:, :, CH - 1:CH].to_broadcast([P, 8, CH])
                nc.vector.tensor_tensor(cum[1], cum[0], sig, ALU.subtract)
                c0v, c2v = (x.rearrange("p a (c e) -> p (a c) e", e=CH) for x in (cum[0], cum[2]))
                V(nc.vector.tensor_tensor(c2v, total, c0v, ALU.subtract))
                if d == 1:
                    V(nc.vector.tensor_tensor(cum[3], cum[2], sig, ALU.add))
                nc.vector.tensor_tensor(bb, kkn[:, tt], siga[d][:, tt], ALU.mult)
                V(nc.vector.tensor_tensor(kd, siga[d][:, tt], bc(ka, P, 2), ALU.mult), "rw_cum")
                V(nc.vector.tensor_tensor(kd, kd, bc(nka, P, 2), ALU.add))
                V(nc.vector.tensor_tensor(kd, kd, ks[:, tt], ALU.mult))
                e_in, e_ex, e_end, e_inv = (cum[0], cum[1], cum[2], cum[3]) if d == 0 else (cum[3], cum[2], cum[1],
                                                                                            cum[0])
                dve.wait_ge(sem("rw_exp"), 5 * (b + 1))
                nc.vector.scalar_tensor_tensor(arp[:, :, 0, :], kkn[:, tt], -1.0, e_ex, ALU.mult, ALU.mult)
                halves(bz, bb, e_inv)
                halves(kz, kd, e_inv)
                if latent:
                    nc.vector.tensor_tensor(prod, rrk[:, q], kd, ALU.mult)
                    V(nc.vector.tensor_tensor(arp[:, :, 1, :], rs[:, q], e_in, ALU.mult))
                    for c in range(2):
                        nc.vector.tensor_copy(rz[c][:, :, CH * c:CH * c + CH], arp[:, :, 1, CH * c:CH * c + CH])
                nc.vector.tensor_tensor(bb, bb, e_end, ALU.mult)
                V(nc.vector.tensor_tensor(kd, kd, e_end, ALU.mult), "rw_feat")
                if latent:
                    dve.wait_ge(sem("rw_bonus"), 2 * nlat // 2 + 1)
                    bo = bonus[:, 8 * q:8 * q + 8]
                    if d == 0:
                        V(nc.vector.tensor_copy(bo, bank[4][:, 0:8]), "rw_bonus_out")
                    else:
                        V(nc.vector.tensor_tensor(bo, bo, bank[4][:, 0:8], ALU.add), "rw_bonus_out")
                    nlat += 1
                lo_m, up_m = (lower, upper) if d == 0 else (upper, lower)
                for hf in range(2):
                    hb = 2 * b + hf
                    for j in range(4):
                        dve.wait_ge(sem("rw_mm"), 4 * hb + j + 1)
                        ps = split(bank[j][:, :], 4, P)
                        if latent:
                            ins = nc.vector.tensor_tensor(um[:, j], ps, masks[d], ALU.mult)
                        else:
                            ins = nc.vector.tensor_tensor(um[:, j, 0:4:2], ps[:, 0:4:2], masks[d][:, 0:4:2], ALU.mult)
                        V(ins, "rw_um")
                    dve.wait_ge(sem("rw_l"), hb + 1)
                    V(nc.vector.tensor_tensor(ls, split(bank[4][:, :], 4, P), bc(masks[1 - d][:, 0], 4, 1), ALU.mult),
                      "rw_ls")
                    V(nc.vector.tensor_tensor(xm, ls, bc(lo_m[:, 0], 4, 1), ALU.mult))
                    nc.vector.tensor_tensor(gm, um[:, :, 0], bc(up_m[:, 0], 4, 1), ALU.mult)
                    V(nc.vector.tensor_tensor(xm, xm, bc(ident, 4, 1), ALU.add))
                    V(nc.vector.tensor_tensor(gm, gm, bc(ident, 4, 1), ALU.add), "rw_init")
                    for lv in range(LEVELS):
                        n = LEVELS * hb + lv + 1
                        dve.wait_ge(sem("rw_lx"), n)
                        V(nc.vector.tensor_tensor(zm, split(bank[5][:, :], 4, P), bc(lo_m[:, lv + 1], 4, 1), ALU.mult),
                          "rw_z")
                        dve.wait_ge(sem("rw_xz"), n)
                        if lv < LEVELS - 1:
                            nc.vector.tensor_tensor(xm, xm, split(bank[6][:, :], 4, P), ALU.add)
                        V(nc.vector.tensor_tensor(gm, gm, split(bank[7][:, :], 4, P), ALU.add), "rw_xg")
                    dve.wait_ge(sem("rw_w2"), hb + 1)
                    for i, c in enumerate((0, 1) if d == 0 else (1, 0)):
                        rows = slice(CH * c, CH * c + CH)
                        pv = pc.rearrange("p (a c) -> p a c", c=2)[:, 2 * hf:2 * hf + 2, c]
                        V(nc.vector.tensor_tensor(stmp, sst[i][:, 2 * hf:2 * hf + 2], bc(pv, P, 2), ALU.mult))
                        dve.wait_ge(sem("rw_u_mm"), 2 * hb + i + 1)
                        V(nc.vector.tensor_tensor(w2[rows], w2[rows], bank[3][rows, 0:2 * P], ALU.add), "rw_u")
                        dve.wait_ge(sem("rw_s_mm"), 2 * hb + i + 1)
                        new, ps = sst[1 - i][:, 2 * hf:2 * hf + 2], split(bank[4][:, 0:2 * P], 2, P)
                        nc.vector.tensor_tensor(new[sel_lo, :, 0:64], ps[sel_lo, :, 0:64], stmp[sel_lo, :, 0:64],
                                                ALU.add)
                        V(nc.vector.tensor_tensor(new[sel_hi, :, 64:P], ps[sel_hi, :, 64:P], stmp[sel_hi, :, 64:P],
                                                  ALU.add), "rw_s")
                    if latent:
                        dve.wait_ge(sem("rw_y_mm"), 2 * (nlat - 1) + hf + 1)
                        ya = yacc[:, q, 2 * P * hf:2 * P * (hf + 1)]
                        if d == 0:
                            V(nc.vector.tensor_copy(ya, bank[5][:, 0:2 * P]), "rw_y")
                        else:
                            V(nc.vector.tensor_tensor(ya, ya, bank[5][:, 0:2 * P], ALU.add), "rw_y")
                if b == 3:
                    V(nc.vector.memset(sst[0], 0.0), "rw_s_reset")
            norm(yacc.rearrange("p a (h e) -> p (a h) e", e=A_HD), na.rearrange("p a (h e) -> p (a h) e", e=A_HD), 16,
                 A_HD, split(stat[:, 0:48], 3, 16), lambda: dve.wait_ge(sem("norm_root"), 2))
            dve.wait_ge(sem("gna_in"), 32)
            V(nc.vector.tensor_tensor(yacc, yacc, bc(gna[:, 0, :], LT, 1), ALU.mult))
            V(nc.vector.tensor_tensor(yacc, yacc, bc(gna[:, 1, :], LT, 1), ALU.add))
            for q in range(LT):
                V(nc.vector.tensor_tensor(split(na[:, q, :], 8, A_HD), split(vtok[:, 2 + q, :], 8, A_HD),
                                          bc(bonus[:, 8 * q:8 * q + 8], A_HD, 2), ALU.mult))
            V(nc.vector.tensor_tensor(yacc, yacc, na, ALU.add))
            dve.wait_ge(sem("g_mm"), 2)
            for q in range(LT):
                V(nc.vector.tensor_tensor(yacc[:, q, :], yacc[:, q, :], bank[6 + q][:, :], ALU.mult), "a_done")
            dve.wait_ge(sem("xl_in"), 16)
            for n in range(8):
                tt, c = n // 4, slice(BANK * (n % 4), BANK * (n % 4 + 1))
                dve.wait_ge(sem("wo_used"), KT)
                V(nc.vector.tensor_tensor(ub[:, tt, c], bank[n][:, :], g1r[:, c], ALU.mult), "mix_out")
                V(nc.vector.scalar_tensor_tensor(x1[:, tt, c], x1[:, tt, c], ALPHA, ub[:, tt, c], ALU.mult, ALU.add))
            norm(x1, ub, LT, D, split(stat[:, 0:6], 3, 2), lambda: dve.wait_ge(sem("norm_root"), 3))
            dve.wait_ge(sem("ln_in"), 32)
            V(nc.vector.tensor_tensor(x1, x1, bc(ln[:, 0, :], LT, 1), ALU.mult))
            V(nc.vector.tensor_tensor(x1, x1, bc(ln[:, 1, :], LT, 1), ALU.add))
            V(nc.vector.tensor_scalar(sc2r, sc2r, 1.0, None, ALU.add))
            V(nc.vector.tensor_tensor(ub, x1, bc(sc2r, LT, 1), ALU.mult))
            V(nc.vector.tensor_tensor(ub, ub, bc(sh2r, LT, 1), ALU.add), "u_ready")
            V(nc.vector.memset(ye, 0.0), "ln1_rows_used")
            s_, sb, t1, t2 = rt(1), rt(2), rt(3), rt(4)
            oh1, oh2 = rt(5), rt(6)
            iota16 = bc(const("iota16"), 2, 1)
            iota4 = bc(const("iota4"), 2, 1)
            dve.wait_ge(*step("scored"))
            dve.wait_ge(sem("router_in"), 32)
            V(nc.vector.tensor_tensor(sb, s_, bc(rbias, 2, 1), ALU.add))
            v4 = sb.rearrange("p t (g e) -> p t g e", e=4)
            m_a, n_a, m_b, n_b, gs, ge = (rg(i) for i in range(6))
            nc.vector.tensor_tensor(m_a, v4[:, :, :, 0], v4[:, :, :, 1], ALU.max)
            nc.vector.tensor_tensor(n_a, v4[:, :, :, 0], v4[:, :, :, 1], ALU.min)
            nc.vector.tensor_tensor(m_b, v4[:, :, :, 2], v4[:, :, :, 3], ALU.max)
            V(nc.vector.tensor_tensor(n_b, v4[:, :, :, 2], v4[:, :, :, 3], ALU.min))
            V(nc.vector.tensor_tensor(n_a, n_a, n_b, ALU.max))
            V(nc.vector.tensor_tensor(n_b, m_a, m_b, ALU.min))
            V(nc.vector.tensor_tensor(n_a, n_a, n_b, ALU.max))
            V(nc.vector.tensor_tensor(m_a, m_a, m_b, ALU.max))
            V(nc.vector.tensor_tensor(gs, m_a, n_a, ALU.add))
            one = small[:, 16:48]

            def first_best(x, hot, iota, width, tmp_):
                best, at_ = one[:, 0:2], one[:, 2:4]
                V(nc.vector.tensor_reduce(best, x, AX.X, ALU.max))
                V(nc.vector.tensor_tensor(hot, x, bc(best, width, 2), ALU.is_lt))
                V(nc.vector.tensor_scalar(hot, hot, 100.0, None, ALU.mult))
                V(nc.vector.tensor_tensor(tmp_, hot, iota, ALU.add))
                V(nc.vector.tensor_reduce(at_, tmp_, AX.X, ALU.min))
                V(nc.vector.tensor_tensor(hot, iota, bc(at_, width, 2), ALU.is_equal))

            first_best(gs, ge, iota4, 4, m_b)
            V(nc.vector.tensor_scalar(n_b, ge, 1e30, -1e30, ALU.mult, ALU.add))
            for tt in range(2):
                V(nc.vector.tensor_tensor(split(t1[:, tt], 4, 4), v4[:, tt], bc(ge[:, tt], 4, 2), ALU.mult))
                V(nc.vector.tensor_tensor(split(t1[:, tt], 4, 4), split(t1[:, tt], 4, 4), bc(n_b[:, tt], 4, 2),
                                          ALU.add))
            first_best(t1, oh1, iota16, 16, t2)
            V(nc.vector.tensor_scalar(t2, oh1, -1e30, None, ALU.mult))
            V(nc.vector.tensor_tensor(t1, t1, t2, ALU.add))
            first_best(t1, oh2, iota16, 16, t2)
            V(nc.vector.tensor_tensor(oh1, oh1, oh2, ALU.add))
            V(nc.vector.tensor_tensor(gates, oh1, s_, ALU.mult))
            V(nc.vector.tensor_reduce(one[:, 0:2], gates, AX.X, ALU.add))
            V(nc.vector.reciprocal(one[:, 0:2], one[:, 0:2]))
            V(nc.vector.tensor_tensor(gates, gates, bc(one[:, 0:2], 16, 2), ALU.mult))
            V(nc.vector.tensor_scalar(gates, gates, ROUTE_SCALE, None, ALU.mult), "gated")

            def expert(e):
                for tt in range(LT):
                    dve.wait_ge(sem("silu"), e * 2 + tt + 1)
                    dve.wait_ge(sem("h_mm"), e * 1 + 1)
                    nc.vector.tensor_tensor(hs, hs, bank[tt][:, :], ALU.mult).then_inc(sem("h_1"), 1)
                    dve.wait_ge(sem("h_1"), e * 2 + tt + 1)
                    gate = gates[:, tt, bass.ds(e, 1)]
                    nc.vector.scalar_tensor_tensor(hd[:, tt, :], hs, gate, bank[2 + tt][:, :], ALU.mult,
                                                   ALU.mult).then_inc(sem("h_out"), 1)
                for n in range(8):
                    tt, c = n // 4, slice(BANK * (n % 4), BANK * (n % 4 + 1))
                    dve.wait_ge(sem("y_mm"), e * 8 + n + 1)
                    nc.vector.tensor_tensor(ye[:, tt, c], ye[:, tt, c], bank[4 + n % 4][:, :], ALU.add).then_inc(
                        sem("y_out"), 1)

            with dve.Fori(0, N_EXPERTS) as e:
                expert(e)
            dve.wait_ge(sem("y_out"), 8 * N_EXPERTS)
            V(nc.vector.tensor_tensor(ye, ye, bc(g2r, LT, 1), ALU.mult))
            V(nc.vector.scalar_tensor_tensor(x1.rearrange("p a b -> p (a b)"), x1.rearrange("p a b -> p (a b)"), ALPHA,
                                             ye.rearrange("p a b -> p (a b)"), ALU.mult, ALU.add))
            norm(x1, ye, LT, D, split(stat[:, 0:6], 3, 2), lambda: dve.wait_ge(sem("norm_root"), 4))
            dve.wait_ge(sem("ln2_in"), 32)
            V(nc.vector.tensor_tensor(x1, x1, bc(ln2[:, 0, :], LT, 1), ALU.mult))
            for tt in range(LT):
                V(nc.vector.tensor_tensor(x1[:, tt], x1[:, tt], ln2[:, 1, :], ALU.add), "done")
        @block.tensor
        def _(pe):
            pe.wait_ge(sem("const_in"), 16)
            pe.wait_ge(*step("c_silu"))
            nc.tensor.transpose(bank[0][:, 0:32], crow[0:32, :], ident[0:32, 0:32]).then_inc(sem("small_t"), 1)
            pe.wait_ge(sem("vec_in"), 160)
            nc.tensor.transpose(bank[1][:, 0:N_VEC], vst[0:N_VEC, :], ident[0:N_VEC, 0:N_VEC]).then_inc(
                sem("small_t"), 1)
            for k in range(KT):
                if k >= 4:
                    pe.wait_ge(sem("xt_out"), k - 3)
                for tt in range(TT):
                    if k == 0:
                        pe.wait_ge(sem(f"x_in{tt}"), 16)
                    last = nc.tensor.transpose(bank[2 + k % 4][:, tt * P:(tt + 1) * P],
                                               xtok[:, tt, k * P:(k + 1) * P], ident)
                last.then_inc(sem("xt_raw"), 1)
            pe.wait_ge(*step("cond"))
            pe.wait_ge(*step("vecs"))
            pe.wait_ge(sem("xt_out"), KT)
            for k in range(KT):
                pe.wait_ge(sem(f"mod_in{k % 3}"), 16 * (k // 3 + 1))
                for b in range(8):
                    last = nc.tensor.matmul(bank[b][0:2, :], cT[:, k, :], mring[k % 3][:, b, :], start=(k == 0),
                                            stop=(k == KT - 1))
                last.then_inc(sem("mod_used"), 1)
            for b in range(8):
                pe.wait_ge(sem("mod_row"), b + 1)
            for c in range(32):
                last = nc.tensor.transpose(bank[0][:, 2 * c:2 * c + 2], mrow[:, c // 4, (c % 4) * P:(c % 4 + 1) * P],
                                           ident[0:2, 0:2])
            last.then_inc(step("mod")[0], 1)
            for n, (g, stationary, j, w, (t0, t1), dst) in enumerate(tiles):
                if n == 0 or g != tiles[n - 1][0]:
                    pe.wait_ge(sem(f"win_in{g % 3}"), 16 * (g // 3 + 1))
                    if groups[g][0] == COL_KR:
                        pe.wait_ge(sem("kr_in"), 16)
                if n < 8:
                    pe.wait_ge(sem("xt_mod"), KT)
                else:
                    pe.wait_ge(sem("proj_out"), n - 7)
                for k in range(KT):
                    if stationary:
                        last = nc.tensor.matmul(bank[n % 8][0:w, 0:t1 - t0], wring[g % 3][:, k, j:j + w],
                                                xT[:, k, t0:t1], start=(k == 0), stop=(k == KT - 1))
                    else:
                        last = nc.tensor.matmul(bank[n % 8][:, 0:256], xT[:, k, t0:t1], wring[g % 3][:, k, :],
                                                start=(k == 0), stop=(k == KT - 1))
                last.then_inc(sem("proj"), 1)
            for s in range(4):
                pe.wait_ge(sem(f"gate_used{s}"), 2 * KT)
            for q in range(16):
                pe.wait_ge(sem("proj_out"), len(tiles))
                if q >= 2:
                    pe.wait_ge(sem("rows_out"), q - 1)
                nc.tensor.matmul(bank[q % 2][:, :], ones, acc.rearrange("p a b -> p (a b)")[:, BANK * q:BANK * (q + 1)],
                                 start=True, stop=True).then_inc(sem("rows"), 1)
            pe.wait_ge(*step("rms_sq"))
            pe.wait_ge(sem("rows_out"), 16)
            for c in range(4):
                last = nc.tensor.matmul(bank[0][:, 0:LAT], ones, sqq[:, c, :], start=(c == 0), stop=(c == 3))
            last.then_inc(sem("rms_sum"), 1)
            for c in range(2):
                last = nc.tensor.matmul(bank[1][:, :], ones, sqk[:, c, :], start=(c == 0), stop=(c == 1))
            last.then_inc(sem("rms_sum"), 1)
            nc.tensor.matmul(bank[2][:, 0:LAT], rot, kr[:, CTX:TOK], start=True, stop=True).then_inc(step("kr_rot")[0], 1)
            pe.wait_ge(sem("uq_in"), 16)
            pe.wait_ge(*step("cq_norm"))
            wuq_h = wuq.rearrange("p k (h e) -> p k h e", e=B_NOPE + B_ROPE)
            for p in range(4):
                if p >= 2:
                    pe.wait_ge(sem("qr_raw"), p - 1)
                for c in range(4):
                    for o in range(2):
                        last = nc.tensor.matmul(bank[4 + p % 2][64 * o:64 * o + 64, 0:LAT],
                                                wuq_h[:, c, 2 * p + o, B_NOPE:], cq[:, c, :], start=(c == 0),
                                                stop=(c == 3), skip_group_check=True)
                last.then_inc(sem("qr_mm"), 1)
                if p >= 1:
                    w = p - 1
                    pe.wait_ge(sem("qr_raw"), w + 1)
                    if w >= 2:
                        pe.wait_ge(sem("q_rot_read"), w - 1)
                    nc.tensor.matmul(bank[6 + w % 2][:, 0:LAT], rot, qr[:, w, :], start=True, stop=True).then_inc(
                        sem("q_rot"), 1)
            pe.wait_ge(sem("qr_raw"), 4)
            pe.wait_ge(sem("q_rot_read"), 2)
            nc.tensor.matmul(bank[7][:, 0:LAT], rot, qr[:, 3, :], start=True, stop=True).then_inc(sem("q_rot"), 1)
            pe.wait_ge(sem("rms_root"), 2)
            pe.wait_ge(*step("kr_ready"))
            for h in range(B_HEADS):
                if h >= 4:
                    pe.wait_ge(sem("qn_out"), h - 3)
                for c in range(4):
                    last = nc.tensor.matmul(bank[h % 4][:, 0:LAT], wuq_h[:, c, h, 0:B_NOPE], cq[:, c, :],
                                            start=(c == 0), stop=(c == 3))
                last.then_inc(sem("qn_mm"), 1)
            pe.wait_ge(sem("ukv_in"), 16)
            pe.wait_ge(*step("ckv_norm"))
            wukv_h = wukv.rearrange("p k (h e) -> p k h e", e=B_NOPE + B_VD)
            for h in range(B_HEADS):
                pe.wait_ge(sem("qn_out"), min(8, h + 5))
                if h >= 4:
                    pe.wait_ge(sem("kn_out"), h - 3)
                for c in range(2):
                    last = nc.tensor.matmul(bank[h % 4][:, :], wukv_h[:, c, h, 0:B_NOPE], ckv[:, c, :],
                                            start=(c == 0), stop=(c == 1))
                last.then_inc(sem("kn_mm"), 1)
            pe.wait_ge(sem("qr_ready"), 4)
            for n in range(2 * TT):
                if n >= 4:
                    pe.wait_ge(sem("v_out"), n - 3)
                tt, half = n // 2, n % 2
                for c in range(2):
                    last = nc.tensor.matmul(bank[4 + n % 4][:, :], ckv[:, c, tt * P:(tt + 1) * P],
                                            wukv_h[:, c, 4 * half:4 * half + 4, B_NOPE:], start=(c == 0),
                                            stop=(c == 1))
                last.then_inc(sem("v_mm"), 1)
            pe.wait_ge(sem("kn_out"), B_HEADS)
            pe.wait_ge(sem("v_out"), 2 * TT)
            for u in range(2 * B_HEADS + 2):
                if u < 2 * B_HEADS:
                    h, q = u // 2, slice((u % 2) * P, (u % 2 + 1) * P)
                    if u >= 2:
                        pe.wait_ge(sem("exps"), u - 1)
                    nc.tensor.matmul(bank[u % 2][:, :], qn[:, h, q], kn[:, h, :], start=True, stop=False)
                    nc.tensor.matmul(bank[u % 2][:, :], qrz[:, h, q], kr, start=False, stop=True).then_inc(
                        sem("scores"), 1)
                if 1 <= u <= 2 * B_HEADS:
                    w = u - 1
                    pe.wait_ge(sem("probs"), w + 1)
                    if w >= 2:
                        pe.wait_ge(sem("prob_t_out"), w - 1)
                    for tt in range(TT):
                        last = nc.tensor.transpose(bank[2 + w % 2][:, tt * P:(tt + 1) * P],
                                                   prob[w % 2][:, tt * P:(tt + 1) * P], ident)
                    last.then_inc(sem("prob_t"), 1)
                if u >= 2:
                    w = u - 2
                    h = w // 2
                    pe.wait_ge(sem("prob_t_out"), w + 1)
                    if w >= 2:
                        pe.wait_ge(sem("att_out"), w - 1)
                    for tt in range(TT):
                        last = nc.tensor.matmul(bank[4 + w % 2][:, 0:P], vB[:, tt, h * P:(h + 1) * P],
                                                probT[w % 2][:, tt, :], start=(tt == 0), stop=(tt == TT - 1))
                    last.then_inc(sem("att_o"), 1)
            for c in range(2):
                last = nc.tensor.matmul(bank[6][:, c * LAT:(c + 1) * LAT], rot, rq[:, c, :], start=True, stop=True,
                                        skip_group_check=True)
            last.then_inc(sem("ret_rot"), 1)
            for c in range(2):
                last = nc.tensor.matmul(bank[7][:, c * LAT:(c + 1) * LAT], rot, rk[:, c, CTX:TOK], start=True,
                                        stop=True, skip_group_check=True)
            last.then_inc(sem("ret_rot"), 1)
            pe.wait_ge(*step("ret_qk"))
            pe.wait_ge(sem("prob_t_out"), 2 * B_HEADS)
            pe.wait_ge(sem("att_out"), 2 * B_HEADS)
            for h in range(C_HEADS + 1):
                if h < C_HEADS:
                    for j in range(2):
                        n = 2 * h + j
                        if n >= 4:
                            pe.wait_ge(sem("ret_att"), n - 3)
                        for kt in range(2 * j, 2 * j + 2):
                            last = nc.tensor.matmul(bank[n % 4][:, (kt % 2) * LAT:(kt % 2 + 1) * LAT],
                                                    rk[:, h // 2, kt * P:(kt + 1) * P], rqz[:, h, :], start=True,
                                                    stop=True, skip_group_check=True)
                        last.then_inc(sem("ret_s"), 1)
                if h >= 1:
                    w = h - 1
                    pe.wait_ge(sem("ret_att"), 2 * w + 2)
                    if w >= 2:
                        pe.wait_ge(sem("ret_out"), w - 1)
                    for q in range(LT):
                        for kt in range(TT):
                            last = nc.tensor.matmul(bank[4 + w % 2][:, q * P:(q + 1) * P],
                                                    att[w % 2][:, kt, q * P:(q + 1) * P], rv[:, kt, w * P:(w + 1) * P],
                                                    start=(kt == 0), stop=(kt == TT - 1), skip_group_check=True)
                    last.then_inc(sem("ret_o"), 1)
            pe.wait_ge(*step("ret_done"))
            for q in range(LT):
                for c in range(4):
                    last = nc.tensor.transpose(bank[5 + q][:, c * P:(c + 1) * P], oC[:, q, c * P:(c + 1) * P], ident)
                last.then_inc(sem("ret_t"), 1)
            pe.wait_ge(*step("wad_tanh"))
            pe.wait_ge(sem("lora_in"), 64)
            for n in range(16):
                if n >= 4:
                    pe.wait_ge(sem("lora_out"), n - 3)
                nc.tensor.matmul(bank[n % 4][:, :], lw[n // 4][:, (n % 4) * P:(n % 4 + 1) * P],
                                 wadt.rearrange("p a b -> p (a b)"), start=True, stop=True).then_inc(sem("lora"), 1)
            pe.wait_ge(sem("v_shift"), 4)
            pe.wait_ge(sem("ret_t_out"), 2)
            for tt in range(TT):
                for c in range(4):
                    last = nc.tensor.transpose(bank[4 + tt][:, c * P:(c + 1) * P], vs[:, tt, c, :], ident)
                last.then_inc(sem("v_t"), 1)
            pe.wait_ge(*step("kk_sq"))
            pe.wait_ge(sem("lora_out"), 16)
            for tt in range(TT):
                nc.tensor.matmul(bank[tt][:, :], headones, sqa[:, tt, :], start=True, stop=True).then_inc(
                    sem("kk_sum"), 1)
            pe.wait_ge(sem("v_t_out"), TT)
            pe.wait_ge(sem("kk_root"), TT)
            nlat = 0
            for b, (d, tt) in enumerate(batches):
                latent = tt >= 2
                pe.wait_ge(sem("rw_feat"), b + 1)
                for n, src in enumerate((arp[:, :, 0, :], bb, kd)):
                    for c in range(4):
                        last = nc.tensor.transpose(bank[5 + n][:, c * P:(c + 1) * P], src[:, c, :], ident)
                    last.then_inc(sem("rw_t"), 1)
                if latent:
                    for c in range(4):
                        last = nc.tensor.matmul(bank[4][:, 2 * c:2 * c + 2], prod[:, c, :], headsel, start=True,
                                                stop=True, skip_group_check=True)
                    last.then_inc(sem("rw_bonus"), 1)
                    nlat += 1
                for hf in range(2):
                    hb = 2 * b + hf
                    if hb >= 1:
                        pe.wait_ge(sem("rw_w2"), hb)
                        pe.wait_ge(sem("rw_s"), 2 * hb)
                    for j in range(4):
                        h = 4 * hf + j
                        out_ = split(bank[j][:, :], 4, P)
                        n = 2 if latent else 1
                        rhs = arp[:, h // 2, 0:n, :]
                        nc.tensor.matmul(out_[:, 0:n], bz[:, h, :], rhs, start=True, stop=True, skip_group_check=True)
                        nc.tensor.matmul(out_[:, 2:2 + n], kz[:, h, :], rhs, start=True, stop=True,
                                         skip_group_check=True).then_inc(sem("rw_mm"), 1)
                    if latent and hf == 0:
                        pe.wait_ge(sem("rw_bonus_out"), nlat)
                    for j in range(4):
                        h = 4 * hf + j
                        last = nc.tensor.matmul(bank[4][:, j * P:(j + 1) * P], arp[:, h // 2, 0, :], bz[:, h, :],
                                                start=True, stop=True, skip_group_check=True)
                    last.then_inc(sem("rw_l"), 1)
                    pe.wait_ge(sem("rw_init"), hb + 1)
                    pe.wait_ge(sem("rw_tok"), b + 1)
                    n_y = 2 * (nlat - 1) + hf if latent else 2 * nlat
                    if n_y > 0:
                        pe.wait_ge(sem("rw_y"), n_y)
                    for lv in range(LEVELS):
                        n = LEVELS * hb + lv
                        if lv:
                            pe.wait_ge(sem("rw_xg"), n)
                        for j in range(4):
                            last = nc.tensor.matmul(bank[5][:, j * P:(j + 1) * P], um[:, j, 0], xm[:, j, :],
                                                    start=True, stop=True, skip_group_check=True)
                        last.then_inc(sem("rw_lx"), 1)
                        pe.wait_ge(sem("rw_z"), n + 1)
                        if lv < LEVELS - 1:
                            for j in range(4):
                                nc.tensor.matmul(bank[6][:, j * P:(j + 1) * P], gm[:, j, :], zm[:, j, :],
                                                 start=True, stop=True, skip_group_check=True)
                        for j in range(4):
                            last = nc.tensor.matmul(bank[7][:, j * P:(j + 1) * P], zm[:, j, :], gm[:, j, :],
                                                    start=True, stop=True, skip_group_check=True)
                        last.then_inc(sem("rw_xz"), 1)
                    pe.wait_ge(sem("rw_xg"), LEVELS * (hb + 1))
                    for j in range(4):
                        h = 4 * hf + j
                        last = nc.tensor.matmul(bank[0][64 * (j % 2):64 * (j % 2) + 64, (j // 2) * P:(j // 2 + 1) * P],
                                                atok[:, 64 * h:64 * h + 64], gm[:, j, :], start=True, stop=True,
                                                skip_group_check=True)
                    last.then_inc(sem("rw_w1_mm"), 1)
                    for j in range(4):
                        h = 4 * hf + j
                        last = nc.tensor.matmul(bank[1][:, j * 64:(j + 1) * 64], um[:, j, 2],
                                                vtok[:, tt, 64 * h:64 * h + 64], start=True, stop=True,
                                                skip_group_check=True)
                    last.then_inc(sem("rw_mv_mm"), 1)
                    pe.wait_ge(sem("rw_mv"), hb + 1)
                    for j in range(4):
                        last = nc.tensor.matmul(bank[2][:, j * 64:(j + 1) * 64], gm[:, j, :],
                                                mv[:, j * 64:(j + 1) * 64], start=True, stop=True,
                                                skip_group_check=True)
                    last.then_inc(sem("rw_w2_mm"), 1)
                    if b == 4 and hf == 0:
                        pe.wait_ge(*step("rw_s_reset"))
                    for i, c in enumerate((0, 1) if d == 0 else (1, 0)):
                        if i or hb:
                            pe.wait_ge(sem("rw_s"), 2 * hb + i)
                        for p in range(2):
                            last = nc.tensor.matmul(bank[3][:, p * P:(p + 1) * P], w1t[:, p, :],
                                                    sst[i][:, 2 * hf + p, :], start=True, stop=True,
                                                    skip_group_check=True)
                        last.then_inc(sem("rw_u_mm"), 1)
                        if latent:
                            for p in range(2):
                                nc.tensor.matmul(bank[5][:, p * P:(p + 1) * P], rz[c][:, 2 * hf + p, :],
                                                 sst[i][:, 2 * hf + p, :], start=(i == 0 and p == 0), stop=False,
                                                 skip_group_check=True)
                        for p in range(2):
                            w = 2 * hf + p
                            nc.tensor.matmul(bank[4][:, p * P:(p + 1) * P], ktz[c][:, w * P:(w + 1) * P],
                                             vtok[:, tt, w * P:(w + 1) * P], start=(p == 0), stop=False,
                                             skip_group_check=True)
                        pe.wait_ge(sem("rw_u"), 2 * hb + i + 1)
                        for p in range(2):
                            w = 2 * hf + p
                            last = nc.tensor.matmul(bank[4][:, p * P:(p + 1) * P], btz[c][:, w * P:(w + 1) * P],
                                                    w2[:, p * P:(p + 1) * P], start=False, stop=True,
                                                    skip_group_check=True)
                        last.then_inc(sem("rw_s_mm"), 1)
                    if latent:
                        for j in range(4):
                            h = 4 * hf + j
                            nc.tensor.matmul(bank[5][:, j * 64:(j + 1) * 64], um[:, j, 1], w2[:, j * 64:(j + 1) * 64],
                                             start=False, stop=False, skip_group_check=True)
                            last = nc.tensor.matmul(bank[5][:, j * 64:(j + 1) * 64], um[:, j, 3],
                                                    vtok[:, tt, 64 * h:64 * h + 64], start=False, stop=(j == 3),
                                                    skip_group_check=True)
                        last.then_inc(sem("rw_y_mm"), 1)
            pe.wait_ge(sem("gup_in"), 16)
            for q in range(LT):
                nc.tensor.matmul(bank[6 + q][:, :], gsig[0:GD, q * P:(q + 1) * P], gup[0:GD, :], start=True,
                                 stop=True).then_inc(sem("g_mm"), 1)
            pe.wait_ge(sem("a_done"), LT)
            for q in range(LT):
                for c in range(4):
                    last = nc.tensor.transpose(bank[q][:, c * P:(c + 1) * P], yacc[:, q, c * P:(c + 1) * P], ident)
                last.then_inc(sem("a_t"), 1)
            pe.wait_ge(sem("a_t_out"), LT)
            for n, (_, x) in enumerate(mix):
                pe.wait_ge(sem(f"wo_in{n % 6}"), 16 * (n // 6 + 1))
                for b in range(8):
                    tt, c = b // 4, b % 4
                    last = nc.tensor.matmul(bank[b][:, :], x[:, tt * P:(tt + 1) * P],
                                            woring[n % 6][:, BANK * c:BANK * (c + 1)], start=(n == 0),
                                            stop=(n == KT - 1))
                last.then_inc(sem("wo_used"), 1)
            pe.wait_ge(*step("u_ready"))
            for n in range(8):
                if n >= 4:
                    pe.wait_ge(sem("u_t_out"), n - 3)
                for k in range(2 * n, 2 * n + 2):
                    for tt in range(LT):
                        last = nc.tensor.transpose(bank[n % 4][:, (k % 2) * LAT + tt * P:(k % 2) * LAT + (tt + 1) * P],
                                                   ub[:, tt, k * P:(k + 1) * P], ident)
                last.then_inc(sem("u_t"), 1)
            pe.wait_ge(sem("router_in"), 32)
            pe.wait_ge(sem("u_t_out"), 8)
            for k in range(KT):
                last = nc.tensor.matmul(bank[4][0:N_EXPERTS, 0:LAT], rwt[:, k, :], uT[:, k, :], start=(k == 0),
                                        stop=(k == KT - 1))
            last.then_inc(step("logits")[0], 1)
            pe.wait_ge(*step("logits_out"))
            for tt in range(LT):
                last = nc.tensor.transpose(bank[5][:, N_EXPERTS * tt:N_EXPERTS * (tt + 1)],
                                           lgT[0:N_EXPERTS, tt * P:(tt + 1) * P], ident[0:N_EXPERTS, 0:N_EXPERTS])
            last.then_inc(step("logits_t")[0], 1)
            pe.wait_ge(*step("gated"))

            def expert(e, first):
                if not first:
                    pe.wait_ge(sem("h_out"), e * 2)
                for j in range(4):
                    pe.wait_ge(sem(f"ew_in{j}"), e * 32 + 32)
                    for w in range(2):
                        for tt in range(LT):
                            for k in range(4 * j, 4 * j + 4):
                                last = nc.tensor.matmul(bank[2 * w + tt][:, :], uT[:, k, tt * P:(tt + 1) * P],
                                                        ering[2 * j + w][:, k % 4, :], start=(k == 0),
                                                        stop=(k == KT - 1))
                    if j < 3:
                        last.then_inc(sem(f"ew_used{j}"), 1)
                last.then_inc(sem("h_mm"), 1)
                for tt in range(LT):
                    pe.wait_ge(sem("h_out"), e * 2 + tt + 1)
                    if not first:
                        pe.wait_ge(sem("y_out"), e * 8)
                    for c in range(4):
                        last = nc.tensor.transpose(bank[4 + tt][:, c * P:(c + 1) * P], hd[:, tt, c * P:(c + 1) * P],
                                                   ident)
                    last.then_inc(sem("h_t"), 1)
                pe.wait_ge(sem("h_t_out"), e * 2 + 2)
                pe.wait_ge(sem("ew_in4"), e * 64 + 64)
                for n in range(8):
                    tt, c = n // 4, n % 4
                    if n >= 4:
                        pe.wait_ge(sem("y_out"), e * 8 + n - 3)
                    for f in range(4):
                        last = nc.tensor.matmul(bank[4 + n % 4][:, :], hT[:, f, tt * P:(tt + 1) * P],
                                                ering[8 + f][:, c, :], start=(f == 0), stop=(f == 3))
                    last.then_inc(sem("y_mm"), 1)

            expert(0, True)
            with pe.Fori(1, N_EXPERTS) as e:
                expert(e, False)


_INS = ["x", "c", "ctx", "c_ctx", "mod_w", "mod_b", "w_in", "w_out", "rw_mu", "rw_w0", "rw_w_up", "rw_a0", "rw_a_up",
        "rw_g_up", "rw_k_k", "rw_k_a", "rw_r_k", "rw_gn_g", "rw_gn_b", "mla_q_norm", "mla_kv_norm", "mla_w_uq",
        "mla_w_ukv", "ret_gn_g", "ret_gn_b", "ln1_g", "ln1_b", "ln2_g", "ln2_b", "router_w", "router_b", "exp_w1",
        "exp_w3", "exp_w2"]


def _constants():
    import numpy as np

    c = np.zeros((P, N_CONST), np.float32)

    def put(name, a):
        at, n = CONST[name]
        c[:, at:at + n] = np.asarray(a, np.float64).reshape(P, n)

    i = np.arange(P)
    put("ident", np.eye(P))
    put("ones", np.ones((P, P)))
    put("headones", (i[:, None] // A_HD == i[None] // A_HD))
    rot = np.zeros((P, P))
    for d in range(P):
        low = d % 64 < 32
        rot[d + 32 if low else d - 32, d] = -1.0 if low else 1.0
    put("rot", rot)
    n = B_ROPE // 4
    inv = (10000.0 ** (-np.arange(n, dtype=np.float32) / n)).astype(np.float32)
    pos = np.arange(LAT)
    ang = np.concatenate([(pos // 64).astype(np.float32)[:, None] * inv,
                          (pos % 64).astype(np.float32)[:, None] * inv], -1)
    put("cos", np.cos(ang)[:, i % 32].T)
    put("sin", np.sin(ang)[:, i % 32].T)
    put("reset", np.broadcast_to((np.arange(BANK) % CH != 0), (P, BANK)))
    same = i[:, None] // CH == i[None] // CH
    before, upto = (i[:, None] < i[None]) & same, (i[:, None] <= i[None]) & same
    put("mask_f", np.concatenate([before, upto, before, upto], 1))
    put("mask_b", np.concatenate([before.T, upto.T, before.T, upto.T], 1))
    levels = [1, 2, 4, 8, 16, 32]
    low = [(i[:, None] // b == i[None] // b + 1) & (i[:, None] // (2 * b) == i[None] // (2 * b)) for b in levels]
    put("lower", np.concatenate(low, 1))
    put("upper", np.concatenate([m.T for m in low], 1))
    put("headsel", i[:, None] // A_HD == np.arange(2)[None])
    put("eps", np.broadcast_to([LN_EPS, RWKV_GN_EPS, KK_EPS, 0.0], (P, 4)))
    put("iota16", np.broadcast_to(np.arange(N_EXPERTS), (P, N_EXPERTS)))
    put("iota4", np.broadcast_to(np.arange(4), (P, 4)))
    key, query = np.arange(TOK)[:, None] - CTX, np.arange(LAT)[None]
    decay = []
    for h in range(C_HEADS):
        gf, gb = 1.0 - 2.0 ** (-5.0 - h), 1.0 - 2.0 ** (-5.5 - h)
        fwd = np.where(query >= key, gf ** np.maximum(query - key, 0), 0.0)
        ahead = np.where(key >= 0, key - query, LAT - query + key + CTX)
        bwd = np.where(ahead >= 0, gb ** np.maximum(ahead, 0), 0.0)
        decay.append((fwd + bwd) * C_KD ** -0.5)
    decay = np.stack(decay).reshape(C_HEADS, TT, P, LAT).transpose(2, 0, 1, 3).reshape(P, -1)
    return c, np.ascontiguousarray(decay, np.float32)


def kernel(**inputs):
    import numpy as _np
    import concourse.bacc as _bacc
    from concourse import mybir as _mybir
    from concourse.bass_utils import run_bass_kernel_spmd as _run

    nc = _bacc.Bacc("TRN2", target_bir_lowering=False, num_devices=1)
    arrays, args = {}, {}
    tables = dict(zip(("const", "decay"), _constants()))
    for name in _INS + list(tables):
        a = _np.ascontiguousarray(tables[name] if name in tables else inputs[name])
        arrays[f"in_{name}_dram"] = a
        args[name] = nc.dram_tensor(f"in_{name}_dram", a.shape, _mybir.dt.from_np(a.dtype), kind="ExternalInput").ap()
    args["out"] = nc.dram_tensor("out_0_dram", (1, LAT, D), F32, kind="ExternalOutput").ap()
    build_program(nc, args)
    r = _run(nc, [arrays], core_ids=[0])
    return r.results[0]["out_0_dram"]
```

```python
from contextlib import ExitStack
import math

import concourse.bass as bass
from concourse import mybir

F32 = mybir.dt.float32
ALU = mybir.AluOpType
ACT = mybir.ActivationFunctionType
AX = mybir.AxisListType

P = 128
D = 2048
KT = D // P
LAT = 256
CTX = 256
TOK = LAT + CTX
TT = TOK // P
LT = LAT // P
BANK = 512

A_HEADS, A_HD = 8, 64
A_W = A_HEADS * A_HD
A_PAIRS = A_HEADS // 2
CH = 64
DECAY = math.exp(-0.5)
B_HEADS, B_NOPE, B_ROPE, B_VD, B_QR, B_KVR = 8, 128, 64, 128, 512, 256
C_HEADS, C_KD, C_VD = 4, 64, 128
C_W = C_HEADS * C_VD
N_EXPERTS, N_GROUPS, D_EXPERT = 16, 4, 512
ROUTE_SCALE = 2.5
ALPHA = 2 ** 0.25
LN_EPS, RWKV_GN_EPS, KK_EPS = 1e-5, 64e-5, 1e-12

COL_R, COL_K, COL_V = 0, A_W, 2 * A_W
COL_WAD = 3 * A_W
COL_GD = COL_WAD + 128
GD = 96
COL_CQ = COL_GD + GD
COL_CKV = COL_CQ + B_QR
COL_KR = COL_CKV + B_KVR
COL_RQ = COL_KR + B_ROPE
COL_RK = COL_RQ + C_HEADS * C_KD
COL_RV = COL_RK + C_HEADS * C_KD
COL_GT = COL_RV + C_W

V_MU, V_W0, V_A0, V_KK, V_KA, V_RK, V_QN, V_KVN, V_MODB = 0, 14, 22, 30, 34, 38, 42, 46, 48
N_VEC = 80


def const_layout():
    sizes = [("ident", P), ("ones", P), ("zero", P), ("headones", P), ("rot", P), ("cos", LAT), ("sin", LAT),
             ("iota16", N_EXPERTS), ("reset", BANK), ("mask_f", BANK), ("mask_b", BANK), ("lower", 6 * P), ("upper", 6 * P),
             ("headsel", 2), ("eps", 4), ("iota4", 4)]
    at, out = 0, {}
    for name, n in sizes:
        out[name] = (at, n)
        at += n
    return out, at


CONST, N_CONST = const_layout()


STEPS = {
    "vector": ("vst_zero", "acc_zero", "c_silu", "cond", "vecs", "rms_sq", "cq_norm", "ckv_norm", "kr_ready", "ret_qk", "ret_done", "wad_shift", "gd_shift", "kk_sq", "rw_prep", "rw_s_reset", "u_ready", "selected", "onehot"),
    "gpsimd": ("pads", "qrz_zero", "rqz_zero", "lw_zero", "rw_zero", "xg_pad"),
    "scalar": ("c_sig", "ret_gate", "wad_tanh", "gd_sig", "logits_out", "scored"),
    "tensor": ("mod", "kr_rot", "logits", "logits_t", "ranks"),
}


def build_program(nc, t):
    with ExitStack() as ctx:
        starts = ctx.enter_context(nc.sbuf_tensor("starts", [1, 2 * N_EXPERTS + 1], mybir.dt.int32))
        parked = nc.dram_tensor("parked_rows", (1, 4 * D), F32).ap()
        arena = ctx.enter_context(nc.sbuf_tensor("arena", [P, 52800], F32))
        bank = [ctx.enter_context(nc.psum_tensor(f"bank{i}", [P, BANK], F32)) for i in range(8)]
        S = {}

        def sem(name):
            if name not in S:
                S[name] = ctx.enter_context(nc.semaphore(name))
            return S[name]

        def step(name):
            for engine, names in STEPS.items():
                if name in names:
                    return sem(f"{engine}_steps"), names.index(name) + 1
            raise KeyError(name)

        class Counter:

            def __init__(self, eng, name):
                self.eng, self.name, self.n = eng, name, {}

            def __call__(self, ins, signal=None):
                name = signal or self.name
                if name in sum(STEPS.values(), ()):
                    s, n = step(name)
                    ins.then_inc(s, 1)
                    self.eng.wait_ge(s, n)
                    return
                self.n[name] = self.n.get(name, 0) + 1
                ins.then_inc(sem(name), 1)
                self.eng.wait_ge(sem(name), self.n[name])

        def cols(at, *dims):
            n = math.prod(dims)
            v = arena[:, at:at + n]
            if len(dims) == 2:
                v = v.rearrange("p (a b) -> p a b", a=dims[0])
            elif len(dims) == 3:
                v = v.rearrange("p (a b c) -> p a b c", a=dims[0], b=dims[1])
            elif len(dims) == 4:
                v = v.rearrange("p (a b c d) -> p a b c d", a=dims[0], b=dims[1], c=dims[2])
            return v

        def split(ap, *dims):
            if len(dims) == 2:
                return ap.rearrange("p (a b) -> p a b", a=dims[0])
            return ap.rearrange("p (a b c) -> p a b c", a=dims[0], b=dims[1])

        at = 0

        def take(*dims):
            nonlocal at
            v = cols(at, *dims)
            at += math.prod(dims)
            return v

        cst = take(N_CONST)
        vec = take(N_VEC)
        cT = take(KT, 2)
        modT = take(32, 2)
        small = take(600)
        acc = take(4, D)
        gaterow0 = at
        x0 = at
        xT = cols(x0, KT, TOK)
        gr0 = x0 + 8192
        wr0 = gr0 + 4096
        o0 = wr0 + 12288
        xtok = cols(o0, TT, D)
        end = 52800

        def const(name):
            a, n = CONST[name]
            return cst[:, a:a + n]

        ident, ones, zero, headones, rot = (const(n) for n in ("ident", "ones", "zero", "headones", "rot"))
        cosT, sinT, reset = const("cos"), const("sin"), const("reset")
        lower, upper = split(const("lower"), 6, P), split(const("upper"), 6, P)
        masks = [split(const("mask_f"), 4, P), split(const("mask_b"), 4, P)]
        headsel = const("headsel")
        eps = const("eps")

        a2 = o0

        def out(*dims):
            nonlocal a2
            v = cols(a2, *dims)
            a2 += math.prod(dims)
            return v

        cq = out(4, LAT)
        ckv = out(2, TOK)
        kr = out(TOK)
        ret0 = a2
        rq = out(2, LAT)
        rk = out(2, TOK)
        rv = out(TT, C_W)
        gt = out(LT, C_W)
        ret1 = a2
        rp = out(4, LAT + 2)
        kp = out(4, 2, 258)
        vp = out(4, 2, 258)
        wp = out(2, 258)
        gp = out(LAT + 2)
        assert a2 <= end, a2
        spare0 = a2

        vst = cols(gr0, P)
        crow = cols(gr0 + P, P)
        csig = cols(gr0 + 2 * P, P)
        mring = [cols(wr0 + 4096 * s, 8, BANK) for s in range(3)]
        mrow = cols(gr0, 8, BANK)[0:2]
        wring = [cols(wr0 + 4096 * s, KT, 256) for s in range(3)]
        gring = [cols(gr0 + 1024 * s, 1024) for s in range(4)]

        groups = ([(c, 256) for c in range(0, COL_WAD, 256)] + [(COL_WAD, 224), (COL_CQ, 256), (COL_CQ + 256, 256),
                  (COL_CKV, 256), (COL_KR, 64), (COL_RQ, 256), (COL_RK, 256), (COL_RV, 256), (COL_RV + 256, 256),
                  (COL_GT, 256), (COL_GT + 256, 256)])
        tiles = []
        both = (0, TOK)
        lat = (CTX, TOK)
        for g, (c0, n) in enumerate(groups):
            for j in range(0, n, P):
                c = c0 + j
                w = min(P, n - j)
                if c < COL_K:
                    tiles.append((g, True, j, w, lat, rp[:, c // P, 1:1 + LAT]))
                elif c < COL_V:
                    tiles.append((g, True, j, w, both, kp[:, (c - COL_K) // P, :, 1:257]))
                elif c < COL_WAD:
                    tiles.append((g, True, j, w, both, vp[:, (c - COL_V) // P, :, 1:257]))
                elif c == COL_WAD:
                    tiles.append((g, True, j, w, both, wp[:, :, 1:257]))
                elif c == COL_GD:
                    tiles.append((g, True, j, w, lat, gp[:GD, 1:1 + LAT]))
                elif c < COL_CKV:
                    tiles.append((g, True, j, w, lat, cq[:, (c - COL_CQ) // P, :]))
                elif c < COL_KR:
                    tiles.append((g, True, j, w, both, ckv[:, (c - COL_CKV) // P, :]))
                elif c == COL_KR:
                    tiles.append((g, True, 0, P, both, kr))
                elif c < COL_RK:
                    tiles.append((g, True, j, w, lat, rq[:, (c - COL_RQ) // P, :]))
                elif c < COL_RV:
                    tiles.append((g, True, j, w, both, rk[:, (c - COL_RK) // P, :]))
            if c0 >= COL_RV:
                gate = c0 >= COL_GT
                dst, cc = (gt, c0 - COL_GT) if gate else (rv, c0 - COL_RV)
                for tt in range(LT if gate else TT):
                    t0 = tt * P + (CTX if gate else 0)
                    tiles.append((g, False, 0, 256, (t0, t0 + P), dst[:, tt, cc:cc + 256]))
        last_tile = {g: n for n, (g, *_) in enumerate(tiles)}

        wuq = cols(wr0, 4, 8 * 192)
        wukv = cols(wr0 + 6144, 2, 2048)
        oB = cols(wr0 + 10240, B_HEADS, LAT)
        qn = cols(x0, B_HEADS, LAT)
        qrz = cols(x0 + 2048, B_HEADS, LAT)
        kn = cols(x0 + 4096, B_HEADS, TOK)
        sqq = cols(gr0, 4, LAT)
        sqk = cols(gr0 + 1024, 2, TOK)
        rsq = cols(gr0 + 2048, LAT)
        rsk = cols(gr0 + 2304, TOK)
        qr = cols(gr0 + 2816, 4, LAT)
        rtmpk = cols(gr0 + 3840, LAT)
        vB = cols(wr0, TT, B_HEADS * B_VD)
        prob = [cols(wr0 + 4096 + BANK * s, TOK) for s in range(2)]
        probT = [cols(wr0 + 5120 + BANK * s, TT, P) for s in range(2)]
        mx, den, rden = small[:, 0:16], small[:, 16:32], small[:, 32:48]

        dTall = cols(gr0, C_HEADS * TT, LAT)
        rqz = cols(x0, C_HEADS, LAT)
        att = [cols(x0 + 1024 * (1 + s), TT, LAT) for s in range(2)]
        oC = cols(x0 + 3072, LT, C_W)
        nt = cols(x0 + 4096, LT, C_W)
        rtmp2 = cols(x0 + 5120, BANK)
        gnc = cols(x0 + 6144, 2, C_W)
        oCT = cols(o0, 4, LAT)
        oAT = cols(o0 + 1024, 4, LAT)
        stat = small[:, 48:304]

        b1 = x0

        def r1(*dims):
            nonlocal b1
            v = cols(b1, *dims)
            b1 += math.prod(dims)
            return v

        sigw = [r1(TT, 4, P) for _ in range(2)]
        siga = [r1(TT, 4, P) for _ in range(2)]
        kkn = r1(TT, 4, P)
        ks = r1(TT, 4, P)
        rs = r1(LT, 4, P)
        rrk = r1(LT, 4, P)
        vtok = r1(TT, A_W)
        gsig = r1(LAT)
        gup = r1(A_W)
        lw0 = b1
        lw = [r1(A_W) for _ in range(4)]
        wadt = r1(2, 256)
        assert b1 <= wr0 + 10240, (b1, wr0)
        vs = cols(ret0, TT, 4, P)
        sqa = cols(ret0 + 2048, 4, TOK)
        pools = [[lw0, wr0 + 10240], [ret0, ret1], [ret1, end]]

        def tmp(*dims):
            n = math.prod(dims)
            for p in pools:
                if p[1] - p[0] >= n:
                    v = cols(p[0], *dims)
                    p[0] += n
                    return v
            raise AssertionError((pools, dims))

        acc0 = cst.shape[1] + N_VEC + KT * 2 + 32 * 2 + 600
        um = [tmp(2, 4, 4, P), cols(acc0, 2, 4, 4, P)]
        xm, gm, zm = (cols(acc0 + 4096 + 1024 * i, 2, 4, P) for i in range(3))
        w1mv = cols(acc0 + 7168, 2, BANK)
        arp = tmp(4, 2, P)
        bz = tmp(A_HEADS, P)
        kz = tmp(A_HEADS, P)
        yacc = tmp(LT, A_W)
        sst = [tmp(4, P) for _ in range(2)]
        cum = [tmp(4, P) for _ in range(4)]
        kd = tmp(4, P)
        bb = tmp(4, P)
        rr, atok, btok, ktok = ([tmp(4, P) for _ in range(2)] for _ in range(4))
        w2 = tmp(2, 2 * P)
        stmp = tmp(2, 2, P)
        pc = [small[:, 304:312], small[:, 384:392]]
        nka = small[:, 312:316]
        bonus = small[:, 316:332]
        sel_lo, sel_hi = slice(0, 64), slice(64, 128)

        def bc(ap, n, axis):
            shape = list(ap.shape)
            shape.insert(axis, n)
            return ap.unsqueeze(axis).to_broadcast(shape)

        block = ctx.enter_context(nc.Block())

        batches = [(0, 0), (0, 1), (0, 2), (0, 3), (1, 1), (1, 0), (1, 3), (1, 2)]
        LEVELS = 5
        items, evacuated = [], {"vector": 0, "scalar": 0}
        for b_, (_, tt_) in enumerate(batches):
            for kind in ["bonus"] * (tt_ >= 2) + ["a", 0, "b", 1, "k", 2, 3, 4, 5, 6, 7, "low0", "low1"]:
                engine = "scalar" if kind in ("a", "b", "k") else "vector"
                evacuated[engine] += 1
                items.append((b_, kind, engine, evacuated[engine]))

        def items_of(b, part=None):
            own = [n for n, it in enumerate(items) if it[0] == b]
            at_ = (0, 4, 6, 8, 10, 12, 99)
            return own if part is None else own[at_[part]:at_[part + 1]]

        def blocks(x, n, which):
            return x.rearrange("p j (g two n) -> p j g two n", two=2, n=n)[:, :, :, which]

        mu5, omu = small[:, 332:346], small[:, 346:360]
        umf = um[0][:, 0].rearrange("p a b c -> p (a b c)")
        gna = split(umf[:, 0:2 * A_W], 2, A_W)
        na = split(umf[:, 2 * A_W:4 * A_W], LT, A_W)

        x1 = cols(x0, LT, D)
        ln = cols(x0 + 4096, 2, D)
        ub = cols(x0 + 14336, LT, D)
        uT = cols(x0 + 18432, KT, LAT)
        rw0 = o0 + 2048 + 6 * 2048
        rwt = cols(rw0, KT, N_EXPERTS)
        rbias = cols(rw0 + 256, N_EXPERTS)
        lgT = cols(rw0 + 272, LAT)
        woring = [cols(o0 + 2048 + 2048 * s, D) for s in range(6)]
        mix = ([(A_W // P + h, oB[:, h, :]) for h in range(B_HEADS)] +
               [((A_W + B_HEADS * B_VD) // P + c, oCT[:, c, :]) for c in range(4)] +
               [(c, oAT[:, c, :]) for c in range(4)])
        PAIRS = 2 * LAT
        ST = PAIRS // P
        xg = cols(x0 + 4096, KT, PAIRS + P)
        ys = cols(x0 + 14336, KT, PAIRS + P)
        yt = cols(x0 + 4096, ST, D)
        ering = [cols(o0 + 2048 * s, 4, BANK) for s in range(6)]
        hot = cols(o0 + 12288, LT, PAIRS)
        hotT = cols(o0 + 13312, ST, LAT)
        assert o0 + 14336 <= rw0
        hotg = cols(CONST["lower"][0], LT, PAIRS)
        hot2 = cols(CONST["lower"][0] + 2 * BANK, BANK)
        lnt = cols(o0, LT, D)
        hs = cols(CONST["lower"][0], 2, 2, P)
        hT = cols(CONST["lower"][0] + BANK, 4, P)
        route = cols(CONST["reset"][0], P + PAIRS)
        before, iota = route[:, 0:P], route[:, P:P + PAIRS]
        ln2 = acc[:, 0:2, :]
        g1r, sh2r, sc2r, g2r = (acc[:, i, :] for i in range(4))
        rt0 = 48
        def rt(i):
            return split(small[:, rt0 + 32 * i:rt0 + 32 * (i + 1)], 2, N_EXPERTS)
        def rg(i):
            return split(small[:, rt0 + 288 + 8 * i:rt0 + 288 + 8 * (i + 1)], 2, 4)
        cnt, off, base, late, ipos = (small[:, 400 + 16 * i:416 + 16 * i] for i in range(5))
        excl = split(small[:, 480:512], 2, N_EXPERTS)
        pair_at = [small[:, 512 + 2 * i:514 + 2 * i] for i in range(2)]
        gate = [small[:, 516 + 2 * i:518 + 2 * i] for i in range(2)]
        most = small[:, 520:521]
        @block.sync
        def _(sp):
            sp.wait_ge(*step("acc_zero"))
            sp.dma_start(acc[0:1, :, :].rearrange("p a b -> p (a b)"), t["mod_b"][:, 4096:12288]).then_inc(
                sem("accb_in"), 16)
            sp.dma_start(cst[:, :], t["const"]).then_inc(sem("const_in"), 16)
            sp.dma_start(crow[0:16, :], t["c"].rearrange("a (k p) -> (a k) p", p=P)).then_inc(sem("c_in"), 16)
            sp.dma_start(crow[16:32, :], t["c_ctx"].rearrange("(k p) -> k p", p=P)).then_inc(sem("c_in"), 16)
            for tt in range(TT):
                src = t["ctx"] if tt < 2 else t["x"]
                sp.dma_start(xtok[:, tt, :], src[0, (tt % 2) * P:(tt % 2 + 1) * P, :]).then_inc(
                    sem(f"x_in{tt}"), 16)
            mw = t["mod_w"][0]
            for k in range(KT):
                if k >= 3:
                    sp.wait_ge(sem("mod_used"), k - 2)
                sp.dma_start(mring[k % 3].rearrange("p a b -> p (a b)"), mw[k * P:(k + 1) * P, 0:4096]).then_inc(
                    sem(f"mod_in{k % 3}"), 16)
            win = t["w_in"][0].rearrange("(k p) n -> p k n", p=P)
            for g, (c0, n) in enumerate(groups):
                s = g % 3
                if g == 0:
                    sp.wait_ge(sem("mod_used"), KT)
                if g >= 3:
                    sp.wait_ge(sem("proj"), last_tile[g - 3] + 1)
                sp.dma_start(wring[s][:, :, 0:n], win[:, :, c0:c0 + n]).then_inc(sem(f"win_in{s}"), 16)
                if c0 == COL_KR:
                    sp.dma_start(wring[s][:, :, n:2 * n], win[:, :, c0:c0 + n]).then_inc(sem("kr_in"), 16)

            sp.wait_ge(sem("proj"), len(tiles))
            sp.dma_start(wuq, t["mla_w_uq"][0].rearrange("(k p) n -> p k n", p=P)).then_inc(sem("uq_in"), 16)
            sp.dma_start(wukv, t["mla_w_ukv"][0].rearrange("(k p) n -> p k n", p=P)).then_inc(sem("ukv_in"), 16)
            sp.wait_ge(sem("rows_out"), 16)
            sp.dma_start(parked, acc[0:1].rearrange("p a b -> p (a b)")).then_inc(sem("parked"), 16)
            sp.wait_ge(sem("qr_ready"), 4)
            sp.wait_ge(sem("rms_sum"), 2)
            sp.dma_start(dTall.rearrange("p a b -> p (a b)"), t["decay"]).then_inc(sem("decay_in"), 16)
            sp.wait_ge(sem("scores"), 2 * B_HEADS)
            sp.dma_start(gnc[:, 0, :], t["ret_gn_g"][0].partition_broadcast(P)).then_inc(sem("gnc_in"), 16)
            sp.dma_start(gnc[:, 1, :], t["ret_gn_b"][0].partition_broadcast(P)).then_inc(sem("gnc_in"), 16)
            sp.wait_ge(*step("lw_zero"))
            for i, name in enumerate(("rw_w_up", "rw_w_up", "rw_a_up", "rw_a_up")):
                sp.dma_start(lw[i][32 * i:32 * i + 32, :], t[name][0, i % 2]).then_inc(sem("lora_in"), 16)
            sp.dma_start(gup[0:GD, :], t["rw_g_up"][0]).then_inc(sem("gup_in"), 16)
            sp.wait_ge(sem("rw_y"), 8)
            sp.wait_ge(sem("rw_y_mm"), 8)
            sp.dma_start(gna[:, 0, :], t["rw_gn_g"][0].partition_broadcast(P)).then_inc(sem("gna_in"), 16)
            sp.dma_start(gna[:, 1, :], t["rw_gn_b"][0].partition_broadcast(P)).then_inc(sem("gna_in"), 16)
            sp.wait_ge(sem("parked"), 16)
            sp.dma_start(acc.rearrange("p a b -> p (a b)"), parked[0].partition_broadcast(P)).then_inc(sem("rows_in"), 16)
            sp.dma_start(route, t["route"]).then_inc(sem("route_in"), 16)
            sp.dma_start(x1, t["x"][0].rearrange("(a p) n -> p a n", p=P)).then_inc(sem("xl_in"), 16)
            sp.dma_start(ln[:, 0, :], t["ln1_g"][0].partition_broadcast(P)).then_inc(sem("ln_in"), 16)
            sp.dma_start(ln[:, 1, :], t["ln1_b"][0].partition_broadcast(P)).then_inc(sem("ln_in"), 16)
            sp.wait_ge(sem("a_t"), LT)
            for n, (kt, _) in enumerate(mix):
                if n >= 6:
                    sp.wait_ge(sem("wo_used"), n - 5)
                sp.dma_start(woring[n % 6], t["w_out"][0, kt * P:(kt + 1) * P, :]).then_inc(sem(f"wo_in{n % 6}"), 16)
            sp.wait_ge(sem("a_t_out"), LT)
            sp.dma_start(rwt, t["router_w"].rearrange("(k p) n -> p k n", p=P)).then_inc(sem("router_in"), 16)
            sp.dma_start(rbias, t["router_b"].partition_broadcast(P)).then_inc(sem("router_in"), 16)
            sp.wait_ge(*step("u_ready"))
            sp.dma_start(ln2[:, 0, :], t["ln2_g"][0].partition_broadcast(P)).then_inc(sem("ln2_in"), 16)
            sp.dma_start(ln2[:, 1, :], t["ln2_b"][0].partition_broadcast(P)).then_inc(sem("ln2_in"), 16)

            def piece_used(n, i):
                if i < 6:
                    sp.wait_ge(sem("ew_used"), n * 6 + (i + 1))
                elif i < 8:
                    sp.wait_ge(sem("h_mm"), n * 2 + 2)
                else:
                    sp.wait_ge(sem("y_mm"), n * 8 + 2 * (i - 7))

            def expert(n, e, first):
                for i in range(12):
                    if i >= 6:
                        piece_used(n, i - 6)
                    elif not first:
                        piece_used(n - 1, i + 6)
                    if i < 8:
                        w = t["exp_w1" if i % 2 == 0 else "exp_w3"][0]
                        src = w[bass.ds(e, 1), BANK * (i // 2):BANK * (i // 2 + 1), :].rearrange(
                            "a (k p) n -> p (a k) n", p=P)
                    else:
                        src = t["exp_w2"][0][bass.ds(e, 1), :, BANK * (i - 8):BANK * (i - 7)].rearrange(
                            "a (k p) n -> p (a k) n", p=P)
                    sp.dma_start(ering[i % 6], src).then_inc(sem(f"ew_in{i % 6}"), 16)

            sp.wait_ge(sem("wo_used"), KT)
            expert(0, 0, True)
            with sp.Fori(1, N_EXPERTS) as e:
                expert(e, e, False)
            sp.wait_ge(*step("onehot"))
            with sp.If(sp.value_load(starts[0:1, 2 * N_EXPERTS:2 * N_EXPERTS + 1]) > P):
                with sp.Fori(N_EXPERTS, 2 * N_EXPERTS) as n:
                    expert(n, n - N_EXPERTS, False)
            for tt in range(LT):
                sp.wait_ge(sem("done"), tt + 1)
                sp.dma_start(t["out"][0, tt * P:(tt + 1) * P, :], x1[:, tt, :]).then_inc(sem("stored"), 16)
            sp.wait_ge(sem("stored"), 16 * LT)
        @block.gpsimd
        def _(pool):
            pool.wait_ge(sem("xt_raw"), KT)
            nc.gpsimd.memset(rp[:, :, 0:LAT + 2:LAT + 1], 0.0)
            nc.gpsimd.memset(kp[:, :, :, 0:258:257].rearrange("p a b c -> p (a b) c"), 0.0)
            nc.gpsimd.memset(vp[:, :, :, 0:258:257].rearrange("p a b c -> p (a b) c"), 0.0)
            nc.gpsimd.memset(wp[:, :, 0:258:257], 0.0)
            nc.gpsimd.memset(gp[:, 0:LAT + 2:LAT + 1], 0.0).then_inc(step("pads")[0], 1)
            mw = t["mod_w"][0]
            pool.wait_ge(*step("mod"))
            for q in range(8):
                s = q % 4
                if q >= 4:
                    pool.wait_ge(sem(f"gate_used{s}"), 1)
                pool.dma_start(gring[s], mw[0:P, 4096 + 1024 * q:4096 + 1024 * (q + 1)]).then_inc(
                    sem(f"gate_in{s}"), 16)
            with pool.Fori(1, KT) as k:
                for q in range(8):
                    s = q % 4
                    pool.wait_ge(sem(f"gate_used{s}"), k * 2 + q // 4)
                    pool.dma_start(gring[s], mw[bass.ds(k * P, P), 4096 + 1024 * q:4096 + 1024 * (q + 1)]).then_inc(
                        sem(f"gate_in{s}"), 16)

            pool.wait_ge(sem("proj"), len(tiles))
            nc.gpsimd.memset(qrz, 0.0).then_inc(step("qrz_zero")[0], 1)
            pool.wait_ge(sem("scores"), 2 * B_HEADS)
            nc.gpsimd.memset(rqz, 0.0).then_inc(step("rqz_zero")[0], 1)
            pool.wait_ge(sem("ret_t_out"), 2)
            pool.wait_ge(sem("ret_att"), 2 * C_HEADS)
            for i in range(4):
                last = nc.gpsimd.memset(lw[i], 0.0)
            last.then_inc(step("lw_zero")[0], 1)
            pool.wait_ge(sem("lora"), 16)
            pool.wait_ge(*step("rw_prep"))
            pool.wait_ge(sem("parked"), 16)
            for v in (bz, kz, sst[0], sst[1]):
                last = nc.gpsimd.memset(v, 0.0)
            last.then_inc(step("rw_zero")[0], 1)
            for b in range(len(batches)):
                for m, name in ((xm, "rw_gz"), (gm, "rw_w2_mm")):
                    for hf in range(2):
                        if b:
                            pool.wait_ge(sem(name), 2 * LEVELS * b - 1 + hf if m is xm else 2 * b - 1 + hf)
                        nc.gpsimd.tensor_copy(m[:, hf], bc(ident, 4, 1)).then_inc(sem("rw_ident"), 1)
            pool.wait_ge(*step("u_ready"))
            nc.gpsimd.memset(xg[:, :, PAIRS:], 0.0).then_inc(step("xg_pad")[0], 1)
        @block.scalar
        def _(act):
            A = Counter(act, "act_chain")
            act.wait_ge(*step("vst_zero"))

            def rows(at, src, n):
                act.dma_start(vst[at:at + n, :], src).then_inc(sem("vec_in"), 16)

            mu = t["rw_mu"][0]
            rows(V_MU, mu[0:13 * P].rearrange("(r p) -> r p", p=P), 13)
            act.dma_start(vst[V_MU + 13:V_MU + 14, 0:GD], mu[13 * P:13 * P + GD].rearrange(
                "(r p) -> r p", p=GD)).then_inc(sem("vec_in"), 16)
            rows(V_W0, t["rw_w0"][0].rearrange("d (r p) -> (d r) p", p=P), 8)
            rows(V_A0, t["rw_a0"][0].rearrange("d (r p) -> (d r) p", p=P), 8)
            rows(V_KK, t["rw_k_k"][0].rearrange("(r p) -> r p", p=P), 4)
            rows(V_KA, t["rw_k_a"][0].rearrange("(r p) -> r p", p=P), 4)
            rows(V_RK, t["rw_r_k"][0].rearrange("h e -> (h e)").rearrange("(r p) -> r p", p=P), 4)
            rows(V_QN, t["mla_q_norm"][0].rearrange("(r p) -> r p", p=P), 4)
            rows(V_KVN, t["mla_kv_norm"][0].rearrange("(r p) -> r p", p=P), 2)
            rows(V_MODB, t["mod_b"][0, 0:4096].rearrange("(r p) -> r p", p=P), 32)
            act.wait_ge(sem("c_in"), 32)
            nc.scalar.activation(csig[0:32, :], crow[0:32, :], ACT.Sigmoid).then_inc(step("c_sig")[0], 1)
            for k in range(KT):
                act.wait_ge(sem("xt_raw"), k + 1)
                nc.scalar.activation(xT[:, k, :], bank[2 + k % 4][:, :], ACT.Copy).then_inc(sem("xt_out"), 1)
            for b in range(8):
                act.wait_ge(sem("mod_used"), KT)
                nc.scalar.activation(mrow[:, b, :], bank[b][0:2, :], ACT.Copy).then_inc(sem("mod_row"), 1)
            act.wait_ge(*step("pads"))
            for n, (g, stationary, j, w, (t0, t1), dst) in enumerate(tiles):
                act.wait_ge(sem("proj"), n + 1)
                rows_ = w if stationary else P
                width = t1 - t0 if stationary else 256
                src = bank[n % 8][0:rows_, 0:width]
                if len(dst.shape) == 3:
                    src = src.rearrange("p (a b) -> p a b", a=2)
                nc.scalar.activation(dst, src, ACT.Copy).then_inc(sem("proj_out"), 1)
            for q in range(16):
                act.wait_ge(sem("rows"), q + 1)
                nc.scalar.activation(acc.rearrange("p a b -> p (a b)")[:, BANK * q:BANK * (q + 1)], bank[q % 2][:, :],
                                     ACT.Copy).then_inc(sem("rows_out"), 1)

            act.wait_ge(sem("rms_sum"), 1)
            A(nc.scalar.activation(rsq, bank[0][:, 0:LAT], ACT.Sqrt, bias=eps[:, 0:1], scale=1.0 / B_QR), "rms_root")
            act.wait_ge(sem("rms_sum"), 2)
            A(nc.scalar.activation(rsk, bank[1][:, :], ACT.Sqrt, bias=eps[:, 0:1], scale=1.0 / B_KVR), "rms_root")
            for p in range(4):
                act.wait_ge(sem("qr_mm"), p + 1)
                nc.scalar.activation(qr[:, p, :], bank[4 + p % 2][:, 0:LAT], ACT.Copy).then_inc(sem("qr_raw"), 1)
            for h in range(B_HEADS):
                act.wait_ge(sem("qn_mm"), h + 1)
                nc.scalar.activation(qn[:, h, :], bank[h % 4][:, 0:LAT], ACT.Copy).then_inc(sem("qn_out"), 1)
            for h in range(B_HEADS):
                act.wait_ge(sem("kn_mm"), h + 1)
                nc.scalar.activation(kn[:, h, :], bank[h % 4][:, :], ACT.Copy).then_inc(sem("kn_out"), 1)
            for n in range(2 * TT):
                act.wait_ge(sem("v_mm"), n + 1)
                nc.scalar.activation(vB[:, n // 2, BANK * (n % 2):BANK * (n % 2 + 1)], bank[4 + n % 4][:, :],
                                     ACT.Copy).then_inc(sem("v_out"), 1)
            for u in range(2 * B_HEADS + 2):
                if u < 2 * B_HEADS:
                    act.wait_ge(sem("row_max"), u + 1)
                    if u >= 2:
                        act.wait_ge(sem("prob_t"), u - 1)
                    A(nc.scalar.activation(prob[u % 2], bank[u % 2][:, :], ACT.Exp, bias=mx[:, u:u + 1],
                                           scale=(B_NOPE + B_ROPE) ** -0.5, accum_out=den[:, u:u + 1]), "exps")
                if 1 <= u <= 2 * B_HEADS:
                    w = u - 1
                    act.wait_ge(sem("prob_t"), w + 1)
                    if w >= 2:
                        act.wait_ge(sem("att_o"), w - 1)
                    nc.scalar.activation(probT[w % 2].rearrange("p a b -> p (a b)"), bank[2 + w % 2][:, :],
                                         ACT.Copy).then_inc(sem("prob_t_out"), 1)
                if u >= 2:
                    w = u - 2
                    act.wait_ge(sem("att_o"), w + 1)
                    nc.scalar.activation(oB[:, w // 2, (w % 2) * P:(w % 2 + 1) * P], bank[4 + w % 2][:, 0:P],
                                         ACT.Copy).then_inc(sem("att_out"), 1)
            for h in range(C_HEADS):
                act.wait_ge(sem("ret_o"), h + 1)
                nc.scalar.activation(oC[:, :, h * P:(h + 1) * P], split(bank[4 + h % 2][:, 0:2 * P], 2, P),
                                     ACT.Copy).then_inc(sem("ret_out"), 1)
            act.wait_ge(sem("variance"), 1)
            st = split(stat[:, 0:24], 3, 8)
            nc.scalar.activation(st[:, 2, :], st[:, 1, :], ACT.Sqrt, bias=eps[:, 0:1], scale=1.0 / C_VD).then_inc(
                sem("norm_root"), 1)
            nc.scalar.activation(nt, gt, ACT.Sigmoid).then_inc(step("ret_gate")[0], 1)
            for q in range(LT):
                act.wait_ge(sem("ret_t"), q + 1)
                nc.scalar.activation(oCT[:, :, q * P:(q + 1) * P], split(bank[5 + q][:, :], 4, P), ACT.Copy).then_inc(
                    sem("ret_t_out"), 1)
            act.wait_ge(*step("wad_shift"))
            nc.scalar.activation(wadt[sel_lo], wadt[sel_lo], ACT.Tanh).then_inc(step("wad_tanh")[0], 1)
            act.wait_ge(*step("gd_shift"))
            nc.scalar.activation(gsig[0:GD, :], gsig[0:GD, :], ACT.Sigmoid).then_inc(step("gd_sig")[0], 1)
            for n in range(16):
                i, c = n // 4, n % 4
                act.wait_ge(sem("lora"), n + 1)
                bias = (V_W0 if i < 2 else V_A0) + 4 * (i % 2) + c
                dst = (sigw if i < 2 else siga)[i % 2][:, :, c, :]
                nc.scalar.activation(dst, split(bank[n % 4][:, :], 4, P), ACT.Sigmoid,
                                     bias=vec[:, bias:bias + 1]).then_inc(sem("lora_out"), 1)
            for tt in range(TT):
                act.wait_ge(sem("v_t"), tt + 1)
                nc.scalar.activation(vtok[:, tt, :], bank[4 + tt][:, :], ACT.Copy).then_inc(sem("v_t_out"), 1)
            for tt in range(TT):
                act.wait_ge(sem("kk_sum"), tt + 1)
                nc.scalar.activation(sqa[:, tt, :], bank[tt][:, :], ACT.Sqrt, bias=eps[:, 2:3]).then_inc(
                    sem("kk_root"), 1)

            def decays(b):
                d = batches[b][0]
                e_in, e_ex, e_end, e_inv = (cum[0], cum[1], cum[2], cum[3]) if d == 0 else (cum[3], cum[2], cum[1],
                                                                                            cum[0])
                act.wait_ge(sem("rw_cum"), b + 1)
                total = cum[0].rearrange("p a (c e) -> p (a c) e", e=CH)[:, :, CH - 1]
                A(nc.scalar.activation(pc[b % 2], total, ACT.Exp, scale=-DECAY), "rw_exp")
                A(nc.scalar.activation(e_ex, e_ex, ACT.Exp, scale=-DECAY), "rw_exp")
                A(nc.scalar.activation(e_inv, e_in, ACT.Exp, scale=DECAY), "rw_exp")
                A(nc.scalar.activation(e_in, e_in, ACT.Exp, scale=-DECAY), "rw_exp")
                A(nc.scalar.activation(e_end, e_end, ACT.Exp, scale=-DECAY), "rw_exp")

            def token_major(b):
                for n in items_of(b):
                    if items[n][2] == "scalar":
                        dst = {"a": atok, "b": btok, "k": ktok}[items[n][1]][b % 2]
                        act.wait_ge(sem("rw_item"), n + 1)
                        nc.scalar.activation(dst, split(bank[n % 2][:, :], 4, P), ACT.Copy).then_inc(
                            sem("rw_item_scalar"), 1)

            decays(0)
            token_major(0)
            for b, (d, tt) in enumerate(batches):
                if b + 1 < len(batches):
                    decays(b + 1)
                for hf in range(2):
                    act.wait_ge(sem("rw_w1_mm"), 2 * b + hf + 1)
                    nc.scalar.activation(w1mv[:, hf], bank[6 + hf][:, :], ACT.Copy).then_inc(sem("rw_mv"), 1)
                if b + 1 < len(batches):
                    token_major(b + 1)
                for i, c in enumerate((0, 1) if d == 0 else (1, 0)):
                    rows = slice(CH * c, CH * c + CH)
                    for hf in range(2):
                        act.wait_ge(sem("rw_u_mm"), 4 * b + 2 * i + hf + 1)
                        nc.scalar.activation(w2[rows, hf], bank[4 + hf][rows, 0:2 * P], ACT.Copy).then_inc(
                            sem("rw_u"), 1)

            def root(n, width, groups_, which):
                act.wait_ge(sem("variance"), n)
                st = split(stat[:, 0:3 * groups_], 3, groups_)
                nc.scalar.activation(st[:, 2, :], st[:, 1, :], ACT.Sqrt, bias=eps[:, which:which + 1],
                                     scale=1.0 / width).then_inc(sem("norm_root"), 1)

            root(2, A_HD, 16, 1)
            for q in range(LT):
                act.wait_ge(sem("a_t"), q + 1)
                nc.scalar.activation(oAT[:, :, q * P:(q + 1) * P], split(bank[6 + q][:, :], 4, P), ACT.Copy).then_inc(
                    sem("a_t_out"), 1)
            root(3, D, LT, 0)
            for n in range(8):
                act.wait_ge(sem("u_t"), n + 1)
                nc.scalar.activation(uT[:, 2 * n:2 * n + 2, :], split(bank[n % 4][:, :], 2, LAT), ACT.Copy).then_inc(
                    sem("u_t_out"), 1)
            act.wait_ge(*step("logits"))
            A(nc.scalar.activation(lgT[0:N_EXPERTS, :], bank[4][0:N_EXPERTS, 0:LAT], ACT.Copy), "logits_out")
            act.wait_ge(*step("logits_t"))
            nc.scalar.activation(rt(1), split(bank[5][:, 0:32], 2, N_EXPERTS), ACT.Sigmoid).then_inc(step("scored")[0], 1)

            for k in range(KT):
                act.wait_ge(sem("xg_mm"), k + 1)
                nc.scalar.activation(xg[:, k, 0:PAIRS], bank[k % 4][:, :], ACT.Copy).then_inc(sem("xg_out"), 1)
            for s in range(2):
                act.wait_ge(sem("hot_t"), s + 1)
                nc.scalar.activation(hotT[:, 2 * s:2 * s + 2, :], split(bank[6 + s][:, :], 2, LAT), ACT.Copy).then_inc(
                    sem("hot_t_out"), 1)
            act.wait_ge(*step("onehot"))

            def expert(n, first):
                start = act.value_load(starts[0:1, bass.ds(n, 1)], min_val=0, max_val=PAIRS)
                for half in range(2):
                    act.wait_ge(sem("h_mm"), n * 2 + half + 1)
                    nc.scalar.activation(hs[:, half], split(bank[2 * half][:, 0:2 * P], 2, P), ACT.Sigmoid).then_inc(
                        sem("silu"), 1)
                if not first:
                    act.wait_ge(sem("y_out"), n * 8)
                for m in range(8):
                    act.wait_ge(sem("y_mm"), n * 8 + m + 1)
                    nc.scalar.activation(ys[:, 2 * m:2 * m + 2, bass.ds(start, P)],
                                         split(bank[4 + m % 4][:, 0:2 * P], 2, P), ACT.Copy).then_inc(sem("y_out"), 1)

            expert(0, True)
            with act.Fori(1, N_EXPERTS) as e:
                expert(e, False)
            with act.If(act.value_load(starts[0:1, 2 * N_EXPERTS:2 * N_EXPERTS + 1]) > P):
                with act.Fori(N_EXPERTS, 2 * N_EXPERTS) as n:
                    expert(n, False)
            for c in range(4):
                for s in range(ST):
                    act.wait_ge(sem("yt_t"), ST * c + s + 1)
                    nc.scalar.activation(yt[:, s, BANK * c:BANK * (c + 1)], bank[s][:, :], ACT.Copy).then_inc(
                        sem("yt_out"), 1)
            root(4, D, LT, 0)
        @block.vector
        def _(dve):
            V = Counter(dve, "dve_chain")
            nc.vector.memset(vst[:, :], 0.0).then_inc(step("vst_zero")[0], 1)
            V(nc.vector.memset(acc[:, :, :], 0.0), "acc_zero")
            dve.wait_ge(*step("c_sig"))
            nc.vector.tensor_tensor(crow[0:32, :], crow[0:32, :], csig[0:32, :], ALU.mult).then_inc(step("c_silu")[0], 1)
            dve.wait_ge(sem("small_t"), 1)
            V(nc.vector.tensor_copy(cT[:, :, :], bank[0][:, 0:32].rearrange("p (j k) -> p k j", j=2)), "cond")
            dve.wait_ge(sem("small_t"), 2)
            V(nc.vector.tensor_copy(vec[:, :], bank[1][:, 0:N_VEC]), "vecs")
            dve.wait_ge(*step("mod"))
            V(nc.vector.tensor_tensor(modT[:, :, :], split(bank[0][:, 0:64], 32, 2),
                                      vec[:, V_MODB:V_MODB + 32].unsqueeze(2).to_broadcast([P, 32, 2]), ALU.add))
            V(nc.vector.tensor_scalar(modT[:, 16:32, :], modT[:, 16:32, :], 1.0, None, ALU.add))
            for k in range(KT):
                dve.wait_ge(sem("xt_out"), k + 1)
                for j, half in enumerate((slice(CTX, TOK), slice(0, CTX))):
                    last = nc.vector.tensor_scalar(xT[:, k, half], xT[:, k, half], modT[:, 16 + k, j:j + 1],
                                                   modT[:, k, j:j + 1], ALU.mult, ALU.add)
                last.then_inc(sem("xt_mod"), 1)
            dve.wait_ge(sem("accb_in"), 16)

            def gate_rows(k, first):
                for q in range(8):
                    s = q % 4
                    row = acc.rearrange("p a b -> p (a b)")[:, 1024 * q:1024 * (q + 1)]
                    dve.wait_ge(sem(f"gate_in{s}"), k * 32 + 16 * (q // 4 + 1))
                    if not first:
                        dve.wait_ge(sem(f"gate_used{s}"), k * 2 + (q // 4 - 1))
                    nc.vector.scalar_tensor_tensor(row, gring[s], cT[:, k, 0:1] if first else cT[:, bass.ds(k, 1), 0:1].rearrange("p a b -> p (a b)"), row, ALU.mult,
                                                   ALU.add).then_inc(sem(f"gate_used{s}"), 1)

            gate_rows(0, True)
            with dve.Fori(1, KT) as k:
                gate_rows(k, False)

            dve.wait_ge(sem("proj_out"), len(tiles))
            for s in range(4):
                dve.wait_ge(sem(f"gate_used{s}"), 2 * KT)
            nc.vector.tensor_tensor(sqq, cq, cq, ALU.mult)
            V(nc.vector.tensor_tensor(sqk, ckv, ckv, ALU.mult), "rms_sq")
            dve.wait_ge(sem("rms_root"), 1)
            V(nc.vector.reciprocal(rsq, rsq))
            V(nc.vector.tensor_tensor(cq, cq, bc(rsq, 4, 1), ALU.mult))
            for c in range(4):
                ins = nc.vector.tensor_scalar(cq[:, c, :], cq[:, c, :], vec[:, V_QN + c:V_QN + c + 1], None, ALU.mult)
            V(ins, "cq_norm")
            dve.wait_ge(sem("rms_root"), 2)
            V(nc.vector.reciprocal(rsk, rsk))
            V(nc.vector.tensor_tensor(ckv, ckv, bc(rsk, 2, 1), ALU.mult))
            for c in range(2):
                ins = nc.vector.tensor_scalar(ckv[:, c, :], ckv[:, c, :], vec[:, V_KVN + c:V_KVN + c + 1], None,
                                              ALU.mult)
            V(ins, "ckv_norm")
            dve.wait_ge(*step("kr_rot"))
            V(nc.vector.tensor_tensor(rtmpk, bank[2][:, 0:LAT], sinT, ALU.mult))
            V(nc.vector.tensor_tensor(kr[:, CTX:TOK], kr[:, CTX:TOK], cosT, ALU.mult))
            V(nc.vector.tensor_tensor(kr[:, CTX:TOK], kr[:, CTX:TOK], rtmpk, ALU.add), "kr_ready")
            dve.wait_ge(*step("qrz_zero"))
            for p in range(4):
                dve.wait_ge(sem("q_rot"), p + 1)
                V(nc.vector.tensor_tensor(rtmpk, bank[6 + p % 2][:, 0:LAT], sinT, ALU.mult), "q_rot_read")
                V(nc.vector.tensor_tensor(qr[:, p, :], qr[:, p, :], cosT, ALU.mult))
                nc.vector.tensor_tensor(qrz[sel_lo, 2 * p, :], qr[sel_lo, p, :], rtmpk[sel_lo, :], ALU.add)
                V(nc.vector.tensor_tensor(qrz[sel_hi, 2 * p + 1, :], qr[sel_hi, p, :], rtmpk[sel_hi, :], ALU.add),
                  "qr_ready")
            for u in range(2 * B_HEADS + 1):
                if u < 2 * B_HEADS:
                    dve.wait_ge(sem("scores"), u + 1)
                    V(nc.vector.tensor_reduce(mx[:, u:u + 1], bank[u % 2][:, :], AX.X, ALU.max))
                    V(nc.vector.tensor_scalar(mx[:, u:u + 1], mx[:, u:u + 1], -((B_NOPE + B_ROPE) ** -0.5), None,
                                              ALU.mult), "row_max")
                if u >= 1:
                    w = u - 1
                    dve.wait_ge(sem("exps"), w + 1)
                    V(nc.vector.reciprocal(rden[:, w:w + 1], den[:, w:w + 1]))
                    V(nc.vector.tensor_scalar(prob[w % 2], prob[w % 2], rden[:, w:w + 1], None, ALU.mult), "probs")
            rtv = rtmp2.rearrange("p (a b) -> p a b", a=2)
            cos2, sin2 = bc(cosT, 2, 1), bc(sinT, 2, 1)
            dve.wait_ge(*step("rqz_zero"))
            dve.wait_ge(sem("ret_rot"), 1)
            V(nc.vector.tensor_tensor(rtv, split(bank[6][:, :], 2, LAT), sin2, ALU.mult))
            V(nc.vector.tensor_tensor(rq, rq, cos2, ALU.mult))
            nc.vector.tensor_tensor(rqz[sel_lo, 0:4:2, :], rq[sel_lo], rtv[sel_lo], ALU.add)
            V(nc.vector.tensor_tensor(rqz[sel_hi, 1:4:2, :], rq[sel_hi], rtv[sel_hi], ALU.add))
            dve.wait_ge(sem("ret_rot"), 2)
            V(nc.vector.tensor_tensor(rtv, split(bank[7][:, :], 2, LAT), sin2, ALU.mult))
            V(nc.vector.tensor_tensor(rk[:, :, CTX:TOK], rk[:, :, CTX:TOK], cos2, ALU.mult))
            V(nc.vector.tensor_tensor(rk[:, :, CTX:TOK], rk[:, :, CTX:TOK], rtv, ALU.add), "ret_qk")
            dve.wait_ge(sem("decay_in"), 16)
            for h in range(C_HEADS):
                if h >= 2:
                    dve.wait_ge(sem("ret_o"), h - 1)
                for j in range(2):
                    dve.wait_ge(sem("ret_s"), 2 * h + j + 1)
                    nc.vector.tensor_tensor(att[h % 2][:, 2 * j:2 * j + 2, :],
                                            split(bank[(2 * h + j) % 4][:, :], 2, LAT),
                                            dTall[:, h * TT + 2 * j:h * TT + 2 * j + 2, :], ALU.mult).then_inc(
                                                sem("ret_att"), 1)

            def norm(x, scratch, groups_, width, st, root_wait):
                V(nc.vector.tensor_reduce(st[:, 0, :], x, AX.X, ALU.add))
                V(nc.vector.tensor_scalar(st[:, 0, :], st[:, 0, :], -1.0 / width, None, ALU.mult))
                V(nc.vector.tensor_tensor(x, x, bc(st[:, 0, :], width, 2), ALU.add))
                V(nc.vector.tensor_tensor(scratch, x, x, ALU.mult))
                V(nc.vector.tensor_reduce(st[:, 1, :], scratch, AX.X, ALU.add), "variance")
                root_wait()
                V(nc.vector.reciprocal(st[:, 2, :], st[:, 2, :]))
                V(nc.vector.tensor_tensor(x, x, bc(st[:, 2, :], width, 2), ALU.mult))

            dve.wait_ge(sem("ret_out"), C_HEADS)
            norm(oC.rearrange("p a (h e) -> p (a h) e", e=C_VD), nt.rearrange("p a (h e) -> p (a h) e", e=C_VD), 8,
                 C_VD, split(stat[:, 0:24], 3, 8), lambda: dve.wait_ge(sem("norm_root"), 1))
            dve.wait_ge(sem("gnc_in"), 32)
            V(nc.vector.tensor_tensor(oC, oC, bc(gnc[:, 0, :], LT, 1), ALU.mult))
            V(nc.vector.tensor_tensor(oC, oC, bc(gnc[:, 1, :], LT, 1), ALU.add))
            dve.wait_ge(*step("ret_gate"))
            V(nc.vector.tensor_tensor(gt, gt, nt, ALU.mult))
            V(nc.vector.tensor_tensor(oC, oC, gt, ALU.mult), "ret_done")
            dve.wait_ge(sem("ret_t_out"), 2)
            dve.wait_ge(sem("ret_o"), C_HEADS)
            nc.vector.tensor_scalar(mu5, vec[:, V_MU:V_MU + 14], 0.5, None, ALU.mult)
            V(nc.vector.tensor_scalar(omu, vec[:, V_MU:V_MU + 14], -1.0, 1.0, ALU.mult, ALU.add))

            def shift(dst, padded, row, parts=P, signal=None):
                t4 = sqa[0:parts, 0, 0:math.prod(dst.shape[1:])].rearrange("p (a b c) -> p a b c", a=dst.shape[1], b=2)
                prev, cur, nxt = (padded[0:parts, :, i:i + LAT].rearrange("p s (u e) -> p s u e", u=2)
                                  for i in range(3))
                V(nc.vector.tensor_tensor(t4, prev, nxt, ALU.add))
                V(nc.vector.tensor_scalar(t4, t4, mu5[0:parts, row:row + 1], None, ALU.mult))
                V(nc.vector.scalar_tensor_tensor(dst, cur, omu[0:parts, row:row + 1], t4, ALU.mult, ALU.add), signal)

            def tiles4(x, c):
                return x[:, :, c, :].rearrange("p (s u) e -> p s u e", u=2)

            shift(wadt.rearrange("p s (u e) -> p s u e", u=2), wp, 12, signal="wad_shift")
            shift(split(gsig[0:GD, :], 1, LAT).rearrange("p s (u e) -> p s u e", u=2), split(gp[:, :], 1, LAT + 2), 13,
                  parts=GD, signal="gd_shift")
            for c in range(4):
                shift(tiles4(ks, c), kp[:, c], 4 + c)
            for c in range(4):
                shift(tiles4(vs, c), vp[:, c], 8 + c, signal="v_shift")
            for c in range(4):
                shift(tiles4(rs, c), split(rp[:, c, :], 1, LAT + 2), c)
            for c in range(4):
                nc.vector.tensor_scalar(kkn[:, :, c, :], ks[:, :, c, :], vec[:, V_KK + c:V_KK + c + 1], None, ALU.mult)
                last = nc.vector.tensor_scalar(rrk[:, :, c, :], rs[:, :, c, :], vec[:, V_RK + c:V_RK + c + 1], None,
                                               ALU.mult)
            V(last)
            flat = kkn.rearrange("p a b c -> p a (b c)")
            V(nc.vector.tensor_tensor(sqa, flat, flat, ALU.mult), "kk_sq")
            for tt in range(TT):
                dve.wait_ge(sem("kk_root"), tt + 1)
                V(nc.vector.reciprocal(sqa[:, tt, :], sqa[:, tt, :]))
                V(nc.vector.tensor_tensor(flat[:, tt, :], flat[:, tt, :], sqa[:, tt, :], ALU.mult))
            V(nc.vector.tensor_scalar(nka, vec[:, V_KA:V_KA + 4], -1.0, 1.0, ALU.mult, ALU.add), "rw_prep")
            ka = vec[:, V_KA:V_KA + 4]
            dve.wait_ge(*step("rw_zero"))

            def halves(dst, x, y):
                nc.vector.tensor_tensor(dst[sel_lo, 0:8:2, :], x[sel_lo], y[sel_lo], ALU.mult)
                V(nc.vector.tensor_tensor(dst[sel_hi, 1:8:2, :], x[sel_hi], y[sel_hi], ALU.mult))


            def features(b, part):
                d, tt = batches[b]
                q = tt - 2
                sig = sigw[d][:, tt]
                e_in, e_ex, e_end, e_inv = (cum[0], cum[1], cum[2], cum[3]) if d == 0 else (cum[3], cum[2], cum[1],
                                                                                            cum[0])
                if part == 0:
                    V(nc.vector.tensor_tensor_scan(cum[0].rearrange("p a b -> p (a b)"), reset,
                                                   sig.rearrange("p a b -> p (a b)"), 0.0, ALU.mult, ALU.add))
                    total = cum[0].rearrange("p a (c e) -> p (a c) e", e=CH)[:, :, CH - 1:CH].to_broadcast([P, 8, CH])
                    nc.vector.tensor_tensor(cum[1], cum[0], sig, ALU.subtract)
                    c0v, c2v = (x.rearrange("p a (c e) -> p (a c) e", e=CH) for x in (cum[0], cum[2]))
                    ins = nc.vector.tensor_tensor(c2v, total, c0v, ALU.subtract)
                    if d == 1:
                        V(ins)
                        ins = nc.vector.tensor_tensor(cum[3], cum[2], sig, ALU.add)
                    V(ins, "rw_cum")
                elif part == 1:
                    nc.vector.tensor_tensor(bb, kkn[:, tt], siga[d][:, tt], ALU.mult)
                    V(nc.vector.tensor_tensor(kd, siga[d][:, tt], bc(ka, P, 2), ALU.mult))
                elif part == 2:
                    V(nc.vector.tensor_tensor(kd, kd, bc(nka, P, 2), ALU.add))
                    V(nc.vector.tensor_tensor(kd, kd, ks[:, tt], ALU.mult))
                elif part == 3:
                    dve.wait_ge(sem("rw_exp"), 5 * (b + 1))
                    V(nc.vector.scalar_tensor_tensor(arp[:, :, 0, :], kkn[:, tt], -1.0, e_ex, ALU.mult, ALU.mult))
                    halves(bz, bb, e_inv)
                    halves(kz, kd, e_inv)
                else:
                    if tt >= 2:
                        nc.vector.tensor_tensor(cum[1 + d], rrk[:, q], kd, ALU.mult)
                        V(nc.vector.tensor_tensor(arp[:, :, 1, :], rs[:, q], e_in, ALU.mult))
                        nc.vector.tensor_copy(rr[b % 2], arp[:, :, 1, :])
                    nc.vector.tensor_tensor(bb, bb, e_end, ALU.mult)
                    V(nc.vector.tensor_tensor(kd, kd, e_end, ALU.mult), "rw_feat")

            def item(n):
                b, kind, engine, _ = items[n]
                if engine != "vector":
                    return
                d, tt = batches[b]
                dve.wait_ge(sem("rw_item"), n + 1)
                ps = split(bank[n % 2][:, :], 4, P)
                if kind == "bonus":
                    bo = bonus[:, 8 * (tt - 2):8 * (tt - 1)]
                    if d == 0:
                        ins = nc.vector.tensor_copy(bo, bank[n % 2][:, 0:8])
                    else:
                        ins = nc.vector.tensor_tensor(bo, bo, bank[n % 2][:, 0:8], ALU.add)
                elif kind in ("low0", "low1"):
                    hf = int(kind[3])
                    lo_m, up_m = (lower, upper) if d == 0 else (upper, lower)
                    dve.wait_ge(sem("rw_ident"), 4 * b + 3 + hf)

                    def pairs(x, which):
                        return x.rearrange("p (g two) -> p g two", two=2)[:, :, which]

                    x_, g_ = blocks(xm[:, hf], 1, d), blocks(gm[:, hf], 1, 1 - d)
                    x_, g_ = (v.rearrange("p j g n -> p j (g n)") for v in (x_, g_))
                    l_ = ps.rearrange("p j (g two) -> p j g two", two=2)[:, :, :, d]
                    lt_ = um[b % 2][:, hf, :, 0].rearrange("p j (g two) -> p j g two", two=2)[:, :, :, 1 - d]
                    nc.vector.tensor_tensor(x_, l_, bc(pairs(lo_m[:, 0], d), 4, 1), ALU.mult)
                    V(nc.vector.tensor_tensor(g_, lt_, bc(pairs(up_m[:, 0], 1 - d), 4, 1), ALU.mult))
                    V(nc.vector.tensor_tensor(x_, x_, bc(pairs(ident, d), 4, 1), ALU.add))
                    ins = nc.vector.tensor_tensor(g_, g_, bc(pairs(ident, 1 - d), 4, 1), ALU.add)
                elif tt >= 2:
                    ins = nc.vector.tensor_tensor(um[b % 2][:, kind // 4, kind % 4], ps, masks[d], ALU.mult)
                else:
                    ins = nc.vector.tensor_tensor(um[b % 2][:, kind // 4, kind % 4, 0:4:2], ps[:, 0:4:2],
                                                  masks[d][:, 0:4:2], ALU.mult)
                V(ins, "rw_item_vector")

            for part in range(5):
                features(0, part)
            for n in items_of(0):
                item(n)
            nlat = 0
            for b, (d, tt) in enumerate(batches):
                latent = tt >= 2
                q = tt - 2
                lo_m = lower if d == 0 else upper
                for lv in range(LEVELS):
                    n = 2 * (LEVELS * b + lv)
                    for hf in range(2):
                        dve.wait_ge(sem("rw_lx"), n + hf + 1)
                        V(nc.vector.tensor_tensor(zm[:, hf], split(bank[4 + hf][:, :], 4, P),
                                                  bc(lo_m[:, lv + 1], 4, 1), ALU.mult), "rw_z")
                    if b + 1 < len(batches):
                        features(b + 1, lv)
                    for hf in range(2):
                        n_x, nx = 2 << lv, 2 * ((LEVELS - 1) * b + lv)
                        if lv < LEVELS - 1:
                            dve.wait_ge(sem("rw_xz"), nx + hf + 1)
                            x_ = blocks(xm[:, hf], n_x, d)
                            V(nc.vector.tensor_tensor(x_, x_, blocks(split(bank[hf][:, :], 4, P), n_x, d), ALU.add),
                              "rw_x")
                        dve.wait_ge(sem("rw_gz"), n + hf + 1)
                        g_ = blocks(gm[:, hf], n_x, 1 - d)
                        V(nc.vector.tensor_tensor(g_, g_, blocks(split(bank[2 + hf][:, :], 4, P), n_x, 1 - d), ALU.add),
                          "rw_g")

                def next_items(part):
                    if b + 1 < len(batches):
                        for n in items_of(b + 1, part):
                            item(n)

                next_items(0)
                next_items(1)
                pv = pc[b % 2].rearrange("p (a c) -> p a c", c=2)
                for i, c in enumerate((0, 1) if d == 0 else (1, 0)):
                    for hf in range(2):
                        V(nc.vector.tensor_tensor(stmp[:, hf], sst[i][:, 2 * hf:2 * hf + 2],
                                                  bc(pv[:, 2 * hf:2 * hf + 2, c], P, 2), ALU.mult))
                    next_items(2 + 2 * i)
                    for hf in range(2):
                        dve.wait_ge(sem("rw_s_mm"), 4 * b + 2 * i + hf + 1)
                        new, ps = sst[1 - i][:, 2 * hf:2 * hf + 2], split(bank[2 + hf][:, 0:2 * P], 2, P)
                        nc.vector.tensor_tensor(new[sel_lo, :, 0:64], ps[sel_lo, :, 0:64], stmp[sel_lo, hf, :, 0:64],
                                                ALU.add)
                        V(nc.vector.tensor_tensor(new[sel_hi, :, 64:P], ps[sel_hi, :, 64:P],
                                                  stmp[sel_hi, hf, :, 64:P], ALU.add), "rw_s")
                    if i == 0:
                        next_items(3)
                if latent:
                    for hf in range(2):
                        dve.wait_ge(sem("rw_y_mm"), 2 * nlat + hf + 1)
                        ya = yacc[:, q, 2 * P * hf:2 * P * (hf + 1)]
                        if d == 0:
                            V(nc.vector.tensor_copy(ya, bank[6 + hf][:, 0:2 * P]), "rw_y")
                        else:
                            V(nc.vector.tensor_tensor(ya, ya, bank[6 + hf][:, 0:2 * P], ALU.add), "rw_y")
                    nlat += 1
                if b == 3:
                    V(nc.vector.memset(sst[0], 0.0), "rw_s_reset")
                next_items(5)
            norm(yacc.rearrange("p a (h e) -> p (a h) e", e=A_HD), na.rearrange("p a (h e) -> p (a h) e", e=A_HD), 16,
                 A_HD, split(stat[:, 0:48], 3, 16), lambda: dve.wait_ge(sem("norm_root"), 2))
            dve.wait_ge(sem("gna_in"), 32)
            V(nc.vector.tensor_tensor(yacc, yacc, bc(gna[:, 0, :], LT, 1), ALU.mult))
            V(nc.vector.tensor_tensor(yacc, yacc, bc(gna[:, 1, :], LT, 1), ALU.add))
            for q in range(LT):
                V(nc.vector.tensor_tensor(split(na[:, q, :], 8, A_HD), split(vtok[:, 2 + q, :], 8, A_HD),
                                          bc(bonus[:, 8 * q:8 * q + 8], A_HD, 2), ALU.mult))
            V(nc.vector.tensor_tensor(yacc, yacc, na, ALU.add))
            dve.wait_ge(sem("g_mm"), 2)
            for q in range(LT):
                V(nc.vector.tensor_tensor(yacc[:, q, :], yacc[:, q, :], bank[q][:, :], ALU.mult), "a_done")
            dve.wait_ge(sem("rows_in"), 16)
            dve.wait_ge(sem("xl_in"), 16)
            for n in range(8):
                tt, c = n // 4, slice(BANK * (n % 4), BANK * (n % 4 + 1))
                dve.wait_ge(sem("wo_used"), KT)
                V(nc.vector.tensor_tensor(ub[:, tt, c], bank[n][:, :], g1r[:, c], ALU.mult), "mix_out")
                V(nc.vector.scalar_tensor_tensor(x1[:, tt, c], x1[:, tt, c], ALPHA, ub[:, tt, c], ALU.mult, ALU.add))
            norm(x1, ub, LT, D, split(stat[:, 0:6], 3, 2), lambda: dve.wait_ge(sem("norm_root"), 3))
            dve.wait_ge(sem("ln_in"), 32)
            V(nc.vector.tensor_tensor(x1, x1, bc(ln[:, 0, :], LT, 1), ALU.mult))
            V(nc.vector.tensor_tensor(x1, x1, bc(ln[:, 1, :], LT, 1), ALU.add))
            V(nc.vector.tensor_scalar(sc2r, sc2r, 1.0, None, ALU.add))
            V(nc.vector.tensor_tensor(ub, x1, bc(sc2r, LT, 1), ALU.mult))
            V(nc.vector.tensor_tensor(ub, ub, bc(sh2r, LT, 1), ALU.add), "u_ready")
            s_, sb, t1, t2 = rt(1), rt(2), rt(3), rt(4)
            oh1, oh2 = rt(5), rt(6)
            iota16 = bc(const("iota16"), 2, 1)
            iota4 = bc(const("iota4"), 2, 1)
            dve.wait_ge(*step("scored"))
            dve.wait_ge(sem("router_in"), 32)
            V(nc.vector.tensor_tensor(sb, s_, bc(rbias, 2, 1), ALU.add))
            v4 = sb.rearrange("p t (g e) -> p t g e", e=4)
            m_a, n_a, m_b, n_b, gs, ge = (rg(i) for i in range(6))
            nc.vector.tensor_tensor(m_a, v4[:, :, :, 0], v4[:, :, :, 1], ALU.max)
            nc.vector.tensor_tensor(n_a, v4[:, :, :, 0], v4[:, :, :, 1], ALU.min)
            nc.vector.tensor_tensor(m_b, v4[:, :, :, 2], v4[:, :, :, 3], ALU.max)
            V(nc.vector.tensor_tensor(n_b, v4[:, :, :, 2], v4[:, :, :, 3], ALU.min))
            V(nc.vector.tensor_tensor(n_a, n_a, n_b, ALU.max))
            V(nc.vector.tensor_tensor(n_b, m_a, m_b, ALU.min))
            V(nc.vector.tensor_tensor(n_a, n_a, n_b, ALU.max))
            V(nc.vector.tensor_tensor(m_a, m_a, m_b, ALU.max))
            V(nc.vector.tensor_tensor(gs, m_a, n_a, ALU.add))
            one = small[:, 16:48]

            def first_best(x, hot, iota, width, tmp_):
                best, at_ = one[:, 0:2], one[:, 2:4]
                V(nc.vector.tensor_reduce(best, x, AX.X, ALU.max))
                V(nc.vector.tensor_tensor(hot, x, bc(best, width, 2), ALU.is_lt))
                V(nc.vector.tensor_scalar(hot, hot, 100.0, None, ALU.mult))
                V(nc.vector.tensor_tensor(tmp_, hot, iota, ALU.add))
                V(nc.vector.tensor_reduce(at_, tmp_, AX.X, ALU.min))
                V(nc.vector.tensor_tensor(hot, iota, bc(at_, width, 2), ALU.is_equal))

            first_best(gs, ge, iota4, 4, m_b)
            V(nc.vector.tensor_scalar(n_b, ge, 1e30, -1e30, ALU.mult, ALU.add))
            for tt in range(2):
                V(nc.vector.tensor_tensor(split(t1[:, tt], 4, 4), v4[:, tt], bc(ge[:, tt], 4, 2), ALU.mult))
                V(nc.vector.tensor_tensor(split(t1[:, tt], 4, 4), split(t1[:, tt], 4, 4), bc(n_b[:, tt], 4, 2),
                                          ALU.add))
            first_best(t1, oh1, iota16, 16, t2)
            V(nc.vector.tensor_scalar(t2, oh1, -1e30, None, ALU.mult))
            V(nc.vector.tensor_tensor(t1, t1, t2, ALU.add))
            first_best(t1, oh2, iota16, 16, t2)
            V(nc.vector.tensor_tensor(t1, oh1, oh2, ALU.add), "selected")
            for i, oh in enumerate((oh1, oh2)):
                V(nc.vector.tensor_tensor(t2, oh, s_, ALU.mult))
                V(nc.vector.tensor_reduce(gate[i], t2, AX.X, ALU.add))
            V(nc.vector.tensor_tensor(one[:, 0:2], gate[0], gate[1], ALU.add))
            V(nc.vector.reciprocal(one[:, 0:2], one[:, 0:2]))
            for i in range(2):
                V(nc.vector.scalar_tensor_tensor(gate[i], gate[i], ROUTE_SCALE, one[:, 0:2], ALU.mult, ALU.mult))
            dve.wait_ge(*step("ranks"))
            nc.vector.tensor_copy(cnt, bank[6][:, 32:48])
            V(nc.vector.tensor_copy(excl, split(bank[6][:, 0:32], 2, N_EXPERTS)))
            V(nc.vector.tensor_tensor_scan(base, ones[:, 0:N_EXPERTS], cnt, 0.0, ALU.mult, ALU.add))
            V(nc.vector.tensor_tensor(off, base, cnt, ALU.subtract))
            V(nc.vector.tensor_tensor(excl, excl, bc(off, 2, 1), ALU.add))
            for i, oh in enumerate((oh1, oh2)):
                V(nc.vector.tensor_tensor(t2, oh, excl, ALU.mult))
                V(nc.vector.tensor_reduce(pair_at[i], t2, AX.X, ALU.add))
            V(nc.vector.tensor_scalar(late, cnt, float(P), None, ALU.is_gt))
            V(nc.vector.tensor_scalar(base, base, float(-P - PAIRS), None, ALU.add))
            V(nc.vector.tensor_tensor(late, late, base, ALU.mult))
            V(nc.vector.tensor_scalar(late, late, float(PAIRS), None, ALU.add))
            V(nc.vector.tensor_reduce(most, cnt, AX.X, ALU.max))
            nc.vector.tensor_copy(starts[:, 0:N_EXPERTS], off[0:1, :])
            nc.vector.tensor_copy(starts[:, N_EXPERTS:2 * N_EXPERTS], late[0:1, :])
            V(nc.vector.tensor_copy(starts[:, 2 * N_EXPERTS:], most[0:1, :]))
            for tt in range(LT):
                at_ = [pair_at[i][:, tt:tt + 1] for i in range(2)]
                V(nc.vector.tensor_scalar(hot[:, tt], iota, at_[0], None, ALU.is_equal))
                V(nc.vector.tensor_scalar(hotg[:, tt], hot[:, tt], gate[0][:, tt:tt + 1], None, ALU.mult))
                V(nc.vector.tensor_scalar(hot2, iota, at_[1], None, ALU.is_equal))
                V(nc.vector.scalar_tensor_tensor(hotg[:, tt], hot2, gate[1][:, tt:tt + 1], hotg[:, tt], ALU.mult,
                                                 ALU.add))
                V(nc.vector.tensor_tensor(hot[:, tt], hot[:, tt], hot2, ALU.add), "onehot" if tt else None)

            def expert(n):
                for half in range(2):
                    dve.wait_ge(sem("h_mm"), n * 2 + half + 1)
                    dve.wait_ge(sem("silu"), n * 2 + half + 1)
                    nc.vector.tensor_tensor(hs[:, half], hs[:, half], split(bank[2 * half][:, 0:2 * P], 2, P),
                                            ALU.mult).then_inc(sem("h_1"), 1)
                    dve.wait_ge(sem("h_1"), n * 2 + half + 1)
                    nc.vector.tensor_tensor(hT[:, 2 * half:2 * half + 2], hs[:, half],
                                            split(bank[2 * half + 1][:, 0:2 * P], 2, P), ALU.mult).then_inc(
                                                sem("h_out"), 1)

            dve.wait_ge(sem("hot_t"), 2)
            with dve.Fori(0, N_EXPERTS) as e:
                expert(e)
            with dve.If(dve.value_load(starts[0:1, 2 * N_EXPERTS:2 * N_EXPERTS + 1]) > P):
                with dve.Fori(N_EXPERTS, 2 * N_EXPERTS) as n:
                    expert(n)
            for c in range(4):
                cc = slice(BANK * c, BANK * (c + 1))
                for tt in range(LT):
                    dve.wait_ge(sem("ffn"), 2 * c + tt + 1)
                    dst = lnt[:, tt, cc]
                    V(nc.vector.tensor_tensor(dst, bank[4 + 2 * (c % 2) + tt][:, :], g2r[:, cc], ALU.mult), "ffn_out")
                    V(nc.vector.scalar_tensor_tensor(x1[:, tt, cc], x1[:, tt, cc], ALPHA, dst, ALU.mult, ALU.add))
            norm(x1, lnt, LT, D, split(stat[:, 0:6], 3, 2), lambda: dve.wait_ge(sem("norm_root"), 4))
            dve.wait_ge(sem("ln2_in"), 32)
            V(nc.vector.tensor_tensor(x1, x1, bc(ln2[:, 0, :], LT, 1), ALU.mult))
            for tt in range(LT):
                V(nc.vector.tensor_tensor(x1[:, tt], x1[:, tt], ln2[:, 1, :], ALU.add), "done")
        @block.tensor
        def _(pe):
            pe.wait_ge(sem("const_in"), 16)
            pe.wait_ge(*step("c_silu"))
            nc.tensor.transpose(bank[0][:, 0:32], crow[0:32, :], ident[0:32, 0:32]).then_inc(sem("small_t"), 1)
            pe.wait_ge(sem("vec_in"), 160)
            nc.tensor.transpose(bank[1][:, 0:N_VEC], vst[0:N_VEC, :], ident[0:N_VEC, 0:N_VEC]).then_inc(
                sem("small_t"), 1)
            for k in range(KT):
                if k >= 4:
                    pe.wait_ge(sem("xt_out"), k - 3)
                for tt in range(TT):
                    if k == 0:
                        pe.wait_ge(sem(f"x_in{tt}"), 16)
                    last = nc.tensor.transpose(bank[2 + k % 4][:, tt * P:(tt + 1) * P],
                                               xtok[:, tt, k * P:(k + 1) * P], ident)
                last.then_inc(sem("xt_raw"), 1)
            pe.wait_ge(*step("cond"))
            pe.wait_ge(*step("vecs"))
            pe.wait_ge(sem("xt_out"), KT)
            for k in range(KT):
                pe.wait_ge(sem(f"mod_in{k % 3}"), 16 * (k // 3 + 1))
                for b in range(8):
                    last = nc.tensor.matmul(bank[b][0:2, :], cT[:, k, :], mring[k % 3][:, b, :], start=(k == 0),
                                            stop=(k == KT - 1))
                last.then_inc(sem("mod_used"), 1)
            for b in range(8):
                pe.wait_ge(sem("mod_row"), b + 1)
            for c in range(32):
                last = nc.tensor.transpose(bank[0][:, 2 * c:2 * c + 2], mrow[:, c // 4, (c % 4) * P:(c % 4 + 1) * P],
                                           ident[0:2, 0:2])
            last.then_inc(step("mod")[0], 1)
            for n, (g, stationary, j, w, (t0, t1), dst) in enumerate(tiles):
                if n == 0 or g != tiles[n - 1][0]:
                    pe.wait_ge(sem(f"win_in{g % 3}"), 16 * (g // 3 + 1))
                    if groups[g][0] == COL_KR:
                        pe.wait_ge(sem("kr_in"), 16)
                if n < 8:
                    pe.wait_ge(sem("xt_mod"), KT)
                else:
                    pe.wait_ge(sem("proj_out"), n - 7)
                for k in range(KT):
                    if stationary:
                        last = nc.tensor.matmul(bank[n % 8][0:w, 0:t1 - t0], wring[g % 3][:, k, j:j + w],
                                                xT[:, k, t0:t1], start=(k == 0), stop=(k == KT - 1))
                    else:
                        last = nc.tensor.matmul(bank[n % 8][:, 0:256], xT[:, k, t0:t1], wring[g % 3][:, k, :],
                                                start=(k == 0), stop=(k == KT - 1))
                last.then_inc(sem("proj"), 1)
            for s in range(4):
                pe.wait_ge(sem(f"gate_used{s}"), 2 * KT)
            for q in range(16):
                pe.wait_ge(sem("proj_out"), len(tiles))
                if q >= 2:
                    pe.wait_ge(sem("rows_out"), q - 1)
                nc.tensor.matmul(bank[q % 2][:, :], ones, acc.rearrange("p a b -> p (a b)")[:, BANK * q:BANK * (q + 1)],
                                 start=True, stop=True).then_inc(sem("rows"), 1)
            pe.wait_ge(*step("rms_sq"))
            pe.wait_ge(sem("rows_out"), 16)
            for c in range(4):
                last = nc.tensor.matmul(bank[0][:, 0:LAT], ones, sqq[:, c, :], start=(c == 0), stop=(c == 3))
            last.then_inc(sem("rms_sum"), 1)
            for c in range(2):
                last = nc.tensor.matmul(bank[1][:, :], ones, sqk[:, c, :], start=(c == 0), stop=(c == 1))
            last.then_inc(sem("rms_sum"), 1)
            nc.tensor.matmul(bank[2][:, 0:LAT], rot, kr[:, CTX:TOK], start=True, stop=True).then_inc(step("kr_rot")[0], 1)
            pe.wait_ge(sem("uq_in"), 16)
            pe.wait_ge(*step("cq_norm"))
            wuq_h = wuq.rearrange("p k (h e) -> p k h e", e=B_NOPE + B_ROPE)
            for p in range(4):
                if p >= 2:
                    pe.wait_ge(sem("qr_raw"), p - 1)
                for c in range(4):
                    for o in range(2):
                        last = nc.tensor.matmul(bank[4 + p % 2][64 * o:64 * o + 64, 0:LAT],
                                                wuq_h[:, c, 2 * p + o, B_NOPE:], cq[:, c, :], start=(c == 0),
                                                stop=(c == 3), skip_group_check=True)
                last.then_inc(sem("qr_mm"), 1)
                if p >= 1:
                    w = p - 1
                    pe.wait_ge(sem("qr_raw"), w + 1)
                    if w >= 2:
                        pe.wait_ge(sem("q_rot_read"), w - 1)
                    nc.tensor.matmul(bank[6 + w % 2][:, 0:LAT], rot, qr[:, w, :], start=True, stop=True).then_inc(
                        sem("q_rot"), 1)
            pe.wait_ge(sem("qr_raw"), 4)
            pe.wait_ge(sem("q_rot_read"), 2)
            nc.tensor.matmul(bank[7][:, 0:LAT], rot, qr[:, 3, :], start=True, stop=True).then_inc(sem("q_rot"), 1)
            pe.wait_ge(sem("rms_root"), 2)
            pe.wait_ge(*step("kr_ready"))
            for h in range(B_HEADS):
                if h >= 4:
                    pe.wait_ge(sem("qn_out"), h - 3)
                for c in range(4):
                    last = nc.tensor.matmul(bank[h % 4][:, 0:LAT], wuq_h[:, c, h, 0:B_NOPE], cq[:, c, :],
                                            start=(c == 0), stop=(c == 3))
                last.then_inc(sem("qn_mm"), 1)
            pe.wait_ge(sem("ukv_in"), 16)
            pe.wait_ge(*step("ckv_norm"))
            wukv_h = wukv.rearrange("p k (h e) -> p k h e", e=B_NOPE + B_VD)
            for h in range(B_HEADS):
                pe.wait_ge(sem("qn_out"), min(8, h + 5))
                if h >= 4:
                    pe.wait_ge(sem("kn_out"), h - 3)
                for c in range(2):
                    last = nc.tensor.matmul(bank[h % 4][:, :], wukv_h[:, c, h, 0:B_NOPE], ckv[:, c, :],
                                            start=(c == 0), stop=(c == 1))
                last.then_inc(sem("kn_mm"), 1)
            pe.wait_ge(sem("qr_ready"), 4)
            for n in range(2 * TT):
                if n >= 4:
                    pe.wait_ge(sem("v_out"), n - 3)
                tt, half = n // 2, n % 2
                for c in range(2):
                    last = nc.tensor.matmul(bank[4 + n % 4][:, :], ckv[:, c, tt * P:(tt + 1) * P],
                                            wukv_h[:, c, 4 * half:4 * half + 4, B_NOPE:], start=(c == 0),
                                            stop=(c == 1))
                last.then_inc(sem("v_mm"), 1)
            pe.wait_ge(sem("kn_out"), B_HEADS)
            pe.wait_ge(sem("v_out"), 2 * TT)
            for u in range(2 * B_HEADS + 2):
                if u < 2 * B_HEADS:
                    h, q = u // 2, slice((u % 2) * P, (u % 2 + 1) * P)
                    if u >= 2:
                        pe.wait_ge(sem("exps"), u - 1)
                    nc.tensor.matmul(bank[u % 2][:, :], qn[:, h, q], kn[:, h, :], start=True, stop=False)
                    nc.tensor.matmul(bank[u % 2][:, :], qrz[:, h, q], kr, start=False, stop=True).then_inc(
                        sem("scores"), 1)
                if 1 <= u <= 2 * B_HEADS:
                    w = u - 1
                    pe.wait_ge(sem("probs"), w + 1)
                    if w >= 2:
                        pe.wait_ge(sem("prob_t_out"), w - 1)
                    for tt in range(TT):
                        last = nc.tensor.transpose(bank[2 + w % 2][:, tt * P:(tt + 1) * P],
                                                   prob[w % 2][:, tt * P:(tt + 1) * P], ident)
                    last.then_inc(sem("prob_t"), 1)
                if u >= 2:
                    w = u - 2
                    h = w // 2
                    pe.wait_ge(sem("prob_t_out"), w + 1)
                    if w >= 2:
                        pe.wait_ge(sem("att_out"), w - 1)
                    for tt in range(TT):
                        last = nc.tensor.matmul(bank[4 + w % 2][:, 0:P], vB[:, tt, h * P:(h + 1) * P],
                                                probT[w % 2][:, tt, :], start=(tt == 0), stop=(tt == TT - 1))
                    last.then_inc(sem("att_o"), 1)
            for c in range(2):
                last = nc.tensor.matmul(bank[6][:, c * LAT:(c + 1) * LAT], rot, rq[:, c, :], start=True, stop=True,
                                        skip_group_check=True)
            last.then_inc(sem("ret_rot"), 1)
            for c in range(2):
                last = nc.tensor.matmul(bank[7][:, c * LAT:(c + 1) * LAT], rot, rk[:, c, CTX:TOK], start=True,
                                        stop=True, skip_group_check=True)
            last.then_inc(sem("ret_rot"), 1)
            pe.wait_ge(*step("ret_qk"))
            pe.wait_ge(sem("prob_t_out"), 2 * B_HEADS)
            pe.wait_ge(sem("att_out"), 2 * B_HEADS)
            for h in range(C_HEADS + 1):
                if h < C_HEADS:
                    for j in range(2):
                        n = 2 * h + j
                        if n >= 4:
                            pe.wait_ge(sem("ret_att"), n - 3)
                        for kt in range(2 * j, 2 * j + 2):
                            last = nc.tensor.matmul(bank[n % 4][:, (kt % 2) * LAT:(kt % 2 + 1) * LAT],
                                                    rk[:, h // 2, kt * P:(kt + 1) * P], rqz[:, h, :], start=True,
                                                    stop=True, skip_group_check=True)
                        last.then_inc(sem("ret_s"), 1)
                if h >= 1:
                    w = h - 1
                    pe.wait_ge(sem("ret_att"), 2 * w + 2)
                    if w >= 2:
                        pe.wait_ge(sem("ret_out"), w - 1)
                    for q in range(LT):
                        for kt in range(TT):
                            last = nc.tensor.matmul(bank[4 + w % 2][:, q * P:(q + 1) * P],
                                                    att[w % 2][:, kt, q * P:(q + 1) * P], rv[:, kt, w * P:(w + 1) * P],
                                                    start=(kt == 0), stop=(kt == TT - 1), skip_group_check=True)
                    last.then_inc(sem("ret_o"), 1)
            pe.wait_ge(*step("ret_done"))
            for q in range(LT):
                for c in range(4):
                    last = nc.tensor.transpose(bank[5 + q][:, c * P:(c + 1) * P], oC[:, q, c * P:(c + 1) * P], ident)
                last.then_inc(sem("ret_t"), 1)
            pe.wait_ge(*step("wad_tanh"))
            pe.wait_ge(sem("lora_in"), 64)
            for n in range(16):
                if n >= 4:
                    pe.wait_ge(sem("lora_out"), n - 3)
                nc.tensor.matmul(bank[n % 4][:, :], lw[n // 4][:, (n % 4) * P:(n % 4 + 1) * P],
                                 wadt.rearrange("p a b -> p (a b)"), start=True, stop=True).then_inc(sem("lora"), 1)
            pe.wait_ge(sem("v_shift"), 4)
            pe.wait_ge(sem("ret_t_out"), 2)
            for tt in range(TT):
                for c in range(4):
                    last = nc.tensor.transpose(bank[4 + tt][:, c * P:(c + 1) * P], vs[:, tt, c, :], ident)
                last.then_inc(sem("v_t"), 1)
            pe.wait_ge(*step("kk_sq"))
            pe.wait_ge(sem("lora_out"), 16)
            for tt in range(TT):
                nc.tensor.matmul(bank[tt][:, :], headones, sqa[:, tt, :], start=True, stop=True).then_inc(
                    sem("kk_sum"), 1)
            pe.wait_ge(sem("v_t_out"), TT)
            pe.wait_ge(sem("kk_root"), TT)

            def item(n):
                b, kind, _, _ = items[n]
                d, tt = batches[b]
                _, _, engine, count = items[n - 2]
                if n >= 2:
                    pe.wait_ge(sem(f"rw_item_{engine}"), count)
                ps = bank[n % 2]
                if kind in ("a", "b", "k"):
                    src = {"a": arp[:, :, 0, :], "b": bb, "k": kd}[kind]
                    for c in range(4):
                        last = nc.tensor.transpose(ps[:, c * P:(c + 1) * P], src[:, c, :], ident)
                elif kind == "bonus":
                    for c in range(4):
                        last = nc.tensor.matmul(ps[:, 2 * c:2 * c + 2], cum[1 + d][:, c, :], headsel, start=True,
                                                stop=True, skip_group_check=True)
                elif kind in ("low0", "low1"):
                    for j in range(4):
                        h = 4 * int(kind[3]) + j
                        last = nc.tensor.matmul(ps[:, j * P:(j + 1) * P], arp[:, h // 2, 0, :], bz[:, h, :],
                                                start=True, stop=True, skip_group_check=True)
                else:
                    out_, m = split(ps[:, :], 4, P), 2 if tt >= 2 else 1
                    rhs = arp[:, kind // 2, 0:m, :]
                    nc.tensor.matmul(out_[:, 0:m], bz[:, kind, :], rhs, start=True, stop=True, skip_group_check=True)
                    last = nc.tensor.matmul(out_[:, 2:2 + m], kz[:, kind, :], rhs, start=True, stop=True,
                                            skip_group_check=True)
                last.then_inc(sem("rw_item"), 1)

            pe.wait_ge(sem("rw_feat"), 1)
            for n in items_of(0):
                item(n)
            nlat = 0
            for b, (d, tt) in enumerate(batches):
                latent = tt >= 2
                u4 = um[b % 2]
                for n in items_of(b)[-1:] + [i for i in items_of(b) if items[i][1] == "k"]:
                    pe.wait_ge(sem(f"rw_item_{items[n][2]}"), items[n][3])
                if b:
                    pe.wait_ge(sem("rw_s"), 4 * b)
                for lv in range(LEVELS):
                    n, nx = 2 * (LEVELS * b + lv), 2 * ((LEVELS - 1) * b + lv)
                    for hf in range(2):
                        if lv:
                            pe.wait_ge(sem("rw_x"), nx - 1 + hf)
                        for j in range(4):
                            last = nc.tensor.matmul(bank[4 + hf][:, j * P:(j + 1) * P], u4[:, hf, j, 0],
                                                    xm[:, hf, j, :], start=True, stop=True, skip_group_check=True)
                        last.then_inc(sem("rw_lx"), 1)
                    for hf in range(2):
                        pe.wait_ge(sem("rw_z"), n + hf + 1)
                        if lv:
                            pe.wait_ge(sem("rw_g"), n - 1 + hf)
                        if lv < LEVELS - 1:
                            for j in range(4):
                                last = nc.tensor.matmul(bank[hf][:, j * P:(j + 1) * P], gm[:, hf, j, :],
                                                        zm[:, hf, j, :], start=True, stop=True,
                                                        skip_group_check=True)
                            last.then_inc(sem("rw_xz"), 1)
                        for j in range(4):
                            last = nc.tensor.matmul(bank[2 + hf][:, j * P:(j + 1) * P], zm[:, hf, j, :],
                                                    gm[:, hf, j, :], start=True, stop=True, skip_group_check=True)
                        last.then_inc(sem("rw_gz"), 1)

                def next_items(part):
                    if b + 1 < len(batches):
                        for n in items_of(b + 1, part):
                            item(n)

                if b + 1 < len(batches):
                    pe.wait_ge(sem("rw_feat"), b + 2)
                for hf in range(2):
                    for j in range(4):
                        h = 4 * hf + j
                        if j == 0:
                            if nlat:
                                pe.wait_ge(sem("rw_y"), 2 * (nlat - 1) + hf + 1)
                            else:
                                pe.wait_ge(sem("rw_x"), 2 * (LEVELS - 1) * (b + 1))
                        nc.tensor.matmul(bank[6 + hf][:, 2 * P + j * 64:2 * P + (j + 1) * 64], u4[:, hf, j, 2],
                                         vtok[:, tt, 64 * h:64 * h + 64], start=True, stop=True,
                                         skip_group_check=True)
                    pe.wait_ge(sem("rw_g"), 2 * LEVELS * (b + 1) - 1 + hf)
                    for j in range(4):
                        h = 4 * hf + j
                        last = nc.tensor.matmul(
                            bank[6 + hf][64 * (j % 2):64 * (j % 2) + 64, (j // 2) * P:(j // 2 + 1) * P],
                            atok[b % 2].rearrange("p a b -> p (a b)")[:, 64 * h:64 * h + 64], gm[:, hf, j, :],
                            start=True, stop=True, skip_group_check=True)
                    last.then_inc(sem("rw_w1_mm"), 1)
                next_items(0)
                for hf in range(2):
                    pe.wait_ge(sem("rw_mv"), 2 * b + hf + 1)
                    for j in range(4):
                        last = nc.tensor.matmul(bank[4 + hf][:, j * 64:(j + 1) * 64], gm[:, hf, j, :],
                                                w1mv[:, hf, 2 * P + j * 64:2 * P + (j + 1) * 64], start=(j == 0),
                                                stop=False, skip_group_check=True)
                    last.then_inc(sem("rw_w2_mm"), 1)
                    if latent:
                        for j in range(4):
                            h = 4 * hf + j
                            nc.tensor.matmul(bank[6 + hf][:, j * 64:(j + 1) * 64], u4[:, hf, j, 3],
                                             vtok[:, tt, 64 * h:64 * h + 64], start=(j == 0), stop=False,
                                             skip_group_check=True)
                next_items(1)
                if b == 4:
                    pe.wait_ge(*step("rw_s_reset"))
                for i, c in enumerate((0, 1) if d == 0 else (1, 0)):
                    rows = slice(CH * c, CH * c + CH)
                    for hf in range(2):
                        if 4 * b + 2 * i:
                            pe.wait_ge(sem("rw_s"), 4 * b + 2 * i + hf - 1)
                        for p in range(2):
                            last = nc.tensor.matmul(bank[4 + hf][rows, p * P:(p + 1) * P],
                                                    w1mv[:, hf, p * P + CH * c:p * P + CH * c + CH],
                                                    sst[i][:, 2 * hf + p, :], start=False, stop=True,
                                                    skip_group_check=True)
                        last.then_inc(sem("rw_u_mm"), 1)
                        for p in range(2):
                            w = 2 * hf + p
                            if latent:
                                nc.tensor.matmul(bank[6 + hf][rows, p * P:(p + 1) * P], rr[b % 2][:, w, rows],
                                                 sst[i][:, w, :], start=False, stop=False, skip_group_check=True)
                            nc.tensor.matmul(bank[2 + hf][:, p * P:(p + 1) * P], ktok[b % 2][rows, w, :],
                                             vtok[rows, tt, w * P:(w + 1) * P], start=(p == 0), stop=False,
                                             skip_group_check=True)
                    next_items(2 + 2 * i)
                    for hf in range(2):
                        pe.wait_ge(sem("rw_u"), 4 * b + 2 * i + hf + 1)
                        for p in range(2):
                            last = nc.tensor.matmul(bank[2 + hf][:, p * P:(p + 1) * P],
                                                    btok[b % 2][rows, 2 * hf + p, :],
                                                    w2[rows, hf, p * P:(p + 1) * P], start=False, stop=True,
                                                    skip_group_check=True)
                        last.then_inc(sem("rw_s_mm"), 1)
                    if i == 0:
                        next_items(3)
                if latent:
                    for hf in range(2):
                        for j in range(4):
                            last = nc.tensor.matmul(bank[6 + hf][:, j * 64:(j + 1) * 64], u4[:, hf, j, 1],
                                                    w2[:, hf, j * 64:(j + 1) * 64], start=False, stop=(j == 3),
                                                    skip_group_check=True)
                        last.then_inc(sem("rw_y_mm"), 1)
                    nlat += 1
                next_items(5)
            pe.wait_ge(sem("gup_in"), 16)
            for q in range(LT):
                nc.tensor.matmul(bank[q][:, :], gsig[0:GD, q * P:(q + 1) * P], gup[0:GD, :], start=True,
                                 stop=True).then_inc(sem("g_mm"), 1)
            pe.wait_ge(sem("a_done"), LT)
            for q in range(LT):
                for c in range(4):
                    last = nc.tensor.transpose(bank[6 + q][:, c * P:(c + 1) * P], yacc[:, q, c * P:(c + 1) * P], ident)
                last.then_inc(sem("a_t"), 1)
            pe.wait_ge(sem("a_t_out"), LT)
            for n, (_, x) in enumerate(mix):
                pe.wait_ge(sem(f"wo_in{n % 6}"), 16 * (n // 6 + 1))
                for b in range(8):
                    tt, c = b // 4, b % 4
                    last = nc.tensor.matmul(bank[b][:, :], x[:, tt * P:(tt + 1) * P],
                                            woring[n % 6][:, BANK * c:BANK * (c + 1)], start=(n == 0),
                                            stop=(n == KT - 1))
                last.then_inc(sem("wo_used"), 1)
            pe.wait_ge(*step("u_ready"))
            for n in range(8):
                if n >= 4:
                    pe.wait_ge(sem("u_t_out"), n - 3)
                for k in range(2 * n, 2 * n + 2):
                    for tt in range(LT):
                        last = nc.tensor.transpose(bank[n % 4][:, (k % 2) * LAT + tt * P:(k % 2) * LAT + (tt + 1) * P],
                                                   ub[:, tt, k * P:(k + 1) * P], ident)
                last.then_inc(sem("u_t"), 1)
            pe.wait_ge(sem("router_in"), 32)
            pe.wait_ge(sem("u_t_out"), 8)
            for k in range(KT):
                last = nc.tensor.matmul(bank[4][0:N_EXPERTS, 0:LAT], rwt[:, k, :], uT[:, k, :], start=(k == 0),
                                        stop=(k == KT - 1))
            last.then_inc(step("logits")[0], 1)
            pe.wait_ge(*step("logits_out"))
            for tt in range(LT):
                last = nc.tensor.transpose(bank[5][:, N_EXPERTS * tt:N_EXPERTS * (tt + 1)],
                                           lgT[0:N_EXPERTS, tt * P:(tt + 1) * P], ident[0:N_EXPERTS, 0:N_EXPERTS])
            last.then_inc(step("logits_t")[0], 1)
            pe.wait_ge(sem("route_in"), 16)
            pe.wait_ge(*step("selected"))
            sel = rt(3)
            nc.tensor.matmul(bank[6][:, 0:16], before, sel[:, 0], start=True, stop=True, skip_group_check=True)
            nc.tensor.matmul(bank[6][:, 16:32], before, sel[:, 1], start=True, stop=False, skip_group_check=True)
            nc.tensor.matmul(bank[6][:, 16:32], ones, sel[:, 0], start=False, stop=True, skip_group_check=True)
            nc.tensor.matmul(bank[6][:, 32:48], ones, sel[:, 0], start=True, stop=False, skip_group_check=True)
            nc.tensor.matmul(bank[6][:, 32:48], ones, sel[:, 1], start=False, stop=True,
                             skip_group_check=True).then_inc(step("ranks")[0], 1)
            pe.wait_ge(*step("onehot"))
            for k in range(KT):
                if k >= 4:
                    pe.wait_ge(sem("xg_out"), k - 3)
                for tt in range(LT):
                    last = nc.tensor.matmul(bank[k % 4][:, :], ub[:, tt, k * P:(k + 1) * P], hot[:, tt, :],
                                            start=(tt == 0), stop=(tt == LT - 1))
                last.then_inc(sem("xg_mm"), 1)
            for s in range(ST):
                for tt in range(LT):
                    last = nc.tensor.transpose(bank[6 + s // 2][:, (s % 2) * LAT + tt * P:(s % 2) * LAT + (tt + 1) * P],
                                               hotg[:, tt, s * P:(s + 1) * P], ident)
                if s % 2 == 1:
                    last.then_inc(sem("hot_t"), 1)
            pe.wait_ge(sem("xg_out"), KT)
            pe.wait_ge(sem("hot_t_out"), 2)
            pe.wait_ge(*step("xg_pad"))

            def expert(n, first):
                start = pe.value_load(starts[0:1, bass.ds(n, 1)], min_val=0, max_val=PAIRS)
                window = xg[:, :, bass.ds(start, P)]
                if not first:
                    pe.wait_ge(sem("h_out"), n * 2)
                for j in range(4):
                    for w in range(2) if j < 3 else (0, 1):
                        slot = (2 * j + w) % 6
                        pe.wait_ge(sem(f"ew_in{slot}"), n * 32 + 16 * ((2 * j + w) // 6 + 1))
                        if j == 3:
                            continue
                        for f in range(4):
                            for k in range(4 * j, 4 * j + 4):
                                last = nc.tensor.matmul(bank[2 * (f // 2) + w][:, (f % 2) * P:(f % 2 + 1) * P],
                                                        ering[slot][:, k % 4, f * P:(f + 1) * P], window[:, k, :],
                                                        start=(k == 0 and f % 2 == 0), stop=False, skip_group_check=True)
                        last.then_inc(sem("ew_used"), 1)
                for half in range(2):
                    for w in range(2):
                        for f in range(2 * half, 2 * half + 2):
                            for k in range(12, 16):
                                last = nc.tensor.matmul(bank[2 * half + w][:, (f % 2) * P:(f % 2 + 1) * P],
                                                        ering[w][:, k % 4, f * P:(f + 1) * P], window[:, k, :],
                                                        start=False, stop=(k == KT - 1), skip_group_check=True)
                    last.then_inc(sem("h_mm"), 1)

                def product(m, fs):
                    for i in range(2):
                        for f in fs:
                            c = ((2 * m + i) % 4) * P
                            last = nc.tensor.matmul(bank[4 + m % 4][:, i * P:(i + 1) * P],
                                                    ering[(8 + m // 2) % 6][:, f, c:c + P], hT[:, f, :],
                                                    start=(f == 0 and i == 0), stop=(f == 3), skip_group_check=True)
                    return last

                pe.wait_ge(sem("h_out"), n * 2 + 1)
                if not first:
                    pe.wait_ge(sem("y_out"), n * 8)
                for m in range(4):
                    if m % 2 == 0:
                        pe.wait_ge(sem(f"ew_in{2 + m // 2}"), n * 32 + 32)
                    product(m, (0, 1))
                pe.wait_ge(sem("h_out"), n * 2 + 2)
                for m in range(4):
                    product(m, (2, 3)).then_inc(sem("y_mm"), 1)
                for m in range(4, 8):
                    if m % 2 == 0:
                        pe.wait_ge(sem(f"ew_in{2 + m // 2}"), n * 32 + 32)
                    pe.wait_ge(sem("y_out"), n * 8 + m - 3)
                    product(m, (0, 1, 2, 3)).then_inc(sem("y_mm"), 1)

            expert(0, True)
            with pe.Fori(1, N_EXPERTS) as e:
                expert(e, False)
            pe.wait_ge(sem("y_out"), 8 * N_EXPERTS)
            with pe.If(pe.value_load(starts[0:1, 2 * N_EXPERTS:2 * N_EXPERTS + 1]) > P):
                with pe.Fori(N_EXPERTS, 2 * N_EXPERTS) as n:
                    expert(n, False)
                pe.wait_ge(sem("y_out"), 16 * N_EXPERTS)
            for c in range(5):
                if c < 4:
                    if c >= 1:
                        pe.wait_ge(sem("yt_out"), ST * c)
                    for s in range(ST):
                        for i in range(4):
                            last = nc.tensor.transpose(bank[s][:, i * P:(i + 1) * P], ys[:, 4 * c + i, s * P:(s + 1) * P],
                                                       ident)
                        last.then_inc(sem("yt_t"), 1)
                if c >= 1:
                    w = c - 1
                    pe.wait_ge(sem("yt_out"), ST * (w + 1))
                    for tt in range(LT):
                        if w >= 2:
                            pe.wait_ge(sem("ffn_out"), 2 * (w - 2) + tt + 1)
                        for s in range(ST):
                            last = nc.tensor.matmul(bank[4 + 2 * (w % 2) + tt][:, :], hotT[:, s, tt * P:(tt + 1) * P],
                                                    yt[:, s, BANK * w:BANK * (w + 1)], start=(s == 0),
                                                    stop=(s == ST - 1))
                        last.then_inc(sem("ffn"), 1)


_INS = ["x", "c", "ctx", "c_ctx", "mod_w", "mod_b", "w_in", "w_out", "rw_mu", "rw_w0", "rw_w_up", "rw_a0", "rw_a_up",
        "rw_g_up", "rw_k_k", "rw_k_a", "rw_r_k", "rw_gn_g", "rw_gn_b", "mla_q_norm", "mla_kv_norm", "mla_w_uq",
        "mla_w_ukv", "ret_gn_g", "ret_gn_b", "ln1_g", "ln1_b", "ln2_g", "ln2_b", "router_w", "router_b", "exp_w1",
        "exp_w3", "exp_w2"]


def _constants():
    import numpy as np

    c = np.zeros((P, N_CONST), np.float32)

    def put(name, a):
        at, n = CONST[name]
        c[:, at:at + n] = np.asarray(a, np.float64).reshape(P, n)

    i = np.arange(P)
    put("ident", np.eye(P))
    put("ones", np.ones((P, P)))
    put("headones", (i[:, None] // A_HD == i[None] // A_HD))
    rot = np.zeros((P, P))
    for d in range(P):
        low = d % 64 < 32
        rot[d + 32 if low else d - 32, d] = -1.0 if low else 1.0
    put("rot", rot)
    n = B_ROPE // 4
    inv = (10000.0 ** (-np.arange(n, dtype=np.float32) / n)).astype(np.float32)
    pos = np.arange(LAT)
    ang = np.concatenate([(pos // 64).astype(np.float32)[:, None] * inv,
                          (pos % 64).astype(np.float32)[:, None] * inv], -1)
    put("cos", np.cos(ang)[:, i % 32].T)
    put("sin", np.sin(ang)[:, i % 32].T)
    put("reset", np.broadcast_to((np.arange(BANK) % CH != 0), (P, BANK)))
    same = i[:, None] // CH == i[None] // CH
    before, upto = (i[:, None] < i[None]) & same, (i[:, None] <= i[None]) & same
    put("mask_f", np.concatenate([before, upto, before, upto], 1))
    put("mask_b", np.concatenate([before.T, upto.T, before.T, upto.T], 1))
    levels = [1, 2, 4, 8, 16, 32]
    low = [(i[:, None] // b == i[None] // b + 1) & (i[:, None] // (2 * b) == i[None] // (2 * b)) for b in levels]
    put("lower", np.concatenate(low, 1))
    put("upper", np.concatenate([m.T for m in low], 1))
    put("headsel", i[:, None] // A_HD == np.arange(2)[None])
    put("eps", np.broadcast_to([LN_EPS, RWKV_GN_EPS, KK_EPS, 0.0], (P, 4)))
    put("iota16", np.broadcast_to(np.arange(N_EXPERTS), (P, N_EXPERTS)))
    put("iota4", np.broadcast_to(np.arange(4), (P, 4)))
    key, query = np.arange(TOK)[:, None] - CTX, np.arange(LAT)[None]
    decay = []
    for h in range(C_HEADS):
        gf, gb = 1.0 - 2.0 ** (-5.0 - h), 1.0 - 2.0 ** (-5.5 - h)
        fwd = np.where(query >= key, gf ** np.maximum(query - key, 0), 0.0)
        ahead = np.where(key >= 0, key - query, LAT - query + key + CTX)
        bwd = np.where(ahead >= 0, gb ** np.maximum(ahead, 0), 0.0)
        decay.append((fwd + bwd) * C_KD ** -0.5)
    decay = np.stack(decay).reshape(C_HEADS, TT, P, LAT).transpose(2, 0, 1, 3).reshape(P, -1)
    route = np.concatenate([i[:, None] < i[None], np.broadcast_to(np.arange(2 * LAT), (P, 2 * LAT))], 1)
    return c, np.ascontiguousarray(decay, np.float32), np.ascontiguousarray(route, np.float32)


def kernel(**inputs):
    import numpy as _np
    import concourse.bacc as _bacc
    from concourse import mybir as _mybir
    from concourse.bass_utils import run_bass_kernel_spmd as _run

    nc = _bacc.Bacc("TRN2", target_bir_lowering=False, num_devices=1)
    arrays, args = {}, {}
    tables = dict(zip(("const", "decay", "route"), _constants()))
    for name in _INS + list(tables):
        a = _np.ascontiguousarray(tables[name] if name in tables else inputs[name])
        arrays[f"in_{name}_dram"] = a
        args[name] = nc.dram_tensor(f"in_{name}_dram", a.shape, _mybir.dt.from_np(a.dtype), kind="ExternalInput").ap()
    args["out"] = nc.dram_tensor("out_0_dram", (1, LAT, D), F32, kind="ExternalOutput").ap()
    build_program(nc, args)
    r = _run(nc, [arrays], core_ids=[0])
    return r.results[0]["out_0_dram"]
```

```python
from contextlib import ExitStack
import math

import concourse.bass as bass
from concourse import mybir

F32 = mybir.dt.float32
ALU = mybir.AluOpType
ACT = mybir.ActivationFunctionType
AX = mybir.AxisListType

P = 128
D = 2048
KT = D // P
LAT = 256
CTX = 256
TOK = LAT + CTX
TT = TOK // P
LT = LAT // P
BANK = 512

A_HEADS, A_HD = 8, 64
A_W = A_HEADS * A_HD
A_PAIRS = A_HEADS // 2
CH = 64
DECAY = math.exp(-0.5)
B_HEADS, B_NOPE, B_ROPE, B_VD, B_QR, B_KVR = 8, 128, 64, 128, 512, 256
C_HEADS, C_KD, C_VD = 4, 64, 128
C_W = C_HEADS * C_VD
N_EXPERTS, N_GROUPS, D_EXPERT = 16, 4, 512
ROUTE_SCALE = 2.5
ALPHA = 2 ** 0.25
LN_EPS, RWKV_GN_EPS, KK_EPS = 1e-5, 64e-5, 1e-12

COL_R, COL_K, COL_V = 0, A_W, 2 * A_W
COL_WAD = 3 * A_W
COL_GD = COL_WAD + 128
GD = 96
COL_CQ = COL_GD + GD
COL_CKV = COL_CQ + B_QR
COL_KR = COL_CKV + B_KVR
COL_RQ = COL_KR + B_ROPE
COL_RK = COL_RQ + C_HEADS * C_KD
COL_RV = COL_RK + C_HEADS * C_KD
COL_GT = COL_RV + C_W

V_MU, V_W0, V_A0, V_KK, V_KA, V_RK, V_QN, V_KVN, V_MODB = 0, 14, 22, 30, 34, 38, 42, 46, 48
N_VEC = 80


def const_layout():
    sizes = [("ident", P), ("ones", P), ("headones", P), ("rot", P), ("cos", LAT), ("sin", LAT),
             ("iota16", N_EXPERTS), ("reset", BANK), ("mask_f", BANK), ("mask_b", BANK),
             ("lower", 6 * P), ("upper", 6 * P),
             ("headsel", 2), ("eps", 4), ("iota4", 4)]
    at, out = 0, {}
    for name, n in sizes:
        out[name] = (at, n)
        at += n
    return out, at


CONST, N_CONST = const_layout()


STEPS = {
    "vector": ("vst_zero", "acc_zero", "c_silu", "cond", "vecs", "mod_t", "rms_sq", "cq_norm", "ckv_norm",
               "kr_ready", "ret_qk", "shifted", "wad_shift", "gd_shift", "kk_sq", "ret_normed", "rw_prep",
               "rw_s_reset", "u_ready0", "u_half", "u_ready", "ln1_done", "selected", "onehot", "hot_gates"),
    "gpsimd": ("pads", "qrz_zero", "rqz_zero", "lw_zero", "rw_zero", "ret_done", "xg_pad"),
    "scalar": ("c_sig", "wad_tanh", "ret_gate", "gd_sig", "logits_out", "scored"),
    "tensor": ("mod", "kr_rot", "logits", "logits_t", "ranks"),
}


def build_program(nc, t):
    with ExitStack() as ctx:
        starts = ctx.enter_context(nc.sbuf_tensor("starts", [1, 2 * N_EXPERTS + 1], mybir.dt.int32))
        parked = nc.dram_tensor("parked_rows", (1, 4 * D), F32).ap()
        arena = ctx.enter_context(nc.sbuf_tensor("arena", [P, 52800], F32))
        bank = [ctx.enter_context(nc.psum_tensor(f"bank{i}", [P, BANK], F32)) for i in range(8)]
        S = {}

        def sem(name):
            if name not in S:
                S[name] = ctx.enter_context(nc.semaphore(name))
            return S[name]

        def step(name):
            for engine, names in STEPS.items():
                if name in names:
                    return sem(f"{engine}_steps"), names.index(name) + 1
            raise KeyError(name)

        class Counter:

            def __init__(self, eng, name):
                self.eng, self.name, self.n = eng, name, {}

            def __call__(self, ins, signal=None):
                name = signal or self.name
                if name in sum(STEPS.values(), ()):
                    s, n = step(name)
                    ins.then_inc(s, 1)
                    self.eng.wait_ge(s, n)
                    return
                self.n[name] = self.n.get(name, 0) + 1
                ins.then_inc(sem(name), 1)
                self.eng.wait_ge(sem(name), self.n[name])

        def cols(at, *dims):
            n = math.prod(dims)
            v = arena[:, at:at + n]
            if len(dims) == 2:
                v = v.rearrange("p (a b) -> p a b", a=dims[0])
            elif len(dims) == 3:
                v = v.rearrange("p (a b c) -> p a b c", a=dims[0], b=dims[1])
            elif len(dims) == 4:
                v = v.rearrange("p (a b c d) -> p a b c d", a=dims[0], b=dims[1], c=dims[2])
            return v

        def split(ap, *dims):
            if len(dims) == 2:
                return ap.rearrange("p (a b) -> p a b", a=dims[0])
            return ap.rearrange("p (a b c) -> p a b c", a=dims[0], b=dims[1])

        at = 0

        def take(*dims):
            nonlocal at
            v = cols(at, *dims)
            at += math.prod(dims)
            return v

        cst = take(N_CONST)
        vec = take(N_VEC)
        cT = take(KT, 2)
        modT = take(32, 2)
        small = take(536)
        acc = take(4, D)
        x0 = at
        xT = cols(x0, KT, TOK)
        gr0 = x0 + 8192
        wr0 = gr0 + 4096
        o0 = wr0 + 12288
        xtok = cols(o0, TT, D)
        end = 52800

        def const(name):
            a, n = CONST[name]
            return cst[:, a:a + n]

        ident, ones, headones, rot = (const(n) for n in ("ident", "ones", "headones", "rot"))
        cosT, sinT, reset = const("cos"), const("sin"), const("reset")
        lower, upper = split(const("lower"), 6, P), split(const("upper"), 6, P)
        masks = [split(const("mask_f"), 4, P), split(const("mask_b"), 4, P)]
        headsel = const("headsel")
        eps = const("eps")

        a2 = o0

        def out(*dims):
            nonlocal a2
            v = cols(a2, *dims)
            a2 += math.prod(dims)
            return v

        cq = out(4, LAT)
        ckv = out(2, TOK)
        kr = out(TOK)
        ret0 = a2
        rq = out(2, LAT)
        rk = out(2, TOK)
        rv = out(TT, C_W)
        gt = out(LT, C_W)
        ret1 = a2
        rp = out(4, LAT + 2)
        kp = out(4, 2, 258)
        vp = out(4, 2, 258)
        wp = out(2, 258)
        gp = out(LAT + 2)
        assert a2 <= end, a2

        vst = cols(gr0, P)
        crow = cols(gr0 + P, P)
        csig = cols(gr0 + 2 * P, P)
        mring = [cols(wr0 + 4096 * s, 8, BANK) for s in range(3)]
        mrow = cols(gr0, 8, BANK)[0:2]
        PE_BANKS = 5
        macc = cols(o0 + 8192, 2, (8 - PE_BANKS) * BANK)
        wring = [cols(wr0 + 4096 * s, KT, 256) for s in range(3)]
        gring = [cols(gr0 + 1024 * s, 1024) for s in range(4)]

        groups = ([(c, 256) for c in range(0, COL_WAD, 256)] + [(COL_WAD, 224), (COL_CQ, 256), (COL_CQ + 256, 256),
                  (COL_CKV, 256), (COL_KR, 64), (COL_RQ, 256), (COL_RK, 256), (COL_RV, 256), (COL_RV + 256, 256),
                  (COL_GT, 256), (COL_GT + 256, 256)])
        tiles = []
        both = (0, TOK)
        lat = (CTX, TOK)
        for g, (c0, n) in enumerate(groups):
            for j in range(0, n, P):
                c = c0 + j
                w = min(P, n - j)
                if c < COL_K:
                    tiles.append((g, True, j, w, lat, rp[:, c // P, 1:1 + LAT]))
                elif c < COL_V:
                    tiles.append((g, True, j, w, both, kp[:, (c - COL_K) // P, :, 1:257]))
                elif c < COL_WAD:
                    tiles.append((g, True, j, w, both, vp[:, (c - COL_V) // P, :, 1:257]))
                elif c == COL_WAD:
                    tiles.append((g, True, j, w, both, wp[:, :, 1:257]))
                elif c == COL_GD:
                    tiles.append((g, True, j, w, lat, gp[:GD, 1:1 + LAT]))
                elif c < COL_CKV:
                    tiles.append((g, True, j, w, lat, cq[:, (c - COL_CQ) // P, :]))
                elif c < COL_KR:
                    tiles.append((g, True, j, w, both, ckv[:, (c - COL_CKV) // P, :]))
                elif c == COL_KR:
                    tiles.append((g, True, 0, P, both, kr))
                elif c < COL_RK:
                    tiles.append((g, True, j, w, lat, rq[:, (c - COL_RQ) // P, :]))
                elif c < COL_RV:
                    tiles.append((g, True, j, w, both, rk[:, (c - COL_RK) // P, :]))
            if c0 >= COL_RV:
                gate = c0 >= COL_GT
                dst, cc = (gt, c0 - COL_GT) if gate else (rv, c0 - COL_RV)
                for tt in range(LT if gate else TT):
                    t0 = tt * P + (CTX if gate else 0)
                    tiles.append((g, False, 0, 256, (t0, t0 + P), dst[:, tt, cc:cc + 256]))
        last_tile = {g: n for n, (g, *_) in enumerate(tiles)}

        wuq = cols(wr0, 4, 8 * 192)
        wukv = cols(wr0 + 6144, 2, 2048)
        oB = cols(wr0 + 10240, B_HEADS, LAT)
        qn = cols(x0, B_HEADS, LAT)
        qrz = cols(x0 + 2048, B_HEADS, LAT)
        kn = cols(x0 + 4096, B_HEADS, TOK)
        sqq = cols(gr0, 4, LAT)
        sqk = cols(gr0 + 1024, 2, TOK)
        rsq = cols(gr0 + 2048, LAT)
        rsk = cols(gr0 + 2304, TOK)
        qr = cols(gr0 + 2816, 4, LAT)
        rtmpk = cols(gr0 + 3840, LAT)
        vB = cols(wr0, TT, B_HEADS * B_VD)
        prob = [cols(wr0 + 4096 + BANK * s, TOK) for s in range(3)]
        probT = [cols(wr0 + 4096 + BANK * (3 + s), TT, P) for s in range(2)]
        score_bank = [bank[0], bank[1], bank[6]]
        mx, den, rden = small[:, 0:16], small[:, 16:32], small[:, 32:48]

        dTall = cols(gr0, C_HEADS * TT, LAT)
        rqz = cols(o0, C_HEADS, LAT)
        att = [cols(x0 + 1024 * (1 + s), TT, LAT) for s in range(2)]
        oC = cols(wr0 + 6144, LT, C_W)
        nt = cols(wr0 + 7168, LT, C_W)
        rtmp2 = cols(gr0 + 2304, BANK)
        gnc = cols(wr0 + 8192, 2, C_W)
        oCT = cols(o0, 4, LAT)
        oAT = cols(o0 + 1024, 4, LAT)
        stat = small[:, 48:304]

        b1 = x0
        LORAS = (0, 2, 1, 3)

        def r1(*dims):
            nonlocal b1
            v = cols(b1, *dims)
            b1 += math.prod(dims)
            return v

        sigw = [r1(TT, 4, P) for _ in range(2)]
        siga = [r1(TT, 4, P) for _ in range(2)]
        vtok = r1(TT, A_W)
        gsig = r1(LAT)
        gup = r1(A_W)
        lw0 = b1
        lw = [cols(x0 + 6144 + A_W * i, A_W) for i in range(3)] + [cols(wr0 + 9216, A_W)]
        wadt = cols(wr0 + 9216 + A_W, 2, 256)
        assert b1 <= wr0 + 10240, (b1, wr0)
        acc0 = N_CONST + N_VEC + KT * 2 + 32 * 2 + 536
        kkn, ks, vs = (cols(acc0 + 2048 * i, TT, 4, P) for i in range(3))
        rs, rrk = (cols(acc0 + 6144 + 1024 * i, LT, 4, P) for i in range(2))
        sqa = cols(ret0, 4, TOK)
        pools = [[ret1, end], [lw0, wr0 + 10240], [o0 + 1024, ret1]]

        def tmp(*dims):
            n = math.prod(dims)
            for p in pools:
                if p[1] - p[0] >= n:
                    v = cols(p[0], *dims)
                    p[0] += n
                    return v
            raise AssertionError((pools, dims))

        bz = tmp(A_HEADS, P)
        kz = tmp(A_HEADS, P)
        sst = [tmp(4, P) for _ in range(2)]
        arp = tmp(4, 2, P)
        cum = [tmp(4, P) for _ in range(4)]
        kd = tmp(4, P)
        bb = tmp(4, P)
        um = [tmp(2, 4, 4, P) for _ in range(2)]
        xm, gm, zm = (tmp(2, 4, P) for _ in range(3))
        w1mv = tmp(2, BANK)
        yacc = tmp(LT, A_W)
        rr, atok, btok, ktok = ([tmp(4, P) for _ in range(2)] for _ in range(4))
        w2 = tmp(2, 2 * P)
        stmp = [tmp(2, P) for _ in range(2)]
        pc = [small[:, 304:312], small[:, 384:392]]
        nka = small[:, 312:316]
        bonus = small[:, 316:332]
        sel_lo, sel_hi = slice(0, 64), slice(64, 128)

        def bc(ap, n, axis):
            shape = list(ap.shape)
            shape.insert(axis, n)
            return ap.unsqueeze(axis).to_broadcast(shape)

        block = ctx.enter_context(nc.Block())

        batches = [(0, 0), (0, 1), (0, 2), (0, 3), (1, 1), (1, 0), (1, 3), (1, 2)]
        LEVELS = 5
        items, evacuated = [], {"vector": 0, "scalar": 0}
        for b_, (_, tt_) in enumerate(batches):
            for kind in ["bonus"] * (tt_ >= 2) + ["a", 0, "b", 1, "k", 2, 3, "low0", 4, 5, 6, 7, "low1"]:
                engine = "scalar" if kind in ("a", "b", "k") else "vector"
                evacuated[engine] += 1
                items.append((b_, kind, engine, evacuated[engine]))

        def items_of(b, part=None):
            own = [n for n, it in enumerate(items) if it[0] == b]
            at_ = (0, 4, 6, 8, 10, 12, 99)
            return own if part is None else own[at_[part]:at_[part + 1]]

        def blocks(x, n, which):
            return x.rearrange("p j (g two n) -> p j g two n", two=2, n=n)[:, :, :, which]

        mu5, omu = small[:, 332:346], small[:, 346:360]
        umf = um[0][:, 0].rearrange("p a b c -> p (a b c)")
        gna = split(umf[:, 0:2 * A_W], 2, A_W)
        na = split(umf[:, 2 * A_W:4 * A_W], LT, A_W)

        x1 = cols(x0, LT, D)
        ln = cols(x0 + 4096, 2, D)
        ub = cols(x0 + 14336, LT, D)
        uT = cols(x0 + 18432, KT, LAT)
        rw0 = o0 + 2048 + 6 * 2048
        rwt = cols(rw0, KT, N_EXPERTS)
        rbias = cols(rw0 + 256, N_EXPERTS)
        lgT = cols(rw0 + 272, LAT)
        woring = [cols(o0 + at_, D) for at_ in (10240, 12288, 4096, 6144, 8192)]
        mix = ([(A_W // P + h, oB[:, h, :]) for h in range(B_HEADS)] +
               [((A_W + B_HEADS * B_VD) // P + c, oCT[:, c, :]) for c in range(4)] +
               [(c, oAT[:, c, :]) for c in range(4)])
        EARLY = B_HEADS + 4
        wo_pieces = ([("part", n) for n in range(EARLY)] + [("rest", n) for n in range(0, EARLY, 4)] +
                     [("whole", n) for n in range(EARLY, KT)])

        def mix_bank(tt, c):
            return bank[6 + tt] if c == 3 else bank[3 * tt + c]

        PAIRS = 2 * LAT
        ST = PAIRS // P
        xg = cols(x0 + 4096, KT, PAIRS + P)
        ys = cols(x0 + 14336, KT, PAIRS + P)
        yt = cols(x0 + 4096, ST, D)
        ering = [cols(o0 + 2048 * s, 4, BANK) for s in range(6)]
        hot = cols(o0 + 12288, LT, PAIRS)
        hotT = cols(o0 + 13312, ST, LAT)
        assert o0 + 14336 <= rw0
        hotg = cols(CONST["lower"][0], LT, PAIRS)
        hot2 = cols(CONST["lower"][0] + 2 * BANK, BANK)
        lnt = cols(o0, LT, D)
        hs = cols(CONST["lower"][0], 2, 2, P)
        hT = cols(CONST["lower"][0] + BANK, 4, P)
        route = cols(CONST["reset"][0], P + PAIRS)
        before, iota = route[:, 0:P], route[:, P:P + PAIRS]
        ln2 = acc[:, 0:2, :]
        g1r, sh2r, sc2r, g2r = (acc[:, i, :] for i in range(4))
        rt0 = 48
        def rt(i):
            return split(small[:, rt0 + 32 * i:rt0 + 32 * (i + 1)], 2, N_EXPERTS)
        def rg(i):
            return split(small[:, rt0 + 288 + 8 * i:rt0 + 288 + 8 * (i + 1)], 2, 4)
        cnt, off, base, late = (small[:, 400 + 16 * i:416 + 16 * i] for i in range(4))
        excl = split(small[:, 480:512], 2, N_EXPERTS)
        pair_at = [small[:, 512 + 2 * i:514 + 2 * i] for i in range(2)]
        gate = [small[:, 516 + 2 * i:518 + 2 * i] for i in range(2)]
        nmean, dev, lnsum = small[:, 522:524], small[:, 524:526], small[:, 528:536]
        most = small[:, 520:521]
        @block.sync
        def _(sp):
            head = 2 * P
            sp.dma_start(cst[:, 0:head], t["const"][:, 0:head]).then_inc(sem("const_in"), 16)
            sp.dma_start(crow[0:16, :], t["c"].rearrange("a (k p) -> (a k) p", p=P)).then_inc(sem("c_in"), 16)
            sp.dma_start(crow[16:32, :], t["c_ctx"].rearrange("(k p) -> k p", p=P)).then_inc(sem("c_in"), 16)
            for tt in range(TT):
                src = t["ctx"] if tt < 2 else t["x"]
                sp.dma_start(xtok[:, tt, :], src[0, (tt % 2) * P:(tt % 2 + 1) * P, :]).then_inc(
                    sem(f"x_in{tt}"), 16)
            mw = t["mod_w"][0]
            for k in range(KT):
                if k == 3:
                    sp.wait_ge(*step("acc_zero"))
                    sp.dma_start(acc[0:1, :, :].rearrange("p a b -> p (a b)"), t["mod_b"][:, 4096:12288]).then_inc(
                        sem("accb_in"), 16)
                if k >= 3:
                    sp.wait_ge(sem("mod_used"), k - 2)
                    sp.wait_ge(sem("mod_used_v"), k - 2)
                sp.dma_start(mring[k % 3].rearrange("p a b -> p (a b)"), mw[k * P:(k + 1) * P, 0:4096]).then_inc(
                    sem(f"mod_in{k % 3}"), 16)
            win = t["w_in"][0].rearrange("(k p) n -> p k n", p=P)
            for g, (c0, n) in enumerate(groups):
                s = g % 3
                if g == 0:
                    sp.wait_ge(sem("mod_used"), KT)
                    sp.wait_ge(sem("mod_used_v"), KT)
                if g >= 3:
                    sp.wait_ge(sem("proj"), last_tile[g - 3] + 1)
                sp.dma_start(wring[s][:, :, 0:n], win[:, :, c0:c0 + n]).then_inc(sem(f"win_in{s}"), 16)
                if g == 2:
                    sp.dma_start(cst[:, head:], t["const"][:, head:]).then_inc(sem("const_in"), 16)
                if c0 == COL_KR:
                    sp.dma_start(wring[s][:, :, n:2 * n], win[:, :, c0:c0 + n]).then_inc(sem("kr_in"), 16)

            sp.wait_ge(sem("proj"), len(tiles))
            sp.dma_start(wuq, t["mla_w_uq"][0].rearrange("(k p) n -> p k n", p=P)).then_inc(sem("uq_in"), 16)
            sp.dma_start(wukv, t["mla_w_ukv"][0].rearrange("(k p) n -> p k n", p=P)).then_inc(sem("ukv_in"), 16)
            sp.wait_ge(sem("rows_out"), 16)
            sp.dma_start(parked, acc[0:1].rearrange("p a b -> p (a b)")).then_inc(sem("parked"), 16)
            sp.wait_ge(*step("ret_qk"))
            sp.wait_ge(sem("rms_sum"), 2)
            sp.dma_start(dTall.rearrange("p a b -> p (a b)"), t["decay"]).then_inc(sem("decay_in"), 16)
            sp.wait_ge(sem("scores"), 2 * B_HEADS)
            sp.dma_start(gnc[:, 0, :], t["ret_gn_g"][0].partition_broadcast(P)).then_inc(sem("gnc_in"), 16)
            sp.dma_start(gnc[:, 1, :], t["ret_gn_b"][0].partition_broadcast(P)).then_inc(sem("gnc_in"), 16)
            sp.wait_ge(*step("lw_zero"))
            for i, name in enumerate(("rw_w_up", "rw_w_up", "rw_a_up", "rw_a_up")):
                sp.dma_start(lw[i][32 * i:32 * i + 32, :], t[name][0, i % 2]).then_inc(sem("lora_in"), 16)
            sp.wait_ge(sem("ret_att"), 2 * C_HEADS)
            sp.dma_start(gup[0:GD, :], t["rw_g_up"][0]).then_inc(sem("gup_in"), 16)

            def w_out(i):
                kind, n = wo_pieces[i]
                if i >= 5:
                    sp.wait_ge(sem("wo_used"), i - 4)
                done, dst = sem(f"wo_in{i % 5}"), woring[i % 5]
                if kind == "rest":
                    for j in range(4):
                        kt = mix[n + j][0]
                        sp.dma_start(dst[:, BANK * j:BANK * (j + 1)],
                                     t["w_out"][0, kt * P:(kt + 1) * P, 3 * BANK:]).then_inc(done, 16)
                    return
                kt, width = mix[n][0], 3 * BANK if kind == "part" else D
                sp.dma_start(dst[:, 0:width], t["w_out"][0, kt * P:(kt + 1) * P, 0:width]).then_inc(done, 16)

            sp.wait_ge(sem("rw_item"), len(items))
            w_out(0)
            w_out(1)
            sp.wait_ge(sem("rw_y"), 8)
            sp.wait_ge(sem("rw_y_mm"), 8)
            sp.dma_start(gna[:, 0, :], t["rw_gn_g"][0].partition_broadcast(P)).then_inc(sem("gna_in"), 16)
            sp.dma_start(gna[:, 1, :], t["rw_gn_b"][0].partition_broadcast(P)).then_inc(sem("gna_in"), 16)
            for i in range(2, 9):
                w_out(i)
            sp.dma_start(x1, t["x"][0].rearrange("(a p) n -> p a n", p=P)).then_inc(sem("xl_in"), 16)
            sp.dma_start(ln[:, 0, :], t["ln1_g"][0].partition_broadcast(P)).then_inc(sem("ln_in"), 16)
            sp.dma_start(ln[:, 1, :], t["ln1_b"][0].partition_broadcast(P)).then_inc(sem("ln_in"), 16)
            sp.wait_ge(sem("parked"), 16)
            sp.dma_start(acc.rearrange("p a b -> p (a b)"), parked[0].partition_broadcast(P)).then_inc(
                sem("rows_in"), 16)
            sp.dma_start(route, t["route"]).then_inc(sem("route_in"), 16)
            for i in range(9, len(wo_pieces)):
                w_out(i)
            sp.wait_ge(sem("a_t_out"), LT)
            sp.dma_start(rwt, t["router_w"].rearrange("(k p) n -> p k n", p=P)).then_inc(sem("router_in"), 16)
            sp.dma_start(rbias, t["router_b"].partition_broadcast(P)).then_inc(sem("router_in"), 16)
            sp.wait_ge(*step("u_ready"))
            sp.dma_start(ln2[:, 0, :], t["ln2_g"][0].partition_broadcast(P)).then_inc(sem("ln2_in"), 16)
            sp.dma_start(ln2[:, 1, :], t["ln2_b"][0].partition_broadcast(P)).then_inc(sem("ln2_in"), 16)

            def piece_used(n, i):
                if i < 6:
                    sp.wait_ge(sem("ew_used"), n * 6 + (i + 1))
                elif i < 8:
                    sp.wait_ge(sem("h_mm"), n * 2 + 2)
                else:
                    sp.wait_ge(sem("y_mm"), n * 8 + 2 * (i - 7))

            def expert(n, e, first):
                for i in range(12):
                    if i >= 6:
                        piece_used(n, i - 6)
                    elif not first:
                        piece_used(n - 1, i + 6)
                    if i < 8:
                        w = t["exp_w1" if i % 2 == 0 else "exp_w3"][0]
                        src = w[bass.ds(e, 1), BANK * (i // 2):BANK * (i // 2 + 1), :].rearrange(
                            "a (k p) n -> p (a k) n", p=P)
                    else:
                        src = t["exp_w2"][0][bass.ds(e, 1), :, BANK * (i - 8):BANK * (i - 7)].rearrange(
                            "a (k p) n -> p (a k) n", p=P)
                    sp.dma_start(ering[i % 6], src).then_inc(sem(f"ew_in{i % 6}"), 16)

            sp.wait_ge(sem("mix_mm"), 8)
            expert(0, 0, True)
            with sp.Fori(1, N_EXPERTS) as e:
                expert(e, e, False)
            sp.wait_ge(*step("onehot"))
            with sp.If(sp.value_load(starts[0:1, 2 * N_EXPERTS:2 * N_EXPERTS + 1]) > P):
                with sp.Fori(N_EXPERTS, 2 * N_EXPERTS) as n:
                    expert(n, n - N_EXPERTS, False)
            for tt in range(LT):
                for i in range(2):
                    cc = slice(D // 2 * i, D // 2 * (i + 1))
                    sp.wait_ge(sem("done"), 2 * tt + i + 1)
                    sp.dma_start(t["out"][0, tt * P:(tt + 1) * P, cc], x1[:, tt, cc]).then_inc(sem("stored"), 16)
            sp.wait_ge(sem("stored"), 32 * LT)
        @block.gpsimd
        def _(pool):
            pool.wait_ge(*step("mod"))
            nc.gpsimd.memset(rp[:, :, 0:LAT + 2:LAT + 1], 0.0)
            nc.gpsimd.memset(kp[:, :, :, 0:258:257].rearrange("p a b c -> p (a b) c"), 0.0)
            nc.gpsimd.memset(vp[:, :, :, 0:258:257].rearrange("p a b c -> p (a b) c"), 0.0)
            nc.gpsimd.memset(wp[:, :, 0:258:257], 0.0)
            nc.gpsimd.memset(gp[:, 0:LAT + 2:LAT + 1], 0.0).then_inc(step("pads")[0], 1)
            mw = t["mod_w"][0]
            for q in range(8):
                s = q % 4
                if q >= 4:
                    pool.wait_ge(sem(f"gate_used{s}"), 1)
                pool.dma_start(gring[s], mw[0:P, 4096 + 1024 * q:4096 + 1024 * (q + 1)]).then_inc(
                    sem(f"gate_in{s}"), 16)
            with pool.Fori(1, KT) as k:
                for q in range(8):
                    s = q % 4
                    pool.wait_ge(sem(f"gate_used{s}"), k * 2 + q // 4)
                    pool.dma_start(gring[s], mw[bass.ds(k * P, P), 4096 + 1024 * q:4096 + 1024 * (q + 1)]).then_inc(
                        sem(f"gate_in{s}"), 16)

            pool.wait_ge(sem("proj"), len(tiles))
            nc.gpsimd.memset(qrz, 0.0).then_inc(step("qrz_zero")[0], 1)
            pool.wait_ge(sem("qn_mm"), B_HEADS)
            nc.gpsimd.memset(rqz, 0.0).then_inc(step("rqz_zero")[0], 1)
            pool.wait_ge(sem("scores"), 2 * B_HEADS)
            pool.wait_ge(sem("v_mm"), 2 * TT)
            for i in range(4):
                last = nc.gpsimd.memset(lw[i], 0.0)
            last.then_inc(step("lw_zero")[0], 1)
            pool.wait_ge(*step("shifted"))
            for v in (bz, kz, sst[0], sst[1]):
                last = nc.gpsimd.memset(v, 0.0)
            last.then_inc(step("rw_zero")[0], 1)
            L = Counter(pool, "pool_chain")
            pool.wait_ge(sem("gnc_in"), 32)
            pool.wait_ge(*step("ret_gate"))
            L(nc.gpsimd.tensor_tensor(gt, gt, nt, ALU.mult))
            pool.wait_ge(*step("ret_normed"))
            L(nc.gpsimd.tensor_tensor(oC, oC, bc(gnc[:, 0, :], LT, 1), ALU.mult))
            L(nc.gpsimd.tensor_tensor(oC, oC, bc(gnc[:, 1, :], LT, 1), ALU.add))
            L(nc.gpsimd.tensor_tensor(oC, oC, gt, ALU.mult), "ret_done")
            pool.wait_ge(sem("lora"), 16)
            pool.wait_ge(*step("rw_prep"))
            pool.wait_ge(sem("ret_t_out"), 2)
            for b in range(len(batches)):
                for m, name in ((xm, "rw_gz"), (gm, "rw_w2_mm")):
                    for hf in range(2):
                        if b:
                            pool.wait_ge(sem(name), 2 * LEVELS * b - 1 + hf if m is xm else 2 * b - 1 + hf)
                        nc.gpsimd.tensor_copy(m[:, hf], bc(ident, 4, 1)).then_inc(sem("rw_ident"), 1)
            pool.wait_ge(*step("ln1_done"))
            nc.gpsimd.memset(xg[:, :, PAIRS:], 0.0).then_inc(step("xg_pad")[0], 1)
        @block.scalar
        def _(act):
            A = Counter(act, "act_chain")
            act.wait_ge(*step("vst_zero"))

            def rows(at, src, n):
                act.dma_start(vst[at:at + n, :], src).then_inc(sem("vec_in"), 16)

            mu = t["rw_mu"][0]
            rows(V_MU, mu[0:13 * P].rearrange("(r p) -> r p", p=P), 13)
            act.dma_start(vst[V_MU + 13:V_MU + 14, 0:GD], mu[13 * P:13 * P + GD].rearrange(
                "(r p) -> r p", p=GD)).then_inc(sem("vec_in"), 16)
            rows(V_W0, t["rw_w0"][0].rearrange("d (r p) -> (d r) p", p=P), 8)
            rows(V_A0, t["rw_a0"][0].rearrange("d (r p) -> (d r) p", p=P), 8)
            rows(V_KK, t["rw_k_k"][0].rearrange("(r p) -> r p", p=P), 4)
            rows(V_KA, t["rw_k_a"][0].rearrange("(r p) -> r p", p=P), 4)
            rows(V_RK, t["rw_r_k"][0].rearrange("h e -> (h e)").rearrange("(r p) -> r p", p=P), 4)
            rows(V_QN, t["mla_q_norm"][0].rearrange("(r p) -> r p", p=P), 4)
            rows(V_KVN, t["mla_kv_norm"][0].rearrange("(r p) -> r p", p=P), 2)
            rows(V_MODB, t["mod_b"][0, 0:4096].rearrange("(r p) -> r p", p=P), 32)
            act.wait_ge(sem("c_in"), 32)
            nc.scalar.activation(csig[0:32, :], crow[0:32, :], ACT.Sigmoid).then_inc(step("c_sig")[0], 1)
            for k in range(KT):
                act.wait_ge(sem("xt_raw"), k + 1)
                nc.scalar.activation(xT[:, k, :], bank[2 + k % 4][:, :], ACT.Copy).then_inc(sem("xt_out"), 1)
            act.wait_ge(sem("small_t"), 2)
            for b in range(PE_BANKS):
                act.wait_ge(sem("mod_used"), KT)
                nc.scalar.activation(mrow[:, b, :], bank[b][0:2, :], ACT.Copy).then_inc(sem("mod_row"), 1)
            act.wait_ge(*step("mod_t"))
            for k in range(KT):
                ctx_k = xT[:, k, 0:CTX]
                nc.scalar.activation(ctx_k, ctx_k, ACT.Identity, scale=modT[:, 16 + k, 1:2],
                                     bias=modT[:, k, 1:2]).then_inc(sem("xt_mod_ctx"), 1)
            act.wait_ge(*step("pads"))
            for n, (g, stationary, j, w, (t0, t1), dst) in enumerate(tiles):
                act.wait_ge(sem("proj"), n + 1)
                rows_ = w if stationary else P
                width = t1 - t0 if stationary else 256
                src = bank[n % 8][0:rows_, 0:width]
                if len(dst.shape) == 3:
                    src = src.rearrange("p (a b) -> p a b", a=2)
                nc.scalar.activation(dst, src, ACT.Copy).then_inc(sem("proj_out"), 1)
            for q in range(16):
                act.wait_ge(sem("rows"), q + 1)
                nc.scalar.activation(acc.rearrange("p a b -> p (a b)")[:, BANK * q:BANK * (q + 1)], bank[q % 2][:, :],
                                     ACT.Copy).then_inc(sem("rows_out"), 1)

            act.wait_ge(sem("rms_sum"), 1)
            A(nc.scalar.activation(rsq, bank[0][:, 0:LAT], ACT.Sqrt, bias=eps[:, 0:1], scale=1.0 / B_QR), "rms_root")
            act.wait_ge(sem("rms_sum"), 2)
            A(nc.scalar.activation(rsk, bank[1][:, :], ACT.Sqrt, bias=eps[:, 0:1], scale=1.0 / B_KVR), "rms_root")
            for p in range(4):
                act.wait_ge(sem("qr_mm"), p + 1)
                nc.scalar.activation(qr[:, p, :], bank[4 + p % 2][:, 0:LAT], ACT.Copy).then_inc(sem("qr_raw"), 1)
            for h in range(B_HEADS):
                act.wait_ge(sem("qn_mm"), h + 1)
                nc.scalar.activation(qn[:, h, :], bank[h % 4][:, 0:LAT], ACT.Copy).then_inc(sem("qn_out"), 1)
            for h in range(B_HEADS):
                act.wait_ge(sem("kn_mm"), h + 1)
                nc.scalar.activation(kn[:, h, :], bank[h % 4][:, :], ACT.Copy).then_inc(sem("kn_out"), 1)
            for n in range(2 * TT):
                act.wait_ge(sem("v_mm"), n + 1)
                nc.scalar.activation(vB[:, n // 2, BANK * (n % 2):BANK * (n % 2 + 1)], bank[4 + n % 4][:, :],
                                     ACT.Copy).then_inc(sem("v_out"), 1)
            for u in range(2 * B_HEADS + 3):
                if u < 2 * B_HEADS:
                    act.wait_ge(sem("row_max"), u + 1)
                    if u >= 3:
                        act.wait_ge(sem("prob_t"), u - 2)
                    A(nc.scalar.activation(prob[u % 3], score_bank[u % 3][:, :], ACT.Exp, bias=mx[:, u:u + 1],
                                           scale=(B_NOPE + B_ROPE) ** -0.5, accum_out=den[:, u:u + 1]), "exps")
                if 2 <= u < 2 * B_HEADS + 2:
                    w = u - 2
                    act.wait_ge(sem("prob_t"), w + 1)
                    if w >= 2:
                        act.wait_ge(sem("att_o"), w - 1)
                    nc.scalar.activation(probT[w % 2].rearrange("p a b -> p (a b)"), bank[2 + w % 2][:, :],
                                         ACT.Copy).then_inc(sem("prob_t_out"), 1)
                if u >= 3:
                    w = u - 3
                    act.wait_ge(sem("att_o"), w + 1)
                    nc.scalar.activation(oB[:, w // 2, (w % 2) * P:(w % 2 + 1) * P], bank[4 + w % 2][:, 0:P],
                                         ACT.Copy).then_inc(sem("att_out"), 1)
            act.wait_ge(*step("wad_shift"))
            nc.scalar.activation(wadt[sel_lo], wadt[sel_lo], ACT.Tanh).then_inc(step("wad_tanh")[0], 1)
            for h in range(C_HEADS):
                act.wait_ge(sem("ret_o"), h + 1)
                nc.scalar.activation(oC[:, :, h * P:(h + 1) * P], split(bank[4 + h % 2][:, 0:2 * P], 2, P),
                                     ACT.Copy).then_inc(sem("ret_out"), 1)

            def lora(n):
                i, c = LORAS[n // 4], n % 4
                act.wait_ge(sem("lora"), n + 1)
                bias = (V_W0 if i < 2 else V_A0) + 4 * (i % 2) + c
                dst = (sigw if i < 2 else siga)[i % 2][:, :, c, :]
                nc.scalar.activation(dst, split(bank[n % 4][:, :], 4, P), ACT.Sigmoid,
                                     bias=vec[:, bias:bias + 1]).then_inc(sem("lora_out"), 1)

            def decays(b):
                d = batches[b][0]
                e_in, e_ex, e_end, e_inv = (cum[0], cum[1], cum[2], cum[3]) if d == 0 else (cum[3], cum[2], cum[1],
                                                                                            cum[0])
                act.wait_ge(sem("rw_cum"), b + 1)
                total = cum[0].rearrange("p a (c e) -> p (a c) e", e=CH)[:, :, CH - 1]
                A(nc.scalar.activation(pc[b % 2], total, ACT.Exp, scale=-DECAY), "rw_exp")
                A(nc.scalar.activation(e_ex, e_ex, ACT.Exp, scale=-DECAY), "rw_exp")
                A(nc.scalar.activation(e_inv, e_in, ACT.Exp, scale=DECAY), "rw_exp")
                A(nc.scalar.activation(e_in, e_in, ACT.Exp, scale=-DECAY), "rw_exp")
                A(nc.scalar.activation(e_end, e_end, ACT.Exp, scale=-DECAY), "rw_exp")

            for n in range(8):
                lora(n)
            act.wait_ge(sem("variance"), 1)
            st = split(stat[:, 0:24], 3, 8)
            nc.scalar.activation(st[:, 2, :], st[:, 1, :], ACT.Sqrt, bias=eps[:, 0:1], scale=1.0 / C_VD).then_inc(
                sem("norm_root"), 1)
            nc.scalar.activation(nt, gt, ACT.Sigmoid).then_inc(step("ret_gate")[0], 1)
            for tt in range(TT):
                act.wait_ge(sem("kk_sum"), tt + 1)
                nc.scalar.activation(sqa[:, tt, :], bank[tt][:, :], ACT.Sqrt, bias=eps[:, 2:3]).then_inc(
                    sem("kk_root"), 1)
            act.wait_ge(*step("gd_shift"))
            nc.scalar.activation(gsig[0:GD, :], gsig[0:GD, :], ACT.Sigmoid).then_inc(step("gd_sig")[0], 1)
            decays(0)
            for n in range(8, 16):
                lora(n)
            for q in range(LT):
                act.wait_ge(sem("ret_t"), q + 1)
                nc.scalar.activation(oCT[:, :, q * P:(q + 1) * P], split(bank[5 + q][:, :], 4, P), ACT.Copy).then_inc(
                    sem("ret_t_out"), 1)
            for tt in range(TT):
                act.wait_ge(sem("v_t"), tt + 1)
                nc.scalar.activation(vtok[:, tt, :], bank[4 + tt][:, :], ACT.Copy).then_inc(sem("v_t_out"), 1)

            def token_major(b):
                for n in items_of(b):
                    if items[n][2] == "scalar":
                        dst = {"a": atok, "b": btok, "k": ktok}[items[n][1]][b % 2]
                        act.wait_ge(sem("rw_item"), n + 1)
                        nc.scalar.activation(dst, split(bank[n % 2][:, :], 4, P), ACT.Copy).then_inc(
                            sem("rw_item_scalar"), 1)

            token_major(0)
            for b, (d, tt) in enumerate(batches):
                if b + 1 < len(batches):
                    decays(b + 1)
                for hf in range(2):
                    act.wait_ge(sem("rw_w1_mm"), 2 * b + hf + 1)
                    nc.scalar.activation(w1mv[:, hf], bank[6 + hf][:, :], ACT.Copy).then_inc(sem("rw_mv"), 1)
                if b + 1 < len(batches):
                    token_major(b + 1)
                for i, c in enumerate((0, 1) if d == 0 else (1, 0)):
                    rows = slice(CH * c, CH * c + CH)
                    for hf in range(2):
                        act.wait_ge(sem("rw_u_mm"), 4 * b + 2 * i + hf + 1)
                        nc.scalar.activation(w2[rows, hf], bank[4 + hf][rows, 0:2 * P], ACT.Copy).then_inc(
                            sem("rw_u"), 1)

            def root(n, width, groups_, which):
                act.wait_ge(sem("variance"), n)
                st = split(stat[:, 0:3 * groups_], 3, groups_)
                nc.scalar.activation(st[:, 2, :], st[:, 1, :], ACT.Sqrt, bias=eps[:, which:which + 1],
                                     scale=1.0 / width).then_inc(sem("norm_root"), 1)

            root(2, A_HD, 16, 1)
            for q in range(LT):
                act.wait_ge(sem("a_t"), q + 1)
                nc.scalar.activation(oAT[:, :, q * P:(q + 1) * P], split(bank[6 + q][:, :], 4, P), ACT.Copy).then_inc(
                    sem("a_t_out"), 1)

            def ln_moments(n, tt, junk):
                for c in range(4):
                    cc = slice(BANK * c, BANK * (c + 1))
                    act.wait_ge(sem("ln_part"), 4 * n + c + 1)
                    ins = nc.scalar.activation(junk[:, tt, cc], x1[:, tt, cc], ACT.Copy,
                                               accum_out=lnsum[:, 4 * tt + c:4 * tt + c + 1])
                    A(ins, "ln_sum")
                act.wait_ge(sem("ln_mean"), n + 1)
                A(nc.scalar.activation(junk[:, tt], x1[:, tt], ACT.Square, bias=nmean[:, tt:tt + 1],
                                       accum_out=dev[:, tt:tt + 1]))
                nc.scalar.activation(dev[:, tt:tt + 1], dev[:, tt:tt + 1], ACT.Sqrt, bias=eps[:, 0:1],
                                     scale=1.0 / D).then_inc(sem("ln_root"), 1)

            for tt in range(LT):
                ln_moments(tt, tt, ub)
            for n in range(8):
                act.wait_ge(sem("u_t"), n + 1)
                nc.scalar.activation(uT[:, 4 * (n % 4):4 * (n % 4) + 4, (n // 4) * P:(n // 4 + 1) * P],
                                     split(bank[n % 4][:, :], 4, P), ACT.Copy).then_inc(
                    sem("u_t_out"), 1)
            act.wait_ge(*step("logits"))
            A(nc.scalar.activation(lgT[0:N_EXPERTS, :], bank[4][0:N_EXPERTS, 0:LAT], ACT.Copy), "logits_out")
            act.wait_ge(*step("logits_t"))
            nc.scalar.activation(rt(1), split(bank[5][:, 0:32], 2, N_EXPERTS), ACT.Sigmoid).then_inc(step("scored")[0], 1)

            for k in range(KT):
                act.wait_ge(sem("xg_mm"), k + 1)
                nc.scalar.activation(xg[:, k, 0:PAIRS], bank[k % 4][:, :], ACT.Copy).then_inc(sem("xg_out"), 1)
            for s in range(2):
                act.wait_ge(sem("hot_t"), s + 1)
                nc.scalar.activation(hotT[:, 2 * s:2 * s + 2, :], split(bank[6 + s][:, :], 2, LAT), ACT.Copy).then_inc(
                    sem("hot_t_out"), 1)
            act.wait_ge(*step("onehot"))

            def expert(n, first):
                start = act.value_load(starts[0:1, bass.ds(n, 1)], min_val=0, max_val=PAIRS)
                for half in range(2):
                    act.wait_ge(sem("h_mm"), n * 2 + half + 1)
                    nc.scalar.activation(hs[:, half], split(bank[2 * half][:, 0:2 * P], 2, P), ACT.Sigmoid).then_inc(
                        sem("silu"), 1)
                if not first:
                    act.wait_ge(sem("y_out"), n * 8)
                for m in range(8):
                    act.wait_ge(sem("y_mm"), n * 8 + m + 1)
                    nc.scalar.activation(ys[:, 2 * m:2 * m + 2, bass.ds(start, P)],
                                         split(bank[4 + m % 4][:, 0:2 * P], 2, P), ACT.Copy).then_inc(sem("y_out"), 1)

            expert(0, True)
            with act.Fori(1, N_EXPERTS) as e:
                expert(e, False)
            with act.If(act.value_load(starts[0:1, 2 * N_EXPERTS:2 * N_EXPERTS + 1]) > P):
                with act.Fori(N_EXPERTS, 2 * N_EXPERTS) as n:
                    expert(n, False)
            for c in range(4):
                for s in range(ST):
                    act.wait_ge(sem("yt_t"), ST * c + s + 1)
                    nc.scalar.activation(yt[:, s, BANK * c:BANK * (c + 1)], bank[s][:, :], ACT.Copy).then_inc(
                        sem("yt_out"), 1)
            for tt in range(LT):
                ln_moments(2 + tt, tt, lnt)
        @block.vector
        def _(dve):
            V = Counter(dve, "dve_chain")
            nc.vector.memset(vst[:, :], 0.0).then_inc(step("vst_zero")[0], 1)
            V(nc.vector.memset(acc[:, :, :], 0.0), "acc_zero")
            dve.wait_ge(*step("c_sig"))
            nc.vector.tensor_tensor(crow[0:32, :], crow[0:32, :], csig[0:32, :], ALU.mult).then_inc(step("c_silu")[0], 1)
            dve.wait_ge(sem("small_t"), 1)
            V(nc.vector.tensor_copy(cT[:, :, :], bank[0][:, 0:32].rearrange("p (j k) -> p k j", j=2)), "cond")
            for k in range(KT):
                dve.wait_ge(sem(f"mod_in{k % 3}"), 16 * (k // 3 + 1))
                src = mring[k % 3].rearrange("p a b -> p (a b)")[:, PE_BANKS * BANK:]
                for j in range(2):
                    if k == 0:
                        ins = nc.vector.tensor_scalar(macc[:, j], src, cT[:, k, j:j + 1], None, ALU.mult)
                    else:
                        ins = nc.vector.scalar_tensor_tensor(macc[:, j], src, cT[:, k, j:j + 1], macc[:, j], ALU.mult,
                                                             ALU.add)
                V(ins, "mod_used_v")
            dve.wait_ge(sem("small_t"), 2)
            V(nc.vector.tensor_copy(vec[:, :], bank[7][:, 0:N_VEC]), "vecs")
            dve.wait_ge(*step("mod"))
            V(nc.vector.tensor_tensor(modT[:, :, :], split(bank[0][:, 0:64], 32, 2),
                                      vec[:, V_MODB:V_MODB + 32].unsqueeze(2).to_broadcast([P, 32, 2]), ALU.add))
            V(nc.vector.tensor_scalar(modT[:, 16:32, :], modT[:, 16:32, :], 1.0, None, ALU.add), "mod_t")
            dve.wait_ge(sem("xt_out"), KT)
            for k in range(KT):
                lat_k = xT[:, k, CTX:TOK]
                nc.vector.tensor_scalar(lat_k, lat_k, modT[:, 16 + k, 0:1], modT[:, k, 0:1], ALU.mult,
                                        ALU.add).then_inc(sem("xt_mod"), 1)
            dve.wait_ge(sem("accb_in"), 16)

            def gate_rows(k, first):
                for q in range(8):
                    s = q % 4
                    row = acc.rearrange("p a b -> p (a b)")[:, 1024 * q:1024 * (q + 1)]
                    dve.wait_ge(sem(f"gate_in{s}"), k * 32 + 16 * (q // 4 + 1))
                    if not first:
                        dve.wait_ge(sem(f"gate_used{s}"), k * 2 + (q // 4 - 1))
                    c_k = cT[:, k, 0:1] if first else cT[:, bass.ds(k, 1), 0:1].rearrange("p a b -> p (a b)")
                    nc.vector.scalar_tensor_tensor(row, gring[s], c_k, row, ALU.mult, ALU.add).then_inc(sem(f"gate_used{s}"), 1)

            gate_rows(0, True)
            with dve.Fori(1, KT) as k:
                gate_rows(k, False)

            dve.wait_ge(sem("proj_out"), len(tiles))
            for s in range(4):
                dve.wait_ge(sem(f"gate_used{s}"), 2 * KT)
            nc.vector.tensor_tensor(sqq, cq, cq, ALU.mult)
            V(nc.vector.tensor_tensor(sqk, ckv, ckv, ALU.mult), "rms_sq")
            dve.wait_ge(sem("rms_root"), 1)
            V(nc.vector.reciprocal(rsq, rsq))
            V(nc.vector.tensor_tensor(cq, cq, bc(rsq, 4, 1), ALU.mult))
            for c in range(4):
                ins = nc.vector.tensor_scalar(cq[:, c, :], cq[:, c, :], vec[:, V_QN + c:V_QN + c + 1], None, ALU.mult)
            V(ins, "cq_norm")
            dve.wait_ge(sem("rms_root"), 2)
            V(nc.vector.reciprocal(rsk, rsk))
            V(nc.vector.tensor_tensor(ckv, ckv, bc(rsk, 2, 1), ALU.mult))
            for c in range(2):
                ins = nc.vector.tensor_scalar(ckv[:, c, :], ckv[:, c, :], vec[:, V_KVN + c:V_KVN + c + 1], None,
                                              ALU.mult)
            V(ins, "ckv_norm")
            dve.wait_ge(*step("kr_rot"))
            V(nc.vector.tensor_tensor(rtmpk, bank[2][:, 0:LAT], sinT, ALU.mult))
            V(nc.vector.tensor_tensor(kr[:, CTX:TOK], kr[:, CTX:TOK], cosT, ALU.mult))
            V(nc.vector.tensor_tensor(kr[:, CTX:TOK], kr[:, CTX:TOK], rtmpk, ALU.add), "kr_ready")
            dve.wait_ge(*step("qrz_zero"))
            for p in range(4):
                dve.wait_ge(sem("q_rot"), p + 1)
                V(nc.vector.tensor_tensor(rtmpk, bank[6 + p % 2][:, 0:LAT], sinT, ALU.mult), "q_rot_read")
                V(nc.vector.tensor_tensor(qr[:, p, :], qr[:, p, :], cosT, ALU.mult))
                nc.vector.tensor_tensor(qrz[sel_lo, 2 * p, :], qr[sel_lo, p, :], rtmpk[sel_lo, :], ALU.add)
                V(nc.vector.tensor_tensor(qrz[sel_hi, 2 * p + 1, :], qr[sel_hi, p, :], rtmpk[sel_hi, :], ALU.add),
                  "qr_ready")
            nc.vector.tensor_scalar(mu5, vec[:, V_MU:V_MU + 14], 0.5, None, ALU.mult)
            V(nc.vector.tensor_scalar(omu, vec[:, V_MU:V_MU + 14], -1.0, 1.0, ALU.mult, ALU.add))

            def shift(dst, padded, row, parts=P, signal=None):
                prev, cur, nxt = (padded[0:parts, :, i:i + LAT].rearrange("p s (u e) -> p s u e", u=2)
                                  for i in range(3))
                V(nc.vector.tensor_tensor(dst, prev, nxt, ALU.add))
                V(nc.vector.tensor_scalar(dst, dst, mu5[0:parts, row:row + 1], None, ALU.mult))
                V(nc.vector.scalar_tensor_tensor(dst, cur, omu[0:parts, row:row + 1], dst, ALU.mult, ALU.add), signal)

            def tiles4(x, c):
                return x[:, :, c, :].rearrange("p (s u) e -> p s u e", u=2)

            dve.wait_ge(sem("parked"), 16)
            for c in range(4):
                shift(tiles4(ks, c), kp[:, c], 4 + c)
            rtv = rtmp2.rearrange("p (a b) -> p a b", a=2)
            cos2, sin2 = bc(cosT, 2, 1), bc(sinT, 2, 1)
            dve.wait_ge(*step("rqz_zero"))
            dve.wait_ge(sem("ret_rot"), 1)
            V(nc.vector.tensor_tensor(rtv, split(bank[6][:, :], 2, LAT), sin2, ALU.mult))
            V(nc.vector.tensor_tensor(rq, rq, cos2, ALU.mult))
            nc.vector.tensor_tensor(rqz[sel_lo, 0:4:2, :], rq[sel_lo], rtv[sel_lo], ALU.add)
            V(nc.vector.tensor_tensor(rqz[sel_hi, 1:4:2, :], rq[sel_hi], rtv[sel_hi], ALU.add))
            dve.wait_ge(sem("ret_rot"), 2)
            V(nc.vector.tensor_tensor(rtv, split(bank[7][:, :], 2, LAT), sin2, ALU.mult))
            V(nc.vector.tensor_tensor(rk[:, :, CTX:TOK], rk[:, :, CTX:TOK], cos2, ALU.mult))
            V(nc.vector.tensor_tensor(rk[:, :, CTX:TOK], rk[:, :, CTX:TOK], rtv, ALU.add), "ret_qk")
            for c in range(4):
                shift(tiles4(vs, c), vp[:, c], 8 + c, signal="v_shift")
            for c in range(4):
                shift(tiles4(rs, c), split(rp[:, c, :], 1, LAT + 2), c)
            for c in range(4):
                nc.vector.tensor_scalar(kkn[:, :, c, :], ks[:, :, c, :], vec[:, V_KK + c:V_KK + c + 1], None, ALU.mult)
                last = nc.vector.tensor_scalar(rrk[:, :, c, :], rs[:, :, c, :], vec[:, V_RK + c:V_RK + c + 1], None,
                                               ALU.mult)
            V(last, "shifted")
            for u in range(2 * B_HEADS + 1):
                if u < 2 * B_HEADS:
                    dve.wait_ge(sem("scores"), u + 1)
                    V(nc.vector.tensor_reduce(mx[:, u:u + 1], score_bank[u % 3][:, :], AX.X, ALU.max))
                    V(nc.vector.tensor_scalar(mx[:, u:u + 1], mx[:, u:u + 1], -((B_NOPE + B_ROPE) ** -0.5), None,
                                              ALU.mult), "row_max")
                if u >= 1:
                    w = u - 1
                    dve.wait_ge(sem("exps"), w + 1)
                    V(nc.vector.reciprocal(rden[:, w:w + 1], den[:, w:w + 1]))
                    V(nc.vector.tensor_scalar(prob[w % 3], prob[w % 3], rden[:, w:w + 1], None, ALU.mult), "probs")
            shift(wadt.rearrange("p s (u e) -> p s u e", u=2), wp, 12, signal="wad_shift")
            dve.wait_ge(sem("decay_in"), 16)
            for h in range(C_HEADS):
                if h >= 2:
                    dve.wait_ge(sem("ret_o"), h - 1)
                for j in range(2):
                    dve.wait_ge(sem("ret_s"), 2 * h + j + 1)
                    nc.vector.tensor_tensor(att[h % 2][:, 2 * j:2 * j + 2, :],
                                            split(bank[(2 * h + j) % 4][:, :], 2, LAT),
                                            dTall[:, h * TT + 2 * j:h * TT + 2 * j + 2, :], ALU.mult).then_inc(
                                                sem("ret_att"), 1)

            def norm(x, scratch, groups_, width, st, root_wait, signal=None):
                V(nc.vector.tensor_reduce(st[:, 0, :], x, AX.X, ALU.add))
                V(nc.vector.tensor_scalar(st[:, 0, :], st[:, 0, :], -1.0 / width, None, ALU.mult))
                V(nc.vector.tensor_tensor(x, x, bc(st[:, 0, :], width, 2), ALU.add))
                V(nc.vector.tensor_tensor(scratch, x, x, ALU.mult))
                V(nc.vector.tensor_reduce(st[:, 1, :], scratch, AX.X, ALU.add), "variance")
                root_wait()
                V(nc.vector.reciprocal(st[:, 2, :], st[:, 2, :]))
                V(nc.vector.tensor_tensor(x, x, bc(st[:, 2, :], width, 2), ALU.mult), signal)

            dve.wait_ge(sem("ret_att"), 2 * C_HEADS)
            shift(split(gsig[0:GD, :], 1, LAT).rearrange("p s (u e) -> p s u e", u=2), split(gp[:, :], 1, LAT + 2), 13,
                  parts=GD, signal="gd_shift")
            V(nc.vector.tensor_scalar(nka, vec[:, V_KA:V_KA + 4], -1.0, 1.0, ALU.mult, ALU.add))
            dve.wait_ge(sem("ret_o"), C_HEADS)
            flat = kkn.rearrange("p a b c -> p a (b c)")
            V(nc.vector.tensor_tensor(sqa, flat, flat, ALU.mult), "kk_sq")
            ka = vec[:, V_KA:V_KA + 4]

            dve.wait_ge(sem("ret_out"), C_HEADS)
            norm(oC.rearrange("p a (h e) -> p (a h) e", e=C_VD), nt.rearrange("p a (h e) -> p (a h) e", e=C_VD), 8,
                 C_VD, split(stat[:, 0:24], 3, 8), lambda: dve.wait_ge(sem("norm_root"), 1), "ret_normed")
            def normalise():
                for tt in range(TT):
                    dve.wait_ge(sem("kk_root"), tt + 1)
                    V(nc.vector.reciprocal(sqa[:, tt, :], sqa[:, tt, :]))
                    V(nc.vector.tensor_tensor(flat[:, tt, :], flat[:, tt, :], sqa[:, tt, :], ALU.mult),
                      "rw_prep" if tt == TT - 1 else None)

            dve.wait_ge(*step("rw_zero"))

            def halves(dst, x, y):
                nc.vector.tensor_tensor(dst[sel_lo, 0:8:2, :], x[sel_lo], y[sel_lo], ALU.mult)
                V(nc.vector.tensor_tensor(dst[sel_hi, 1:8:2, :], x[sel_hi], y[sel_hi], ALU.mult))


            def features(b, part):
                d, tt = batches[b]
                q = tt - 2
                sig = sigw[d][:, tt]
                e_in, e_ex, e_end, e_inv = (cum[0], cum[1], cum[2], cum[3]) if d == 0 else (cum[3], cum[2], cum[1],
                                                                                            cum[0])
                if part == 0:
                    V(nc.vector.tensor_tensor_scan(cum[0].rearrange("p a b -> p (a b)"), reset,
                                                   sig.rearrange("p a b -> p (a b)"), 0.0, ALU.mult, ALU.add))
                    total = cum[0].rearrange("p a (c e) -> p (a c) e", e=CH)[:, :, CH - 1:CH].to_broadcast([P, 8, CH])
                    nc.vector.tensor_tensor(cum[1], cum[0], sig, ALU.subtract)
                    c0v, c2v = (x.rearrange("p a (c e) -> p (a c) e", e=CH) for x in (cum[0], cum[2]))
                    ins = nc.vector.tensor_tensor(c2v, total, c0v, ALU.subtract)
                    if d == 1:
                        V(ins)
                        ins = nc.vector.tensor_tensor(cum[3], cum[2], sig, ALU.add)
                    V(ins, "rw_cum")
                elif part == 1:
                    nc.vector.tensor_tensor(bb, kkn[:, tt], siga[d][:, tt], ALU.mult)
                    V(nc.vector.tensor_tensor(kd, siga[d][:, tt], bc(ka, P, 2), ALU.mult))
                elif part == 2:
                    V(nc.vector.tensor_tensor(kd, kd, bc(nka, P, 2), ALU.add))
                    V(nc.vector.tensor_tensor(kd, kd, ks[:, tt], ALU.mult))
                elif part == 3:
                    dve.wait_ge(sem("rw_exp"), 5 * (b + 1))
                    V(nc.vector.scalar_tensor_tensor(arp[:, :, 0, :], kkn[:, tt], -1.0, e_ex, ALU.mult, ALU.mult))
                    halves(bz, bb, e_inv)
                    halves(kz, kd, e_inv)
                else:
                    if tt >= 2:
                        nc.vector.tensor_tensor(cum[1 + d], rrk[:, q], kd, ALU.mult)
                        V(nc.vector.tensor_tensor(arp[:, :, 1, :], rs[:, q], e_in, ALU.mult))
                        nc.vector.tensor_copy(rr[b % 2], arp[:, :, 1, :])
                    nc.vector.tensor_tensor(bb, bb, e_end, ALU.mult)
                    V(nc.vector.tensor_tensor(kd, kd, e_end, ALU.mult), "rw_feat")

            def item(n):
                b, kind, engine, _ = items[n]
                if engine != "vector":
                    return
                d, tt = batches[b]
                dve.wait_ge(sem("rw_item"), n + 1)
                ps = split(bank[n % 2][:, :], 4, P)
                if kind == "bonus":
                    bo = bonus[:, 8 * (tt - 2):8 * (tt - 1)]
                    if d == 0:
                        ins = nc.vector.tensor_copy(bo, bank[n % 2][:, 0:8])
                    else:
                        ins = nc.vector.tensor_tensor(bo, bo, bank[n % 2][:, 0:8], ALU.add)
                elif kind in ("low0", "low1"):
                    hf = int(kind[3])
                    lo_m, up_m = (lower, upper) if d == 0 else (upper, lower)
                    dve.wait_ge(sem("rw_ident"), 4 * b + 3 + hf)

                    def pairs(x, which):
                        return x.rearrange("p (g two) -> p g two", two=2)[:, :, which]

                    x_, g_ = blocks(xm[:, hf], 1, d), blocks(gm[:, hf], 1, 1 - d)
                    x_, g_ = (v.rearrange("p j g n -> p j (g n)") for v in (x_, g_))
                    l_ = ps.rearrange("p j (g two) -> p j g two", two=2)[:, :, :, d]
                    lt_ = um[b % 2][:, hf, :, 0].rearrange("p j (g two) -> p j g two", two=2)[:, :, :, 1 - d]
                    nc.vector.tensor_tensor(x_, l_, bc(pairs(lo_m[:, 0], d), 4, 1), ALU.mult)
                    V(nc.vector.tensor_tensor(g_, lt_, bc(pairs(up_m[:, 0], 1 - d), 4, 1), ALU.mult))
                    V(nc.vector.tensor_tensor(x_, x_, bc(pairs(ident, d), 4, 1), ALU.add))
                    ins = nc.vector.tensor_tensor(g_, g_, bc(pairs(ident, 1 - d), 4, 1), ALU.add)
                elif tt >= 2:
                    ins = nc.vector.tensor_tensor(um[b % 2][:, kind // 4, kind % 4], ps, masks[d], ALU.mult)
                else:
                    ins = nc.vector.tensor_tensor(um[b % 2][:, kind // 4, kind % 4, 0:4:2], ps[:, 0:4:2],
                                                  masks[d][:, 0:4:2], ALU.mult)
                V(ins, "rw_item_vector")

            dve.wait_ge(sem("lora_out"), 8)
            features(0, 0)
            normalise()
            for part in range(1, 5):
                features(0, part)
            dve.wait_ge(sem("lora_out"), 16)
            for n in items_of(0):
                item(n)
            nlat = 0
            for b, (d, tt) in enumerate(batches):
                latent = tt >= 2
                q = tt - 2
                lo_m = lower if d == 0 else upper
                for lv in range(LEVELS):
                    n = 2 * (LEVELS * b + lv)
                    for hf in range(2):
                        dve.wait_ge(sem("rw_lx"), n + hf + 1)
                        V(nc.vector.tensor_tensor(zm[:, hf], split(bank[4 + hf][:, :], 4, P),
                                                  bc(lo_m[:, lv + 1], 4, 1), ALU.mult), "rw_z")
                    if b + 1 < len(batches):
                        features(b + 1, lv)
                    for hf in range(2):
                        n_x, nx = 2 << lv, 2 * ((LEVELS - 1) * b + lv)
                        if lv < LEVELS - 1:
                            dve.wait_ge(sem("rw_xz"), nx + hf + 1)
                            x_ = blocks(xm[:, hf], n_x, d)
                            V(nc.vector.tensor_tensor(x_, x_, blocks(split(bank[hf][:, :], 4, P), n_x, d), ALU.add),
                              "rw_x")
                        dve.wait_ge(sem("rw_gz"), n + hf + 1)
                        g_ = blocks(gm[:, hf], n_x, 1 - d)
                        V(nc.vector.tensor_tensor(g_, g_, blocks(split(bank[2 + hf][:, :], 4, P), n_x, 1 - d), ALU.add),
                          "rw_g")

                def next_items(part):
                    if b + 1 < len(batches):
                        for n in items_of(b + 1, part):
                            item(n)

                next_items(0)
                next_items(1)
                pv = pc[b % 2].rearrange("p (a c) -> p a c", c=2)
                for i, c in enumerate((0, 1) if d == 0 else (1, 0)):
                    for hf in range(2):
                        V(nc.vector.tensor_tensor(stmp[hf], sst[i][:, 2 * hf:2 * hf + 2],
                                                  bc(pv[:, 2 * hf:2 * hf + 2, c], P, 2), ALU.mult))
                    next_items(2 + 2 * i)
                    for hf in range(2):
                        dve.wait_ge(sem("rw_s_mm"), 4 * b + 2 * i + hf + 1)
                        new, ps = sst[1 - i][:, 2 * hf:2 * hf + 2], split(bank[2 + hf][:, 0:2 * P], 2, P)
                        nc.vector.tensor_tensor(new[sel_lo, :, 0:64], ps[sel_lo, :, 0:64], stmp[hf][sel_lo, :, 0:64],
                                                ALU.add)
                        V(nc.vector.tensor_tensor(new[sel_hi, :, 64:P], ps[sel_hi, :, 64:P],
                                                  stmp[hf][sel_hi, :, 64:P], ALU.add), "rw_s")
                    if i == 0:
                        next_items(3)
                if latent:
                    for hf in range(2):
                        dve.wait_ge(sem("rw_y_mm"), 2 * nlat + hf + 1)
                        ya = yacc[:, q, 2 * P * hf:2 * P * (hf + 1)]
                        if d == 0:
                            V(nc.vector.tensor_copy(ya, bank[6 + hf][:, 0:2 * P]), "rw_y")
                        else:
                            V(nc.vector.tensor_tensor(ya, ya, bank[6 + hf][:, 0:2 * P], ALU.add), "rw_y")
                    nlat += 1
                if b == 3:
                    V(nc.vector.memset(sst[0], 0.0), "rw_s_reset")
                next_items(5)
            norm(yacc.rearrange("p a (h e) -> p (a h) e", e=A_HD), na.rearrange("p a (h e) -> p (a h) e", e=A_HD), 16,
                 A_HD, split(stat[:, 0:48], 3, 16), lambda: dve.wait_ge(sem("norm_root"), 2))
            dve.wait_ge(sem("gna_in"), 32)
            V(nc.vector.tensor_tensor(yacc, yacc, bc(gna[:, 0, :], LT, 1), ALU.mult))
            V(nc.vector.tensor_tensor(yacc, yacc, bc(gna[:, 1, :], LT, 1), ALU.add))
            for q in range(LT):
                V(nc.vector.tensor_tensor(split(na[:, q, :], 8, A_HD), split(vtok[:, 2 + q, :], 8, A_HD),
                                          bc(bonus[:, 8 * q:8 * q + 8], A_HD, 2), ALU.mult))
            V(nc.vector.tensor_tensor(yacc, yacc, na, ALU.add))
            dve.wait_ge(sem("g_mm"), 2)
            for q in range(LT):
                V(nc.vector.tensor_tensor(yacc[:, q, :], yacc[:, q, :], bank[6 + q][:, :], ALU.mult), "a_done")
            dve.wait_ge(sem("rows_in"), 16)
            dve.wait_ge(sem("ln_in"), 32)
            V(nc.vector.tensor_scalar(sc2r, sc2r, 1.0, None, ALU.add))
            V(nc.vector.tensor_tensor(ub[:, 0], ln[:, 1], sc2r, ALU.mult))
            nc.vector.tensor_tensor(sh2r, sh2r, ub[:, 0], ALU.add)
            V(nc.vector.tensor_tensor(sc2r, sc2r, ln[:, 0], ALU.mult))

            def normed(tt, dst, gain, bias, signals):
                for i, signal in enumerate(signals):
                    cc = slice(D // 2 * i, D // 2 * (i + 1))
                    V(nc.vector.scalar_tensor_tensor(dst[:, cc], x1[:, tt, cc], nmean[:, tt:tt + 1], gain[:, cc],
                                                     ALU.add, ALU.mult))
                    V(nc.vector.scalar_tensor_tensor(dst[:, cc], dst[:, cc], dev[:, tt:tt + 1], bias[:, cc],
                                                     ALU.mult, ALU.add), signal)

            def moments(n, tt):
                dve.wait_ge(sem("ln_sum"), 4 * n + 4)
                V(nc.vector.tensor_reduce(nmean[:, tt:tt + 1], lnsum[:, 4 * tt:4 * tt + 4], AX.X, ALU.add))
                V(nc.vector.tensor_scalar(nmean[:, tt:tt + 1], nmean[:, tt:tt + 1], -1.0 / D, None, ALU.mult),
                  "ln_mean")

            def deviation(n, tt):
                dve.wait_ge(sem("ln_root"), n + 1)
                V(nc.vector.reciprocal(dev[:, tt:tt + 1], dev[:, tt:tt + 1]))

            dve.wait_ge(sem("xl_in"), 16)
            for tt in range(LT):
                for c in range(4):
                    cc = slice(BANK * c, BANK * (c + 1))
                    dve.wait_ge(sem("mix_mm"), 4 * tt + c + 1)
                    V(nc.vector.tensor_tensor(ub[:, tt, cc], mix_bank(tt, c)[:, :], g1r[:, cc], ALU.mult), "mix_out")
                    V(nc.vector.scalar_tensor_tensor(x1[:, tt, cc], x1[:, tt, cc], ALPHA, ub[:, tt, cc], ALU.mult,
                                                     ALU.add), "ln_part")
                    if tt and c == 1:
                        deviation(0, 0)
                        normed(0, ub[:, 0], sc2r, sh2r, (None, "u_ready0"))
                if tt == 0:
                    moments(0, 0)
            moments(1, 1)
            deviation(1, 1)
            normed(1, ub[:, 1], sc2r, sh2r, ("u_half", "u_ready"))
            for tt in range(LT):
                normed(tt, x1[:, tt], ln[:, 0], ln[:, 1], (None, "ln1_done" if tt else None))
            s_, sb, t1, t2 = rt(1), rt(2), rt(3), rt(4)
            oh1, oh2 = rt(5), rt(6)
            iota16 = bc(const("iota16"), 2, 1)
            iota4 = bc(const("iota4"), 2, 1)
            dve.wait_ge(*step("scored"))
            dve.wait_ge(sem("router_in"), 32)
            V(nc.vector.tensor_tensor(sb, s_, bc(rbias, 2, 1), ALU.add))
            v4 = sb.rearrange("p t (g e) -> p t g e", e=4)
            m_a, n_a, m_b, n_b, gs, ge = (rg(i) for i in range(6))
            nc.vector.tensor_tensor(m_a, v4[:, :, :, 0], v4[:, :, :, 1], ALU.max)
            nc.vector.tensor_tensor(n_a, v4[:, :, :, 0], v4[:, :, :, 1], ALU.min)
            nc.vector.tensor_tensor(m_b, v4[:, :, :, 2], v4[:, :, :, 3], ALU.max)
            V(nc.vector.tensor_tensor(n_b, v4[:, :, :, 2], v4[:, :, :, 3], ALU.min))
            V(nc.vector.tensor_tensor(n_a, n_a, n_b, ALU.max))
            V(nc.vector.tensor_tensor(n_b, m_a, m_b, ALU.min))
            V(nc.vector.tensor_tensor(n_a, n_a, n_b, ALU.max))
            V(nc.vector.tensor_tensor(m_a, m_a, m_b, ALU.max))
            V(nc.vector.tensor_tensor(gs, m_a, n_a, ALU.add))
            one = small[:, 16:48]

            def first_best(x, hot, iota, width, tmp_):
                best, at_ = one[:, 0:2], one[:, 2:4]
                V(nc.vector.tensor_reduce(best, x, AX.X, ALU.max))
                V(nc.vector.tensor_tensor(hot, x, bc(best, width, 2), ALU.is_lt))
                V(nc.vector.tensor_scalar(hot, hot, 100.0, None, ALU.mult))
                V(nc.vector.tensor_tensor(tmp_, hot, iota, ALU.add))
                V(nc.vector.tensor_reduce(at_, tmp_, AX.X, ALU.min))
                V(nc.vector.tensor_tensor(hot, iota, bc(at_, width, 2), ALU.is_equal))

            first_best(gs, ge, iota4, 4, m_b)
            V(nc.vector.tensor_scalar(n_b, ge, 1e30, -1e30, ALU.mult, ALU.add))
            for tt in range(2):
                V(nc.vector.tensor_tensor(split(t1[:, tt], 4, 4), v4[:, tt], bc(ge[:, tt], 4, 2), ALU.mult))
                V(nc.vector.tensor_tensor(split(t1[:, tt], 4, 4), split(t1[:, tt], 4, 4), bc(n_b[:, tt], 4, 2),
                                          ALU.add))
            first_best(t1, oh1, iota16, 16, t2)
            V(nc.vector.tensor_scalar(t2, oh1, -1e30, None, ALU.mult))
            V(nc.vector.tensor_tensor(t1, t1, t2, ALU.add))
            first_best(t1, oh2, iota16, 16, t2)
            V(nc.vector.tensor_tensor(t1, oh1, oh2, ALU.add), "selected")
            for i, oh in enumerate((oh1, oh2)):
                V(nc.vector.tensor_tensor(t2, oh, s_, ALU.mult))
                V(nc.vector.tensor_reduce(gate[i], t2, AX.X, ALU.add))
            V(nc.vector.tensor_tensor(one[:, 0:2], gate[0], gate[1], ALU.add))
            V(nc.vector.reciprocal(one[:, 0:2], one[:, 0:2]))
            for i in range(2):
                V(nc.vector.scalar_tensor_tensor(gate[i], gate[i], ROUTE_SCALE, one[:, 0:2], ALU.mult, ALU.mult))
            dve.wait_ge(*step("ranks"))
            nc.vector.tensor_copy(cnt, bank[6][:, 32:48])
            V(nc.vector.tensor_copy(excl, split(bank[6][:, 0:32], 2, N_EXPERTS)))
            V(nc.vector.tensor_tensor_scan(base, ones[:, 0:N_EXPERTS], cnt, 0.0, ALU.mult, ALU.add))
            V(nc.vector.tensor_tensor(off, base, cnt, ALU.subtract))
            V(nc.vector.tensor_tensor(excl, excl, bc(off, 2, 1), ALU.add))
            for i, oh in enumerate((oh1, oh2)):
                V(nc.vector.tensor_tensor(t2, oh, excl, ALU.mult))
                V(nc.vector.tensor_reduce(pair_at[i], t2, AX.X, ALU.add))
            V(nc.vector.tensor_scalar(late, cnt, float(P), None, ALU.is_gt))
            V(nc.vector.tensor_scalar(base, base, float(-P - PAIRS), None, ALU.add))
            V(nc.vector.tensor_tensor(late, late, base, ALU.mult))
            V(nc.vector.tensor_scalar(late, late, float(PAIRS), None, ALU.add))
            V(nc.vector.tensor_reduce(most, cnt, AX.X, ALU.max))
            nc.vector.tensor_copy(starts[:, 0:N_EXPERTS], off[0:1, :])
            nc.vector.tensor_copy(starts[:, N_EXPERTS:2 * N_EXPERTS], late[0:1, :])
            V(nc.vector.tensor_copy(starts[:, 2 * N_EXPERTS:], most[0:1, :]))
            for tt in range(LT):
                at_ = [pair_at[i][:, tt:tt + 1] for i in range(2)]
                V(nc.vector.tensor_scalar(hot[:, tt], iota, at_[0], None, ALU.is_equal))
                V(nc.vector.scalar_tensor_tensor(hot[:, tt], iota, at_[1], hot[:, tt], ALU.is_equal, ALU.add),
                  "onehot" if tt else None)
            for tt in range(LT):
                for i, dst in enumerate((hotg[:, tt], hot2)):
                    V(nc.vector.tensor_scalar(dst, iota, pair_at[i][:, tt:tt + 1], gate[i][:, tt:tt + 1],
                                              ALU.is_equal, ALU.mult))
                V(nc.vector.tensor_tensor(hotg[:, tt], hotg[:, tt], hot2, ALU.add), "hot_gates" if tt else None)

            def expert(n):
                for half in range(2):
                    dve.wait_ge(sem("h_mm"), n * 2 + half + 1)
                    dve.wait_ge(sem("silu"), n * 2 + half + 1)
                    nc.vector.tensor_tensor(hs[:, half], hs[:, half], split(bank[2 * half][:, 0:2 * P], 2, P),
                                            ALU.mult).then_inc(sem("h_1"), 1)
                    dve.wait_ge(sem("h_1"), n * 2 + half + 1)
                    nc.vector.tensor_tensor(hT[:, 2 * half:2 * half + 2], hs[:, half],
                                            split(bank[2 * half + 1][:, 0:2 * P], 2, P), ALU.mult).then_inc(
                                                sem("h_out"), 1)

            dve.wait_ge(sem("hot_t"), 2)
            with dve.Fori(0, N_EXPERTS) as e:
                expert(e)
            with dve.If(dve.value_load(starts[0:1, 2 * N_EXPERTS:2 * N_EXPERTS + 1]) > P):
                with dve.Fori(N_EXPERTS, 2 * N_EXPERTS) as n:
                    expert(n)
            dve.wait_ge(sem("ln2_in"), 32)
            for tt in range(LT):
                for c in range(4):
                    cc = slice(BANK * c, BANK * (c + 1))
                    dve.wait_ge(sem("ffn"), 4 * tt + c + 1)
                    dst = lnt[:, tt, cc]
                    V(nc.vector.tensor_tensor(dst, bank[4 + c][:, :], g2r[:, cc], ALU.mult), "ffn_out")
                    V(nc.vector.scalar_tensor_tensor(x1[:, tt, cc], x1[:, tt, cc], ALPHA, dst, ALU.mult, ALU.add),
                      "ln_part")
                moments(2 + tt, tt)
                deviation(2 + tt, tt)
                normed(tt, x1[:, tt], ln2[:, 0], ln2[:, 1], ("done", "done"))
        @block.tensor
        def _(pe):
            pe.wait_ge(sem("const_in"), 16)
            pe.wait_ge(*step("c_silu"))
            nc.tensor.transpose(bank[0][:, 0:32], crow[0:32, :], ident[0:32, 0:32]).then_inc(sem("small_t"), 1)
            for k in range(KT):
                if k >= 4:
                    pe.wait_ge(sem("xt_out"), k - 3)
                for tt in range(TT):
                    if k == 0:
                        pe.wait_ge(sem(f"x_in{tt}"), 16)
                    last = nc.tensor.transpose(bank[2 + k % 4][:, tt * P:(tt + 1) * P],
                                               xtok[:, tt, k * P:(k + 1) * P], ident)
                last.then_inc(sem("xt_raw"), 1)
            pe.wait_ge(*step("cond"))
            pe.wait_ge(sem("xt_out"), KT)
            for k in range(KT):
                pe.wait_ge(sem(f"mod_in{k % 3}"), 16 * (k // 3 + 1))
                for b in range(PE_BANKS):
                    last = nc.tensor.matmul(bank[b][0:2, :], cT[:, k, :], mring[k % 3][:, b, :], start=(k == 0),
                                            stop=(k == KT - 1))
                last.then_inc(sem("mod_used"), 1)
            pe.wait_ge(sem("vec_in"), 160)
            nc.tensor.transpose(bank[7][:, 0:N_VEC], vst[0:N_VEC, :], ident[0:N_VEC, 0:N_VEC]).then_inc(
                sem("small_t"), 1)
            pe.wait_ge(sem("mod_row"), PE_BANKS)
            pe.wait_ge(sem("mod_used_v"), KT)
            for c in range(4 * PE_BANKS, 32):
                for j in range(2):
                    at_ = (c - 4 * PE_BANKS) * P
                    nc.tensor.matmul(bank[0][:, 2 * c + j:2 * c + j + 1], macc[:, j, at_:at_ + P], ones[:, 0:1],
                                     start=True, stop=True, skip_group_check=True)
            for c in range(4 * PE_BANKS):
                last = nc.tensor.transpose(bank[0][:, 2 * c:2 * c + 2], mrow[:, c // 4, (c % 4) * P:(c % 4 + 1) * P],
                                           ident[0:2, 0:2])
            last.then_inc(step("mod")[0], 1)
            for n, (g, stationary, j, w, (t0, t1), dst) in enumerate(tiles):
                if n == 0 or g != tiles[n - 1][0]:
                    pe.wait_ge(sem(f"win_in{g % 3}"), 16 * (g // 3 + 1))
                    if groups[g][0] == COL_KR:
                        pe.wait_ge(sem("kr_in"), 16)
                if n >= 8:
                    pe.wait_ge(sem("proj_out"), n - 7)
                for k in range(KT):
                    if n == 0:
                        pe.wait_ge(sem("xt_mod"), k + 1)
                        pe.wait_ge(sem("xt_mod_ctx"), k + 1)
                    if stationary:
                        last = nc.tensor.matmul(bank[n % 8][0:w, 0:t1 - t0], wring[g % 3][:, k, j:j + w],
                                                xT[:, k, t0:t1], start=(k == 0), stop=(k == KT - 1))
                    else:
                        last = nc.tensor.matmul(bank[n % 8][:, 0:256], xT[:, k, t0:t1], wring[g % 3][:, k, :],
                                                start=(k == 0), stop=(k == KT - 1))
                last.then_inc(sem("proj"), 1)
            for s in range(4):
                pe.wait_ge(sem(f"gate_used{s}"), 2 * KT)
            for q in range(16):
                pe.wait_ge(sem("proj_out"), len(tiles))
                if q >= 2:
                    pe.wait_ge(sem("rows_out"), q - 1)
                nc.tensor.matmul(bank[q % 2][:, :], ones, acc.rearrange("p a b -> p (a b)")[:, BANK * q:BANK * (q + 1)],
                                 start=True, stop=True).then_inc(sem("rows"), 1)
            pe.wait_ge(sem("const_in"), 32)
            pe.wait_ge(*step("rms_sq"))
            pe.wait_ge(sem("rows_out"), 16)
            for c in range(4):
                last = nc.tensor.matmul(bank[0][:, 0:LAT], ones, sqq[:, c, :], start=(c == 0), stop=(c == 3))
            last.then_inc(sem("rms_sum"), 1)
            for c in range(2):
                last = nc.tensor.matmul(bank[1][:, :], ones, sqk[:, c, :], start=(c == 0), stop=(c == 1))
            last.then_inc(sem("rms_sum"), 1)
            nc.tensor.matmul(bank[2][:, 0:LAT], rot, kr[:, CTX:TOK], start=True, stop=True).then_inc(step("kr_rot")[0], 1)
            pe.wait_ge(sem("uq_in"), 16)
            pe.wait_ge(*step("cq_norm"))
            wuq_h = wuq.rearrange("p k (h e) -> p k h e", e=B_NOPE + B_ROPE)
            for p in range(4):
                if p >= 2:
                    pe.wait_ge(sem("qr_raw"), p - 1)
                for c in range(4):
                    for o in range(2):
                        last = nc.tensor.matmul(bank[4 + p % 2][64 * o:64 * o + 64, 0:LAT],
                                                wuq_h[:, c, 2 * p + o, B_NOPE:], cq[:, c, :], start=(c == 0),
                                                stop=(c == 3), skip_group_check=True)
                last.then_inc(sem("qr_mm"), 1)
                if p >= 1:
                    w = p - 1
                    pe.wait_ge(sem("qr_raw"), w + 1)
                    if w >= 2:
                        pe.wait_ge(sem("q_rot_read"), w - 1)
                    nc.tensor.matmul(bank[6 + w % 2][:, 0:LAT], rot, qr[:, w, :], start=True, stop=True).then_inc(
                        sem("q_rot"), 1)
            pe.wait_ge(sem("qr_raw"), 4)
            pe.wait_ge(sem("q_rot_read"), 2)
            nc.tensor.matmul(bank[7][:, 0:LAT], rot, qr[:, 3, :], start=True, stop=True).then_inc(sem("q_rot"), 1)
            pe.wait_ge(sem("rms_root"), 2)
            pe.wait_ge(*step("kr_ready"))
            for h in range(B_HEADS):
                if h >= 4:
                    pe.wait_ge(sem("qn_out"), h - 3)
                for c in range(4):
                    last = nc.tensor.matmul(bank[h % 4][:, 0:LAT], wuq_h[:, c, h, 0:B_NOPE], cq[:, c, :],
                                            start=(c == 0), stop=(c == 3))
                last.then_inc(sem("qn_mm"), 1)
            pe.wait_ge(sem("ukv_in"), 16)
            pe.wait_ge(*step("ckv_norm"))
            wukv_h = wukv.rearrange("p k (h e) -> p k h e", e=B_NOPE + B_VD)
            for h in range(B_HEADS):
                pe.wait_ge(sem("qn_out"), min(8, h + 5))
                if h >= 4:
                    pe.wait_ge(sem("kn_out"), h - 3)
                for c in range(2):
                    last = nc.tensor.matmul(bank[h % 4][:, :], wukv_h[:, c, h, 0:B_NOPE], ckv[:, c, :],
                                            start=(c == 0), stop=(c == 1))
                last.then_inc(sem("kn_mm"), 1)
            pe.wait_ge(sem("qr_ready"), 4)
            for c in range(2):
                last = nc.tensor.matmul(bank[6][:, c * LAT:(c + 1) * LAT], rot, rq[:, c, :], start=True, stop=True,
                                        skip_group_check=True)
            last.then_inc(sem("ret_rot"), 1)
            for c in range(2):
                last = nc.tensor.matmul(bank[7][:, c * LAT:(c + 1) * LAT], rot, rk[:, c, CTX:TOK], start=True,
                                        stop=True, skip_group_check=True)
            last.then_inc(sem("ret_rot"), 1)
            for n in range(2 * TT):
                if n == 2:
                    pe.wait_ge(*step("ret_qk"))
                if n >= 4:
                    pe.wait_ge(sem("v_out"), n - 3)
                tt, half = n // 2, n % 2
                for c in range(2):
                    last = nc.tensor.matmul(bank[4 + n % 4][:, :], ckv[:, c, tt * P:(tt + 1) * P],
                                            wukv_h[:, c, 4 * half:4 * half + 4, B_NOPE:], start=(c == 0),
                                            stop=(c == 1))
                last.then_inc(sem("v_mm"), 1)
            pe.wait_ge(sem("kn_out"), B_HEADS)
            pe.wait_ge(sem("v_out"), 2 * TT)
            for u in range(2 * B_HEADS + 3):
                if u < 2 * B_HEADS:
                    h, q = u // 2, slice((u % 2) * P, (u % 2 + 1) * P)
                    if u >= 3:
                        pe.wait_ge(sem("exps"), u - 2)
                    nc.tensor.matmul(score_bank[u % 3][:, :], qn[:, h, q], kn[:, h, :], start=True, stop=False)
                    nc.tensor.matmul(score_bank[u % 3][:, :], qrz[:, h, q], kr, start=False, stop=True).then_inc(
                        sem("scores"), 1)
                if 2 <= u < 2 * B_HEADS + 2:
                    w = u - 2
                    pe.wait_ge(sem("probs"), w + 1)
                    if w >= 2:
                        pe.wait_ge(sem("prob_t_out"), w - 1)
                    for tt in range(TT):
                        last = nc.tensor.transpose(bank[2 + w % 2][:, tt * P:(tt + 1) * P],
                                                   prob[w % 3][:, tt * P:(tt + 1) * P], ident)
                    last.then_inc(sem("prob_t"), 1)
                if u >= 3:
                    w = u - 3
                    h = w // 2
                    pe.wait_ge(sem("prob_t_out"), w + 1)
                    if w >= 2:
                        pe.wait_ge(sem("att_out"), w - 1)
                    for tt in range(TT):
                        last = nc.tensor.matmul(bank[4 + w % 2][:, 0:P], vB[:, tt, h * P:(h + 1) * P],
                                                probT[w % 2][:, tt, :], start=(tt == 0), stop=(tt == TT - 1))
                    last.then_inc(sem("att_o"), 1)
            pe.wait_ge(*step("ret_qk"))
            pe.wait_ge(sem("prob_t_out"), 2 * B_HEADS)
            pe.wait_ge(sem("att_out"), 2 * B_HEADS)
            for h in range(C_HEADS + 1):
                if h < C_HEADS:
                    for j in range(2):
                        n = 2 * h + j
                        if n >= 4:
                            pe.wait_ge(sem("ret_att"), n - 3)
                        for kt in range(2 * j, 2 * j + 2):
                            last = nc.tensor.matmul(bank[n % 4][:, (kt % 2) * LAT:(kt % 2 + 1) * LAT],
                                                    rk[:, h // 2, kt * P:(kt + 1) * P], rqz[:, h, :], start=True,
                                                    stop=True, skip_group_check=True)
                        last.then_inc(sem("ret_s"), 1)
                if h >= 1:
                    w = h - 1
                    pe.wait_ge(sem("ret_att"), 2 * w + 2)
                    if w >= 2:
                        pe.wait_ge(sem("ret_out"), w - 1)
                    for q in range(LT):
                        for kt in range(TT):
                            last = nc.tensor.matmul(bank[4 + w % 2][:, q * P:(q + 1) * P],
                                                    att[w % 2][:, kt, q * P:(q + 1) * P], rv[:, kt, w * P:(w + 1) * P],
                                                    start=(kt == 0), stop=(kt == TT - 1), skip_group_check=True)
                    last.then_inc(sem("ret_o"), 1)
            pe.wait_ge(*step("wad_tanh"))
            pe.wait_ge(sem("lora_in"), 64)

            def lora(n):
                i, c = LORAS[n // 4], n % 4
                nc.tensor.matmul(bank[n % 4][:, :], lw[i][:, c * P:(c + 1) * P],
                                 wadt.rearrange("p a b -> p (a b)"), start=True, stop=True).then_inc(sem("lora"), 1)

            for n in range(8):
                if n >= 4:
                    pe.wait_ge(sem("lora_out"), n - 3)
                lora(n)
            pe.wait_ge(*step("kk_sq"))
            for tt in range(TT):
                pe.wait_ge(sem("lora_out"), tt + 5)
                nc.tensor.matmul(bank[tt][:, :], headones, sqa[:, tt, :], start=True, stop=True).then_inc(
                    sem("kk_sum"), 1)
            for n in range(8, 16):
                if n < 12:
                    pe.wait_ge(sem("kk_root"), n - 7)
                else:
                    pe.wait_ge(sem("lora_out"), n - 3)
                lora(n)
            pe.wait_ge(*step("ret_done"))
            for q in range(LT):
                for c in range(4):
                    last = nc.tensor.transpose(bank[5 + q][:, c * P:(c + 1) * P], oC[:, q, c * P:(c + 1) * P], ident)
                last.then_inc(sem("ret_t"), 1)
            pe.wait_ge(sem("ret_out"), C_HEADS)
            pe.wait_ge(sem("v_shift"), 4)
            pe.wait_ge(sem("ret_t_out"), 2)
            for tt in range(TT):
                for c in range(4):
                    last = nc.tensor.transpose(bank[4 + tt][:, c * P:(c + 1) * P], vs[:, tt, c, :], ident)
                last.then_inc(sem("v_t"), 1)
            pe.wait_ge(sem("v_t_out"), TT)
            pe.wait_ge(sem("lora_out"), 16)

            def item(n):
                b, kind, _, _ = items[n]
                d, tt = batches[b]
                _, _, engine, count = items[n - 2]
                if n >= 2:
                    pe.wait_ge(sem(f"rw_item_{engine}"), count)
                ps = bank[n % 2]
                if kind in ("a", "b", "k"):
                    src = {"a": arp[:, :, 0, :], "b": bb, "k": kd}[kind]
                    for c in range(4):
                        last = nc.tensor.transpose(ps[:, c * P:(c + 1) * P], src[:, c, :], ident)
                elif kind == "bonus":
                    for c in range(4):
                        last = nc.tensor.matmul(ps[:, 2 * c:2 * c + 2], cum[1 + d][:, c, :], headsel, start=True,
                                                stop=True, skip_group_check=True)
                elif kind in ("low0", "low1"):
                    for j in range(4):
                        h = 4 * int(kind[3]) + j
                        last = nc.tensor.matmul(ps[:, j * P:(j + 1) * P], arp[:, h // 2, 0, :], bz[:, h, :],
                                                start=True, stop=True, skip_group_check=True)
                else:
                    out_, m = split(ps[:, :], 4, P), 2 if tt >= 2 else 1
                    rhs = arp[:, kind // 2, 0:m, :]
                    nc.tensor.matmul(out_[:, 0:m], bz[:, kind, :], rhs, start=True, stop=True, skip_group_check=True)
                    last = nc.tensor.matmul(out_[:, 2:2 + m], kz[:, kind, :], rhs, start=True, stop=True,
                                            skip_group_check=True)
                last.then_inc(sem("rw_item"), 1)

            pe.wait_ge(sem("rw_feat"), 1)
            for n in items_of(0):
                item(n)
            nlat = 0
            for b, (d, tt) in enumerate(batches):
                latent = tt >= 2
                u4 = um[b % 2]
                own = {items[n][1]: items[n] for n in items_of(b)}

                def read(kind):
                    pe.wait_ge(sem(f"rw_item_{own[kind][2]}"), own[kind][3])

                read("k")
                if b:
                    pe.wait_ge(sem("rw_s"), 4 * b)
                for lv in range(LEVELS):
                    n, nx = 2 * (LEVELS * b + lv), 2 * ((LEVELS - 1) * b + lv)
                    for hf in range(2):
                        if lv:
                            pe.wait_ge(sem("rw_x"), nx - 1 + hf)
                        else:
                            read(f"low{hf}")
                        for j in range(4):
                            last = nc.tensor.matmul(bank[4 + hf][:, j * P:(j + 1) * P], u4[:, hf, j, 0],
                                                    xm[:, hf, j, :], start=True, stop=True, skip_group_check=True)
                        last.then_inc(sem("rw_lx"), 1)
                    if lv == LEVELS - 1:
                        for hf in range(2):
                            if nlat:
                                pe.wait_ge(sem("rw_y"), 2 * (nlat - 1) + hf + 1)
                            for j in range(4):
                                h = 4 * hf + j
                                nc.tensor.matmul(bank[6 + hf][:, 2 * P + j * 64:2 * P + (j + 1) * 64],
                                                 u4[:, hf, j, 2], vtok[:, tt, 64 * h:64 * h + 64], start=True,
                                                 stop=True, skip_group_check=True)
                    for hf in range(2):
                        pe.wait_ge(sem("rw_z"), n + hf + 1)
                        if lv:
                            pe.wait_ge(sem("rw_g"), n - 1 + hf)
                        if lv < LEVELS - 1:
                            for j in range(4):
                                last = nc.tensor.matmul(bank[hf][:, j * P:(j + 1) * P], gm[:, hf, j, :],
                                                        zm[:, hf, j, :], start=True, stop=True,
                                                        skip_group_check=True)
                            last.then_inc(sem("rw_xz"), 1)
                        for j in range(4):
                            last = nc.tensor.matmul(bank[2 + hf][:, j * P:(j + 1) * P], zm[:, hf, j, :],
                                                    gm[:, hf, j, :], start=True, stop=True, skip_group_check=True)
                        last.then_inc(sem("rw_gz"), 1)

                def next_items(part):
                    if b + 1 < len(batches):
                        for n in items_of(b + 1, part):
                            item(n)

                if b + 1 < len(batches):
                    pe.wait_ge(sem("rw_feat"), b + 2)
                for hf in range(2):
                    pe.wait_ge(sem("rw_g"), 2 * LEVELS * (b + 1) - 1 + hf)
                    for j in range(4):
                        h = 4 * hf + j
                        last = nc.tensor.matmul(
                            bank[6 + hf][64 * (j % 2):64 * (j % 2) + 64, (j // 2) * P:(j // 2 + 1) * P],
                            atok[b % 2].rearrange("p a b -> p (a b)")[:, 64 * h:64 * h + 64], gm[:, hf, j, :],
                            start=True, stop=True, skip_group_check=True)
                    last.then_inc(sem("rw_w1_mm"), 1)
                next_items(0)
                for hf in range(2):
                    pe.wait_ge(sem("rw_mv"), 2 * b + hf + 1)
                    for j in range(4):
                        last = nc.tensor.matmul(bank[4 + hf][:, j * 64:(j + 1) * 64], gm[:, hf, j, :],
                                                w1mv[:, hf, 2 * P + j * 64:2 * P + (j + 1) * 64], start=(j == 0),
                                                stop=False, skip_group_check=True)
                    last.then_inc(sem("rw_w2_mm"), 1)
                    if latent:
                        for j in range(4):
                            h = 4 * hf + j
                            nc.tensor.matmul(bank[6 + hf][:, j * 64:(j + 1) * 64], u4[:, hf, j, 3],
                                             vtok[:, tt, 64 * h:64 * h + 64], start=(j == 0), stop=False,
                                             skip_group_check=True)
                next_items(1)
                if b == 4:
                    pe.wait_ge(*step("rw_s_reset"))
                for i, c in enumerate((0, 1) if d == 0 else (1, 0)):
                    rows = slice(CH * c, CH * c + CH)
                    for hf in range(2):
                        if 4 * b + 2 * i:
                            pe.wait_ge(sem("rw_s"), 4 * b + 2 * i + hf - 1)
                        for p in range(2):
                            last = nc.tensor.matmul(bank[4 + hf][rows, p * P:(p + 1) * P],
                                                    w1mv[:, hf, p * P + CH * c:p * P + CH * c + CH],
                                                    sst[i][:, 2 * hf + p, :], start=False, stop=True,
                                                    skip_group_check=True)
                        last.then_inc(sem("rw_u_mm"), 1)
                        for p in range(2):
                            w = 2 * hf + p
                            if latent:
                                nc.tensor.matmul(bank[6 + hf][rows, p * P:(p + 1) * P], rr[b % 2][:, w, rows],
                                                 sst[i][:, w, :], start=False, stop=False, skip_group_check=True)
                            nc.tensor.matmul(bank[2 + hf][:, p * P:(p + 1) * P], ktok[b % 2][rows, w, :],
                                             vtok[rows, tt, w * P:(w + 1) * P], start=(p == 0), stop=False,
                                             skip_group_check=True)
                    next_items(2 + 2 * i)
                    for hf in range(2):
                        pe.wait_ge(sem("rw_u"), 4 * b + 2 * i + hf + 1)
                        for p in range(2):
                            last = nc.tensor.matmul(bank[2 + hf][:, p * P:(p + 1) * P],
                                                    btok[b % 2][rows, 2 * hf + p, :],
                                                    w2[rows, hf, p * P:(p + 1) * P], start=False, stop=True,
                                                    skip_group_check=True)
                        last.then_inc(sem("rw_s_mm"), 1)
                    if i == 0:
                        next_items(3)
                if latent:
                    for hf in range(2):
                        for j in range(4):
                            last = nc.tensor.matmul(bank[6 + hf][:, j * 64:(j + 1) * 64], u4[:, hf, j, 1],
                                                    w2[:, hf, j * 64:(j + 1) * 64], start=False, stop=(j == 3),
                                                    skip_group_check=True)
                        last.then_inc(sem("rw_y_mm"), 1)
                    nlat += 1
                next_items(5)
            def wo_in(i):
                count = sum(4 if kind == "rest" else 1 for kind, _ in wo_pieces[i % 5:i + 1:5])
                pe.wait_ge(sem(f"wo_in{i % 5}"), 16 * count)

            def mix_step(n, tt, c, weights):
                return nc.tensor.matmul(mix_bank(tt, c)[:, :], mix[n][1][:, tt * P:(tt + 1) * P], weights,
                                        start=(n == 0), stop=(n == KT - 1))

            pe.wait_ge(sem("rw_s"), 4 * len(batches))
            for i, (kind, n) in enumerate(wo_pieces[:EARLY + 3]):
                if i == 1:
                    pe.wait_ge(sem("gup_in"), 16)
                    pe.wait_ge(sem("rw_y"), 8)
                    for q in range(LT):
                        nc.tensor.matmul(bank[6 + q][:, :], gsig[0:GD, q * P:(q + 1) * P], gup[0:GD, :], start=True,
                                         stop=True).then_inc(sem("g_mm"), 1)
                if i == 6:
                    pe.wait_ge(sem("a_done"), LT)
                    for q in range(LT):
                        for c in range(4):
                            last = nc.tensor.transpose(bank[6 + q][:, c * P:(c + 1) * P],
                                                       yacc[:, q, c * P:(c + 1) * P], ident)
                        last.then_inc(sem("a_t"), 1)
                wo_in(i)
                w = woring[i % 5]
                if kind == "part":
                    for tt in range(LT):
                        for c in range(3):
                            last = mix_step(n, tt, c, w[:, BANK * c:BANK * (c + 1)])
                else:
                    pe.wait_ge(sem("a_t_out"), LT)
                    for j in range(4):
                        for tt in range(LT):
                            last = mix_step(n + j, tt, 3, w[:, BANK * j:BANK * (j + 1)])
                last.then_inc(sem("wo_used"), 1)
            for i in range(EARLY + 3, len(wo_pieces)):
                wo_in(i)
            for tt in range(LT):
                for c in range(4):
                    for i in range(EARLY + 3, len(wo_pieces)):
                        last = mix_step(wo_pieces[i][1], tt, c, woring[i % 5][:, BANK * c:BANK * (c + 1)])
                    last.then_inc(sem("mix_mm"), 1)
            for tt in range(LT):
                for n in range(4):
                    if n % 2 == 0:
                        pe.wait_ge(*step(("u_half", "u_ready")[n // 2] if tt else "u_ready0"))
                    if tt:
                        pe.wait_ge(sem("u_t_out"), n + 1)
                    for k in range(4):
                        last = nc.tensor.transpose(bank[n][:, k * P:(k + 1) * P],
                                                   ub[:, tt, (4 * n + k) * P:(4 * n + k + 1) * P], ident)
                    last.then_inc(sem("u_t"), 1)
            pe.wait_ge(sem("router_in"), 32)
            pe.wait_ge(sem("u_t_out"), 8)
            for k in range(KT):
                last = nc.tensor.matmul(bank[4][0:N_EXPERTS, 0:LAT], rwt[:, k, :], uT[:, k, :], start=(k == 0),
                                        stop=(k == KT - 1))
            last.then_inc(step("logits")[0], 1)
            pe.wait_ge(*step("logits_out"))
            for tt in range(LT):
                last = nc.tensor.transpose(bank[5][:, N_EXPERTS * tt:N_EXPERTS * (tt + 1)],
                                           lgT[0:N_EXPERTS, tt * P:(tt + 1) * P], ident[0:N_EXPERTS, 0:N_EXPERTS])
            last.then_inc(step("logits_t")[0], 1)
            pe.wait_ge(sem("route_in"), 16)
            pe.wait_ge(*step("selected"))
            sel = rt(3)
            nc.tensor.matmul(bank[6][:, 0:16], before, sel[:, 0], start=True, stop=True, skip_group_check=True)
            nc.tensor.matmul(bank[6][:, 16:32], before, sel[:, 1], start=True, stop=False, skip_group_check=True)
            nc.tensor.matmul(bank[6][:, 16:32], ones, sel[:, 0], start=False, stop=True, skip_group_check=True)
            nc.tensor.matmul(bank[6][:, 32:48], ones, sel[:, 0], start=True, stop=False, skip_group_check=True)
            nc.tensor.matmul(bank[6][:, 32:48], ones, sel[:, 1], start=False, stop=True,
                             skip_group_check=True).then_inc(step("ranks")[0], 1)
            pe.wait_ge(*step("onehot"))
            for k in range(KT):
                if k >= 4:
                    pe.wait_ge(sem("xg_out"), k - 3)
                for tt in range(LT):
                    last = nc.tensor.matmul(bank[k % 4][:, :], ub[:, tt, k * P:(k + 1) * P], hot[:, tt, :],
                                            start=(tt == 0), stop=(tt == LT - 1))
                last.then_inc(sem("xg_mm"), 1)
            pe.wait_ge(*step("hot_gates"))
            for s in range(ST):
                for tt in range(LT):
                    last = nc.tensor.transpose(bank[6 + s // 2][:, (s % 2) * LAT + tt * P:(s % 2) * LAT + (tt + 1) * P],
                                               hotg[:, tt, s * P:(s + 1) * P], ident)
                if s % 2 == 1:
                    last.then_inc(sem("hot_t"), 1)
            pe.wait_ge(sem("xg_out"), KT)
            pe.wait_ge(sem("hot_t_out"), 2)
            pe.wait_ge(*step("xg_pad"))

            def expert(n, first):
                start = pe.value_load(starts[0:1, bass.ds(n, 1)], min_val=0, max_val=PAIRS)
                window = xg[:, :, bass.ds(start, P)]
                if not first:
                    pe.wait_ge(sem("h_out"), n * 2)
                for j in range(3):
                    for w in range(2):
                        piece = 2 * j + w
                        pe.wait_ge(sem(f"ew_in{piece}"), n * 32 + 16)
                        for f in range(4):
                            for k in range(4 * j, 4 * j + 4):
                                last = nc.tensor.matmul(bank[2 * (f // 2) + w][:, (f % 2) * P:(f % 2 + 1) * P],
                                                        ering[piece][:, k % 4, f * P:(f + 1) * P], window[:, k, :],
                                                        start=(k == 0 and f % 2 == 0), stop=False,
                                                        skip_group_check=True)
                        last.then_inc(sem("ew_used"), 1)
                for w in range(2):
                    pe.wait_ge(sem(f"ew_in{w}"), n * 32 + 32)
                for half in range(2):
                    for w in range(2):
                        for f in range(2 * half, 2 * half + 2):
                            for k in range(12, 16):
                                last = nc.tensor.matmul(bank[2 * half + w][:, (f % 2) * P:(f % 2 + 1) * P],
                                                        ering[w][:, k % 4, f * P:(f + 1) * P], window[:, k, :],
                                                        start=False, stop=(k == KT - 1), skip_group_check=True)
                    last.then_inc(sem("h_mm"), 1)

                def product(m, fs):
                    for i in range(2):
                        for f in fs:
                            c = ((2 * m + i) % 4) * P
                            last = nc.tensor.matmul(bank[4 + m % 4][:, i * P:(i + 1) * P],
                                                    ering[(8 + m // 2) % 6][:, f, c:c + P], hT[:, f, :],
                                                    start=(f == 0 and i == 0), stop=(f == 3), skip_group_check=True)
                    return last

                pe.wait_ge(sem("h_out"), n * 2 + 1)
                if not first:
                    pe.wait_ge(sem("y_out"), n * 8)
                for m in range(4):
                    if m % 2 == 0:
                        pe.wait_ge(sem(f"ew_in{2 + m // 2}"), n * 32 + 32)
                    product(m, (0, 1))
                pe.wait_ge(sem("h_out"), n * 2 + 2)
                for m in range(4):
                    product(m, (2, 3)).then_inc(sem("y_mm"), 1)
                for m in range(4, 8):
                    if m % 2 == 0:
                        pe.wait_ge(sem(f"ew_in{2 + m // 2}"), n * 32 + 32)
                    pe.wait_ge(sem("y_out"), n * 8 + m - 3)
                    product(m, (0, 1, 2, 3)).then_inc(sem("y_mm"), 1)

            expert(0, True)
            with pe.Fori(1, N_EXPERTS) as e:
                expert(e, False)
            pe.wait_ge(sem("y_out"), 8 * N_EXPERTS)
            with pe.If(pe.value_load(starts[0:1, 2 * N_EXPERTS:2 * N_EXPERTS + 1]) > P):
                with pe.Fori(N_EXPERTS, 2 * N_EXPERTS) as n:
                    expert(n, False)
                pe.wait_ge(sem("y_out"), 16 * N_EXPERTS)
            def summed(tt, c):
                if tt:
                    pe.wait_ge(sem("ffn_out"), c + 1)
                for s in range(ST):
                    last = nc.tensor.matmul(bank[4 + c][:, :], hotT[:, s, tt * P:(tt + 1) * P],
                                            yt[:, s, BANK * c:BANK * (c + 1)], start=(s == 0), stop=(s == ST - 1))
                last.then_inc(sem("ffn"), 1)

            for c in range(5):
                if c < 4:
                    if c >= 1:
                        pe.wait_ge(sem("yt_out"), ST * c)
                    for s in range(ST):
                        for i in range(4):
                            last = nc.tensor.transpose(bank[s][:, i * P:(i + 1) * P], ys[:, 4 * c + i, s * P:(s + 1) * P],
                                                       ident)
                        last.then_inc(sem("yt_t"), 1)
                if c >= 1:
                    pe.wait_ge(sem("yt_out"), ST * c)
                    summed(0, c - 1)
            for c in range(4):
                summed(1, c)


_INS = ["x", "c", "ctx", "c_ctx", "mod_w", "mod_b", "w_in", "w_out", "rw_mu", "rw_w0", "rw_w_up", "rw_a0", "rw_a_up",
        "rw_g_up", "rw_k_k", "rw_k_a", "rw_r_k", "rw_gn_g", "rw_gn_b", "mla_q_norm", "mla_kv_norm", "mla_w_uq",
        "mla_w_ukv", "ret_gn_g", "ret_gn_b", "ln1_g", "ln1_b", "ln2_g", "ln2_b", "router_w", "router_b", "exp_w1",
        "exp_w3", "exp_w2"]


def _constants():
    import numpy as np

    c = np.zeros((P, N_CONST), np.float32)

    def put(name, a):
        at, n = CONST[name]
        c[:, at:at + n] = np.asarray(a, np.float64).reshape(P, n)

    i = np.arange(P)
    put("ident", np.eye(P))
    put("ones", np.ones((P, P)))
    put("headones", (i[:, None] // A_HD == i[None] // A_HD))
    rot = np.zeros((P, P))
    for d in range(P):
        low = d % 64 < 32
        rot[d + 32 if low else d - 32, d] = -1.0 if low else 1.0
    put("rot", rot)
    n = B_ROPE // 4
    inv = (10000.0 ** (-np.arange(n, dtype=np.float32) / n)).astype(np.float32)
    pos = np.arange(LAT)
    ang = np.concatenate([(pos // 64).astype(np.float32)[:, None] * inv,
                          (pos % 64).astype(np.float32)[:, None] * inv], -1)
    put("cos", np.cos(ang)[:, i % 32].T)
    put("sin", np.sin(ang)[:, i % 32].T)
    put("reset", np.broadcast_to((np.arange(BANK) % CH != 0), (P, BANK)))
    same = i[:, None] // CH == i[None] // CH
    before, upto = (i[:, None] < i[None]) & same, (i[:, None] <= i[None]) & same
    put("mask_f", np.concatenate([before, upto, before, upto], 1))
    put("mask_b", np.concatenate([before.T, upto.T, before.T, upto.T], 1))
    levels = [1, 2, 4, 8, 16, 32]
    low = [(i[:, None] // b == i[None] // b + 1) & (i[:, None] // (2 * b) == i[None] // (2 * b)) for b in levels]
    put("lower", np.concatenate(low, 1))
    put("upper", np.concatenate([m.T for m in low], 1))
    put("headsel", i[:, None] // A_HD == np.arange(2)[None])
    put("eps", np.broadcast_to([LN_EPS, RWKV_GN_EPS, KK_EPS, 0.0], (P, 4)))
    put("iota16", np.broadcast_to(np.arange(N_EXPERTS), (P, N_EXPERTS)))
    put("iota4", np.broadcast_to(np.arange(4), (P, 4)))
    key, query = np.arange(TOK)[:, None] - CTX, np.arange(LAT)[None]
    decay = []
    for h in range(C_HEADS):
        gf, gb = 1.0 - 2.0 ** (-5.0 - h), 1.0 - 2.0 ** (-5.5 - h)
        fwd = np.where(query >= key, gf ** np.maximum(query - key, 0), 0.0)
        ahead = np.where(key >= 0, key - query, LAT - query + key + CTX)
        bwd = np.where(ahead >= 0, gb ** np.maximum(ahead, 0), 0.0)
        decay.append((fwd + bwd) * C_KD ** -0.5)
    decay = np.stack(decay).reshape(C_HEADS, TT, P, LAT).transpose(2, 0, 1, 3).reshape(P, -1)
    route = np.concatenate([i[:, None] < i[None], np.broadcast_to(np.arange(2 * LAT), (P, 2 * LAT))], 1)
    return c, np.ascontiguousarray(decay, np.float32), np.ascontiguousarray(route, np.float32)


def kernel(**inputs):
    import numpy as _np
    import concourse.bacc as _bacc
    from concourse import mybir as _mybir
    from concourse.bass_utils import run_bass_kernel_spmd as _run

    nc = _bacc.Bacc("TRN2", target_bir_lowering=False, num_devices=1)
    arrays, args = {}, {}
    tables = dict(zip(("const", "decay", "route"), _constants()))
    for name in _INS + list(tables):
        a = _np.ascontiguousarray(tables[name] if name in tables else inputs[name])
        arrays[f"in_{name}_dram"] = a
        args[name] = nc.dram_tensor(f"in_{name}_dram", a.shape, _mybir.dt.from_np(a.dtype), kind="ExternalInput").ap()
    args["out"] = nc.dram_tensor("out_0_dram", (1, LAT, D), F32, kind="ExternalOutput").ap()
    build_program(nc, args)
    r = _run(nc, [arrays], core_ids=[0])
    return r.results[0]["out_0_dram"]
```
